# Optimizing a Trainium2 kernel written in Bass

```python
import jax, jax.numpy as jnp
from jax import lax
import numpy as np

D_MODEL = 1024
BATCH = 1
SEQ = 256
DEPTH = 2
DEC_BATCH = 8
DEC_SEQ = 4
PAST_LEN = 256
PAGE_SIZE = 128

D_PLE = 256
N_BRANCH = 3
W_BRANCH = D_MODEL // 2
NORM_EPS = 1e-6
DK_A = 128
DV_A = 128
H_A = W_BRANCH // DV_A
QKV_A = H_A * (2 * DK_A + DV_A)
CONV_W = 4
CHUNK_A = 64
N_B = 64
H_B = W_BRANCH // N_B
LORA_W = 64
LORA_A = 64
SHIFT_B = 3 * W_BRANCH + LORA_W + LORA_A
GN_EPS = 64e-5
D_C = 64
H_C = W_BRANCH // D_C
MOBA_BLOCK = 256
MOBA_TOPK = 3
ROPE_DIM = D_C // 4
ROPE_THETA = 500000.0
Q_BLOCK = 128
IN_SPLITS = (QKV_A, W_BRANCH, H_A, H_A, SHIFT_B, W_BRANCH, 3 * W_BRANCH, W_BRANCH, N_BRANCH * D_MODEL)
D_IN = sum(IN_SPLITS)
F32 = jnp.float32

kernel_name = 'hybrid_deltanet_rwkv7_moba_decode_step'

def rmsnorm(x, g, eps=NORM_EPS):
    xf = x.astype(F32)
    y = xf * lax.rsqrt(jnp.mean(xf * xf, axis=-1, keepdims=True) + eps)
    return (y * g.astype(F32)).astype(x.dtype)

def l2norm(x, eps=1e-6):
    xf = x.astype(F32)
    return (xf * lax.rsqrt(jnp.sum(xf * xf, axis=-1, keepdims=True) + eps)).astype(x.dtype)

def rope_partial(x, pos):
    half = ROPE_DIM // 2
    inv = ROPE_THETA ** (-jnp.arange(half, dtype=F32) / half)
    ang = pos.astype(F32)[:, None] * inv[None, :]
    cos = jnp.cos(ang)[None, :, None, :]
    sin = jnp.sin(ang)[None, :, None, :]
    xr = x[..., :ROPE_DIM].astype(F32)
    x1, x2 = xr[..., :half], xr[..., half:]
    rot = jnp.concatenate([x1 * cos - x2 * sin, x2 * cos + x1 * sin], axis=-1)
    return jnp.concatenate([rot.astype(x.dtype), x[..., ROPE_DIM:]], axis=-1)

def causal_conv(u, buf, w):
    L = u.shape[1]
    full = jnp.concatenate([buf.astype(u.dtype), u], axis=1)
    out = full[:, 0:L] * w[0]
    for j in range(1, CONV_W):
        out = out + full[:, j:j + L] * w[j]
    return out, full[:, L:]

def gated_delta_chunked(q, k, v, g, beta, s0):
    B, L, H, _ = q.shape
    DV = v.shape[-1]
    C = CHUNK_A if L % CHUNK_A == 0 else L
    N = L // C

    def chunks(t):
        t = t.astype(F32).reshape((B, N, C, H) + t.shape[3:])
        return jnp.moveaxis(t, (1, 3), (0, 2))

    qc, kc, vc, gc, bc = chunks(q), chunks(k), chunks(v), chunks(g), chunks(beta)
    G = jnp.cumsum(gc, axis=-1)
    tri_incl = jnp.tril(jnp.ones((C, C), bool))
    tri_strict = jnp.tril(jnp.ones((C, C), bool), -1)
    decay = jnp.exp(jnp.where(tri_incl, G[..., :, None] - G[..., None, :], -jnp.inf))
    kk = jnp.einsum('nbhid,nbhjd->nbhij', kc, kc)
    lmat = jnp.where(tri_strict, bc[..., :, None] * kk * decay, 0.0)
    a_mat = jnp.eye(C, dtype=F32) + lmat
    rhs = jnp.concatenate([vc * bc[..., None], kc * (bc * jnp.exp(G))[..., None]], axis=-1)
    sol = lax.linalg.triangular_solve(a_mat, rhs, left_side=True, lower=True, unit_diagonal=True)
    bv, wk = sol[..., :DV], sol[..., DV:]
    qk = jnp.where(tri_incl, jnp.einsum('nbhid,nbhjd->nbhij', qc, kc) * decay, 0.0)

    def step(S, inp):
        qi, ki, bvi, wki, qki, Gi = inp
        u = bvi - jnp.einsum('bhcd,bhde->bhce', wki, S)
        o = jnp.einsum('bhcd,bhde->bhce', qi * jnp.exp(Gi)[..., None], S) + jnp.einsum('bhij,bhje->bhie', qki, u)
        g_last = Gi[..., -1:]
        S = S * jnp.exp(g_last)[..., None] + jnp.einsum('bhcd,bhce->bhde', ki * jnp.exp(g_last - Gi)[..., None], u)
        return S, o

    s_fin, o = lax.scan(step, s0.astype(F32), (qc, kc, bv, wk, qk, G))
    o = jnp.moveaxis(o, (0, 2), (1, 3)).reshape(B, L, H, DV)
    return o, s_fin

def rwkv7_scan(r, logw, k, v, a, b, s0):
    def step(S, inp):
        rt, wt, kt, vt, at, bt = inp
        sa = jnp.einsum('bhvk,bhk->bhv', S, at)
        S = S * jnp.exp(wt)[:, :, None, :] + sa[..., None] * bt[:, :, None, :] + vt[..., None] * kt[:, :, None, :]
        return S, jnp.einsum('bhvk,bhk->bhv', S, rt)

    xs = tuple(jnp.moveaxis(t.astype(F32), 1, 0) for t in (r, logw, k, v, a, b))
    s_fin, y = lax.scan(step, s0.astype(F32), xs)
    return jnp.moveaxis(y, 0, 1), s_fin

def moba_attention(q, q_pos, k_all, v_all):
    B, Lq, H, D = q.shape
    Lk = k_all.shape[1]
    nb = -(-Lk // MOBA_BLOCK)
    pad = nb * MOBA_BLOCK - Lk

    def blocks(t):
        t = jnp.pad(t, ((0, 0), (0, pad), (0, 0), (0, 0)))
        return t.reshape(B, nb, MOBA_BLOCK, H, D).transpose(0, 3, 1, 2, 4)

    kb, vb = blocks(k_all), blocks(v_all)
    kmean = jnp.mean(kb.astype(F32), axis=3)
    ksel = min(MOBA_TOPK, nb)
    qb = Q_BLOCK if Lq % Q_BLOCK == 0 else Lq
    nq = Lq // qb
    qs = q.reshape(B, nq, qb, H, D).transpose(1, 0, 3, 2, 4)
    ps = q_pos.reshape(nq, qb)
    scale = D ** -0.5
    bidx = jnp.arange(B)[:, None, None, None]
    hidx = jnp.arange(H)[None, :, None, None]

    def one_block(args):
        qi, pi = args
        own = pi // MOBA_BLOCK
        gate = jnp.einsum('bhqd,bhnd->bhqn', qi.astype(F32), kmean)
        past = jnp.arange(nb)[None, :] < own[:, None]
        gate = jnp.where(past, gate, -jnp.inf)
        _, top = lax.top_k(gate, ksel)
        sel_ok = jnp.arange(ksel)[None, :] < own[:, None]
        own_idx = jnp.broadcast_to(own[None, None, :, None], top.shape[:3] + (1,))
        idx = jnp.concatenate([top, own_idx.astype(top.dtype)], axis=-1)
        kg = kb[bidx, hidx, idx]
        vg = vb[bidx, hidx, idx]
        s = jnp.einsum('bhqd,bhqskd->bhqsk', qi, kg).astype(F32) * scale
        kpos = idx[..., None] * MOBA_BLOCK + jnp.arange(MOBA_BLOCK)
        slot_ok = jnp.concatenate([sel_ok, jnp.ones((qb, 1), bool)], axis=-1)
        mask = slot_ok[None, None, :, :, None] & (kpos <= pi[None, None, :, None, None])
        s = jnp.where(mask, s, -jnp.inf)
        p = jax.nn.softmax(s.reshape(B, H, qb, -1), axis=-1).reshape(s.shape)
        return jnp.einsum('bhqsk,bhqskd->bhqd', p.astype(vg.dtype), vg)

    out = lax.map(one_block, (qs, ps))
    return out.transpose(1, 0, 3, 2, 4).reshape(B, Lq, H, D)

def gather_pages(pool, page_table):
    pages = pool[page_table]
    b, n, p, h, d = pages.shape
    return pages.reshape(b, n * p, h, d)

def mixer_layer(x, ple, pos, past_k, past_v, dn_s, dn_buf, rw_s, rw_prev, lp):
    B, L, _ = x.shape
    dt = x.dtype
    h = rmsnorm(x, lp['norm_g'])
    proj = h @ lp['w_in']
    offs = np.cumsum(IN_SPLITS)[:-1].tolist()
    qkv_a, z_a, beta_raw, alpha_raw, f_b, z_b, qkv_c, z_c, gate_raw = jnp.split(proj, offs, axis=-1)

    u_a, dn_buf_new = causal_conv(qkv_a, dn_buf, lp['conv_a'])
    u_a = jax.nn.silu(u_a)
    q_a, k_a, v_a = jnp.split(u_a, [H_A * DK_A, 2 * H_A * DK_A], axis=-1)
    q_a = l2norm(q_a.reshape(B, L, H_A, DK_A)) * (DK_A ** -0.5)
    k_a = l2norm(k_a.reshape(B, L, H_A, DK_A))
    v_a = v_a.reshape(B, L, H_A, DV_A)
    beta = jax.nn.sigmoid(beta_raw.astype(F32))
    g_a = -jnp.exp(lp['a_log'].astype(F32)) * jax.nn.softplus(alpha_raw.astype(F32) + lp['dt_bias'].astype(F32))
    o_a, dn_s_new = gated_delta_chunked(q_a, k_a, v_a, g_a, beta, dn_s)
    o_a = rmsnorm(o_a, lp['onorm_a']).reshape(B, L, W_BRANCH).astype(dt) * jax.nn.silu(z_a)

    prev = jnp.concatenate([rw_prev[:, None].astype(dt), f_b[:, :-1]], axis=1)
    f_mix = f_b + (prev - f_b) * lp['mu_b']
    r_b, k_b, v_b, wl_b, al_b = jnp.split(f_mix, [W_BRANCH, 2 * W_BRANCH, 3 * W_BRANCH, 3 * W_BRANCH + LORA_W], axis=-1)
    w_raw = (lp['w0_b'] + jnp.tanh(wl_b) @ lp['w2_b']).astype(F32)
    logw = -jnp.exp(-jax.nn.softplus(-w_raw) - 0.5)
    a_b = jax.nn.sigmoid((lp['a0_b'] + al_b @ lp['a2_b']).astype(F32))

    def heads(t):
        return t.reshape(B, L, H_B, N_B)

    kk = l2norm(heads(k_b.astype(F32) * lp['kk_b'].astype(F32)))
    k_mod = k_b.astype(F32) * (1.0 + (a_b - 1.0) * lp['ka_b'].astype(F32))
    r_h, k_h, v_h, a_h = heads(r_b.astype(F32)), heads(k_mod), heads(v_b.astype(F32)), heads(a_b)
    y_b, rw_s_new = rwkv7_scan(r_h, heads(logw), k_h, v_h, -kk, kk * a_h, rw_s)
    mu = jnp.mean(y_b, axis=-1, keepdims=True)
    var = jnp.mean(jnp.square(y_b - mu), axis=-1, keepdims=True)
    y_b = ((y_b - mu) * lax.rsqrt(var + GN_EPS)).reshape(B, L, W_BRANCH) * lp['gn_g_b'] + lp['gn_b_b']
    bonus = jnp.sum(r_h * k_h * lp['rk_b'], axis=-1, keepdims=True) * v_h
    o_b = (y_b + bonus.reshape(B, L, W_BRANCH)).astype(dt) * jax.nn.silu(z_b)
    rw_prev_new = f_b[:, -1]

    q_c, k_c, v_c = jnp.split(qkv_c, [W_BRANCH, 2 * W_BRANCH], axis=-1)
    q_c = rope_partial(rmsnorm(q_c.reshape(B, L, H_C, D_C), lp['qn_c']), pos)
    k_c = rope_partial(rmsnorm(k_c.reshape(B, L, H_C, D_C), lp['kn_c']), pos)
    v_c = v_c.reshape(B, L, H_C, D_C)
    if past_k is None:
        k_all, v_all = k_c, v_c
    else:
        k_all = jnp.concatenate([past_k.astype(dt), k_c], axis=1)
        v_all = jnp.concatenate([past_v.astype(dt), v_c], axis=1)
    o_c = moba_attention(q_c, pos, k_all, v_all).reshape(B, L, W_BRANCH) * jax.nn.silu(z_c)

    o = jnp.stack([o_a, o_b, o_c], axis=2)
    up = jnp.einsum('blnc,ncd->blnd', o, lp['w_branch'])
    gates = jax.nn.sigmoid(gate_raw + lp['b_gate']).reshape(B, L, N_BRANCH, D_MODEL)
    x = x + jnp.sum(gates * up, axis=2) @ lp['w_out']
    x = x + jax.nn.sigmoid(x @ lp['w_pg'] + lp['b_pg']) * (ple @ lp['w_ple'])
    return x, (k_c, v_c, dn_s_new, dn_buf_new, rw_s_new, rw_prev_new)

def setup_inputs(seed: int = 0) -> dict:
    key = jax.random.key(seed)
    keys = list(jax.random.split(key, 40))

    def nrm(shape, scale=1.0, shift=0.0):
        return jax.random.normal(keys.pop(), shape, F32) * scale + shift

    n_pages = PAST_LEN // PAGE_SIZE
    n_used = DEC_BATCH * n_pages
    n_phys = n_used + max(1, n_used // 4)
    page_table = jax.random.permutation(keys.pop(), n_phys)[:n_used].reshape(DEC_BATCH, n_pages).astype(jnp.int32)
    return {
        'x_prompt': nrm((BATCH, SEQ, D_MODEL)),
        'x_sample': nrm((DEC_BATCH, DEC_SEQ, D_MODEL)),
        'cache_k': nrm((DEPTH, n_phys, PAGE_SIZE, H_C, D_C)),
        'cache_v': nrm((DEPTH, n_phys, PAGE_SIZE, H_C, D_C)),
        'state_dn': nrm((DEPTH, DEC_BATCH, H_A, DK_A, DV_A), 0.5),
        'state_dn_conv': nrm((DEPTH, DEC_BATCH, CONV_W - 1, QKV_A)),
        'state_rwkv': nrm((DEPTH, DEC_BATCH, H_B, N_B, N_B), 0.5),
        'state_rwkv_shift': nrm((DEPTH, DEC_BATCH, SHIFT_B)),
        'page_table': page_table,
        'p_prompt': nrm((DEPTH, BATCH, SEQ, D_PLE)),
        'p_sample': nrm((DEPTH, DEC_BATCH, DEC_SEQ, D_PLE)),
        'norm_g': nrm((DEPTH, D_MODEL), 0.02, 1.0),
        'w_in': nrm((DEPTH, D_MODEL, D_IN), D_MODEL ** -0.5),
        'conv_a': nrm((DEPTH, CONV_W, QKV_A), CONV_W ** -0.5),
        'a_log': jnp.log(jax.random.uniform(keys.pop(), (DEPTH, H_A), F32, 1.0, 16.0)),
        'dt_bias': nrm((DEPTH, H_A), 0.5, -4.0),
        'onorm_a': nrm((DEPTH, DV_A), 0.02, 1.0),
        'mu_b': jax.random.uniform(keys.pop(), (DEPTH, SHIFT_B), F32),
        'w0_b': nrm((DEPTH, W_BRANCH), 0.5, -1.0),
        'w2_b': nrm((DEPTH, LORA_W, W_BRANCH), LORA_W ** -0.5),
        'a0_b': nrm((DEPTH, W_BRANCH), 0.1),
        'a2_b': nrm((DEPTH, LORA_A, W_BRANCH), LORA_A ** -0.5),
        'kk_b': nrm((DEPTH, W_BRANCH), 0.05, 0.85),
        'ka_b': nrm((DEPTH, W_BRANCH), 0.05, 1.0),
        'rk_b': nrm((DEPTH, H_B, N_B), 0.1),
        'gn_g_b': nrm((DEPTH, W_BRANCH), 0.02, 1.0),
        'gn_b_b': nrm((DEPTH, W_BRANCH), 0.02),
        'qn_c': nrm((DEPTH, D_C), 0.02, 1.0),
        'kn_c': nrm((DEPTH, D_C), 0.02, 1.0),
        'w_branch': nrm((DEPTH, N_BRANCH, W_BRANCH, D_MODEL), W_BRANCH ** -0.5),
        'b_gate': nrm((DEPTH, N_BRANCH * D_MODEL), 0.1),
        'w_out': nrm((DEPTH, D_MODEL, D_MODEL), D_MODEL ** -0.5),
        'w_ple': nrm((DEPTH, D_PLE, D_MODEL), D_PLE ** -0.5),
        'w_pg': nrm((DEPTH, D_MODEL, D_MODEL), D_MODEL ** -0.5),
        'b_pg': nrm((DEPTH, D_MODEL), 0.1),
    }

def reference(x_prompt, x_sample, cache_k, cache_v, state_dn, state_dn_conv, state_rwkv,
              state_rwkv_shift, page_table, p_prompt, p_sample, norm_g, w_in, conv_a, a_log,
              dt_bias, onorm_a, mu_b, w0_b, w2_b, a0_b, a2_b, kk_b, ka_b, rk_b, gn_g_b, gn_b_b,
              qn_c, kn_c, w_branch, b_gate, w_out, w_ple, w_pg, b_pg):
    b_p, l_p, _ = x_prompt.shape
    l_s = x_sample.shape[1]
    past_len = page_table.shape[1] * cache_k.shape[2]
    pos_p = jnp.arange(l_p, dtype=jnp.int32)
    pos_s = past_len + jnp.arange(l_s, dtype=jnp.int32)
    dt = x_prompt.dtype
    zero_dn = jnp.zeros((b_p, H_A, DK_A, DV_A), dt)
    zero_conv = jnp.zeros((b_p, CONV_W - 1, QKV_A), dt)
    zero_rw = jnp.zeros((b_p, H_B, N_B, N_B), dt)
    zero_shift = jnp.zeros((b_p, SHIFT_B), dt)
    xp, xs = x_prompt, x_sample
    new_p, new_s = [], []
    for i in range(DEPTH):
        lp = {'norm_g': norm_g[i], 'w_in': w_in[i], 'conv_a': conv_a[i], 'a_log': a_log[i],
              'dt_bias': dt_bias[i], 'onorm_a': onorm_a[i], 'mu_b': mu_b[i], 'w0_b': w0_b[i],
              'w2_b': w2_b[i], 'a0_b': a0_b[i], 'a2_b': a2_b[i], 'kk_b': kk_b[i], 'ka_b': ka_b[i],
              'rk_b': rk_b[i], 'gn_g_b': gn_g_b[i], 'gn_b_b': gn_b_b[i], 'qn_c': qn_c[i],
              'kn_c': kn_c[i], 'w_branch': w_branch[i], 'b_gate': b_gate[i], 'w_out': w_out[i],
              'w_ple': w_ple[i], 'w_pg': w_pg[i], 'b_pg': b_pg[i]}
        xp, st_p = mixer_layer(xp, p_prompt[i], pos_p, None, None, zero_dn, zero_conv, zero_rw, zero_shift, lp)
        new_p.append(st_p)
        past_k = gather_pages(cache_k[i], page_table)
        past_v = gather_pages(cache_v[i], page_table)
        xs, st_s = mixer_layer(xs, p_sample[i], pos_s, past_k, past_v, state_dn[i], state_dn_conv[i],
                               state_rwkv[i], state_rwkv_shift[i], lp)
        new_s.append(st_s)
    k_p, v_p, dn_p, conv_p, rw_p, sh_p = [jnp.stack(t) for t in zip(*new_p)]
    k_s, v_s, dn_s, conv_s, rw_s, sh_s = [jnp.stack(t) for t in zip(*new_s)]
    return (xp, xs, k_p, v_p, dn_p, conv_p, rw_p, sh_p, k_s, v_s, dn_s, conv_s, rw_s, sh_s)


_drawn_inputs = setup_inputs


def setup_inputs(seed=0):
    import zlib

    import numpy as np

    out = dict(_drawn_inputs(seed))
    spreads = {}
    factors = {'onorm_a': 7.545,
     'kk_b': 39.425,
     'gn_g_b': 7.629,
     'gn_b_b': 7.32,
     'qn_c': 200.0,
     'b_pg': 8.0}
    for name, (base, spread) in spreads.items():
        noise = np.random.default_rng([zlib.crc32(name.encode()), seed]).standard_normal(out[name].shape)
        drawn = base * np.exp(spread * noise) if base else spread * noise
        out[name] = __import__('jax').numpy.asarray(drawn.astype(out[name].dtype))
    for name, factor in factors.items():
        out[name] = (out[name] * factor).astype(out[name].dtype)
    return out
```

```python
import math

import numpy as np
import concourse.bass as bass
from concourse import mybir
from contextlib import ExitStack

FP32 = mybir.dt.float32
I32 = mybir.dt.int32
ALU = mybir.AluOpType
ACT = mybir.ActivationFunctionType
AXX = mybir.AxisListType.X

D_MODEL, SEQ, DEPTH, NSEQ, LS, PAST, PAGE = 1024, 256, 2, 8, 4, 256, 128
D_PLE, W = 256, 512
KT_ = D_MODEL // 128
NTOK = SEQ + NSEQ * LS
NS = NSEQ * LS
QKV_A, CONV_W, SHIFT_B = 1536, 4, 1664
NA, NF, NC3 = QKV_A // 128, SHIFT_B // 128, 1536 // 128
OFF_QKVA, OFF_ZA, OFF_BA, OFF_F, OFF_ZB, OFF_QKVC, OFF_ZC, OFF_G = 0, 1536, 2048, 2056, 3720, 4232, 5768, 6280
UW = CONV_W - 1 + SEQ
US = CONV_W - 1 + LS
FW = 1 + SEQ
FS = 1 + LS
NEG = -1.0e30
NLEV = 7
TILES = [(0, 128), (128, 128), (256, 32)]
RING = 4
SPARE_B = 9
SLOT = 2048

CONST_LAYOUT = {}


def constants():
    cols, at = [], 0

    def put(name, a):
        nonlocal at
        full = np.zeros((128, a.shape[1]), np.float32)
        full[:a.shape[0]] = a
        CONST_LAYOUT[name] = (at, a.shape[1])
        at += a.shape[1]
        cols.append(full)

    p = np.arange(128)
    s, t = p[:, None], p[None, :]
    put("ident", np.eye(128))
    put("ones", np.ones((128, 128)))
    put("ones_head", (s // 64 == t // 64) * 1.0)
    swap = np.zeros((128, 128))
    for h in range(2):
        for j in range(8):
            swap[64 * h + 8 + j, 64 * h + j] = -1.0
            swap[64 * h + j, 64 * h + 8 + j] = 1.0
    put("swap", swap)
    for k in range(NLEV):
        b = 2 ** k
        put(f"level{k}", ((s // (2 * b) == t // (2 * b)) & ((s // b) % 2 == 0) & ((t // b) % 2 == 1)) * 1.0)
    put("strict_incl", np.concatenate([(s < t) * 1.0, (s <= t) * 1.0], 1))
    same = (s // LS == t // LS)[:32, :32]
    put("strict_incl_s", np.concatenate([(same & (s < t)[:32, :32]) * 1.0, (same & (s <= t)[:32, :32]) * 1.0], 1))
    put("causal", np.where(t <= s, 0.0, NEG))
    new = np.full((128, 2, 32), NEG)
    for q in range(128):
        j, tt = q // 32, q % 4
        for g in range(2):
            new[q, g, (4 * g + j) * 4:(4 * g + j) * 4 + tt + 1] = 0.0
    put("causal_new", new.reshape(128, 64))
    put("own_seq", ((p % 32)[:, None] // LS == np.arange(NSEQ)[None, :])[:64] * 1.0)
    put("eye8", np.eye(8))
    sel = np.zeros((4, 4, 128))
    for h in range(4):
        sel[h, h] = 1.0
    put("pick_head", sel.reshape(4, 512))
    pos = np.concatenate([np.arange(SEQ), np.tile(PAST + np.arange(LS), NSEQ)]).astype(np.float32)
    inv = (np.float32(500000.0) ** (-np.arange(8, dtype=np.float32) / np.float32(8))).astype(np.float32)
    ang = (inv[:, None] * pos[None, :]).astype(np.float32)
    cos, sin = np.ones((128, NTOK)), np.zeros((128, NTOK))
    for h in range(2):
        for half in range(2):
            r = 64 * h + 8 * half
            cos[r:r + 8], sin[r:r + 8] = np.cos(ang), np.sin(ang)
    put("cos", cos)
    put("sin", sin)
    keep = np.ones((128, NTOK))
    keep[:, [0, 128] + list(range(SEQ, NTOK, LS))] = 0.0
    put("keep", keep)
    put("bd", (s // 64 == t // 64) * 1.0)
    for name, v in [("c_1", 1.0), ("c_eps", 1e-6), ("c_4eps", 4e-6), ("c_gneps", 64e-5),
                    ("c_lndk", math.log(128.0 ** -0.5)), ("c_lnhalf", math.log(0.5)), ("c_0", 0.0)]:
        put(name, np.full((128, 1), v))
    return np.concatenate(cols, 1).astype(np.float32)


CONSTS = constants()

PROWS = [("norm_g", 8), ("mu_b", 13), ("b_gate", 24), ("w0_b", 4), ("a0_b", 4), ("kk_b", 4), ("ka_b", 4),
         ("rk_b", 4), ("gn_g_b", 4), ("gn_b_b", 4), ("b_pg", 8), ("onorm_a", 1), ("qn_c", 1), ("kn_c", 1)]
PAT, _n = {}, 0
for _name, _k in PROWS:
    PAT[_name] = _n
    _n += _k
NP1 = _n
NPAR = NP1 + 48


SIGNALS = {
    "consts_loaded": {"x_in": (16, lambda st: st[2] == 0)},
    "x_loaded": {"x_in": (48, lambda st: st[2] == 0)},
    "pages_loaded": {"x_in": (16, lambda st: st[2] == 0)},
    "param_rows_loaded": {"params": (16 * (len(PROWS) + 3), None)},
    "heads_loaded": {"params": (32, None)},
    "ple_rows_loaded": {"params": (48, None)},
    "hist_loaded": {"a_hist": (16, None), "b_hist": (16, None)},
    "lora_loaded": {"b_hist": (32, None)},
    "dn_state_loaded": {"a_conv": (64, None)},
    "rw_state_loaded": {"b_scale": (64, lambda st: st[3] == 0)},
    "past_k0_loaded": {"c_fetch_k": (32, lambda st: st[2] % 2 == 0)},
    "past_k1_loaded": {"c_fetch_k": (32, lambda st: st[2] % 2 == 1)},
    "past_v0_loaded": {"c_fetch_v": (32, lambda st: st[2] < 4)},
    "past_v1_loaded": {"c_fetch_v": (32, lambda st: st[2] >= 4)},
    "kv_stored": {"c_nat": (32, None)},
    "states_stored": {"a_o": (16, lambda st: st[2] == 1), "a_sout": (16, None), "b_fin": (64, None), "b_sout": (32, None)},
    "tail_rows_stored": {"a_convout": (32, None), "b_shiftout": (32, None)},
    "y_stored": {"finish": (16, None)},
    "a_conv_p": {"a_conv": (1, None)},
    "a_conv_s": {"a_conv": (1, None)},
    "a_done": {"a_norm4": (1, None)},
    "a_dst": {"a_sout": (1, None)},
    "a_exps": {"a_scale": (1, None)},
    "a_g": {"a_rows": (1, None)},
    "a_gb": {"a_scale": (1, None)},
    "a_gcol_t": {"a_rows": (1, None)},
    "a_kk": {"a_pairs": (1, None)},
    "a_klast": {"a_scale": (1, None)},
    "a_lt": {"a_pairs": (1, None)},
    "a_nat": {"a_pairs": (1, None)},
    "a_o": {"a_o": (1, None)},
    "a_os": {"a_o": (1, None)},
    "a_scaled": {"a_scale": (1, None)},
    "a_silu": {"a_silu": (1, None)},
    "a_sst": {"a_sout": (1, None)},
    "a_tanh": {"a_silu": (1, None)},
    "a_uex": {"a_sout": (1, None)},
    "a_unit": {"a_l2": (1, None)},
    "b_araw": {"b_lora": (1, None)},
    "b_at": {"b_lora": (1, None)},
    "b_bex": {"b_sout": (1, None)},
    "b_bm": {"b_kk": (1, None)},
    "b_bonus_done": {"b_bonus": (1, None)},
    "b_cleared": {"b_mix": (1, None)},
    "b_done": {"b_norm4": (1, None)},
    "b_ds": {"b_sout": (1, None)},
    "b_exps": {"b_scale": (1, None)},
    "b_fin_s": {"b_fin": (1, None)},
    "b_fin_t": {"b_fin": (1, None)},
    "b_kraw": {"b_kk": (1, None)},
    "b_lc": {"b_lora": (1, None)},
    "b_lt": {"b_lora": (1, None)},
    "b_m": {"b_pairs": (1, None)},
    "b_masked": {"b_pairs": (1, None)},
    "b_mixed": {"b_mix": (1, None)},
    "b_mixed_s": {"b_mix": (1, None)},
    "b_nats": {"b_pairs": (1, None)},
    "b_pcb": {"b_sout": (1, None)},
    "b_pcx": {"b_sout": (1, None)},
    "b_prep": {"b_kk": (1, None)},
    "b_rkm": {"b_bonus": (1, None)},
    "b_s_t": {"b_s0": (1, None)},
    "b_s_ts": {"b_s0": (1, None)},
    "b_scaled": {"b_scale": (1, None)},
    "b_snew": {"b_sout": (1, None)},
    "b_vs": {"b_nat": (1, None)},
    "b_vt": {"b_nat": (1, None)},
    "b_wp": {"b_w": (1, None)},
    "b_wraw": {"b_lora": (1, None)},
    "b_ws": {"b_w": (1, None)},
    "b_wt": {"b_lora": (1, None)},
    "b_y": {"b_y": (1, None)},
    "b_yc": {"b_norm1": (1, None)},
    "b_ys": {"b_y": (1, None)},
    "ba_ln": {"a_rows": (1, None)},
    "ba_neg": {"a_rows": (1, None)},
    "c_done": {"c_out": (1, None)},
    "c_e": {"c_prob": (1, None), "c_sprob": (1, None)},
    "c_max": {"c_score": (1, None), "c_sprob": (1, None)},
    "c_n": {"c_rms": (1, None)},
    "c_ns": {"c_nat": (1, None)},
    "c_nt": {"c_nat": (1, None)},
    "c_o": {"c_pv": (1, None)},
    "c_os": {"c_pv": (1, None)},
    "c_ot": {"c_out": (1, None)},
    "c_pt": {"c_prob": (1, None)},
    "c_pts": {"c_prob": (1, None)},
    "c_rope": {"c_rope": (1, None)},
    "c_s": {"c_score": (1, None)},
    "c_sdone": {"c_spv": (1, None)},
    "c_so": {"c_spv": (1, None)},
    "c_sp": {"c_sprob": (1, None)},
    "c_spt": {"c_sprob": (1, None)},
    "c_spts": {"c_sprob": (1, None)},
    "c_ssc": {"c_past": (1, None)},
    "c_sw": {"c_rope": (1, None)},
    "corrected": {"a_u": (1, None), "b_u": (1, None)},
    "corrected_s": {"a_u": (1, None), "b_u": (1, None)},
    "decay_rate": {"params": (1, None)},
    "h_ready": {"norm": (1, None)},
    "hist_in": {"a_hist": (1, None), "b_hist": (1, None)},
    "hist_t": {"a_hist": (1, None), "b_hist": (1, None)},
    "inv_roots": {"norm": (1, None), "a_l2": (1, None), "b_kk": (1, None), "c_rms": (1, None)},
    "out_normed": {"a_norm3": (1, None), "b_norm3": (1, None)},
    "out_roots": {"a_norm2": (1, None), "b_norm2": (1, None)},
    "out_squares": {"a_norm1": (1, None), "b_norm1": (1, None)},
    "out_sums": {"a_norm2": (1, None), "b_norm2": (1, None)},
    "out_t": {"a_norm3": (1, None), "b_norm3": (1, None)},
    "param_done": {"params": (1, None)},
    "param_t": {"params": (1, None)},
    "past_k_t": {"c_past": (1, None)},
    "past_k_ts": {"c_past": (1, None)},
    "projected": {"p_a": (1, None), "p_z": (1, None), "p_ba": (1, None), "p_f": (1, None), "p_c": (1, None), "p_g": (1, None), "p_up": (1, None), "p_y": (1, None), "p_pg": (1, None), "p_ple": (1, None)},
    "square_sums": {"norm": (1, None), "a_l2": (1, None), "b_kk": (1, None), "b_bonus": (1, None), "c_rms": (1, None)},
    "squares": {"norm": (1, None), "a_l2": (1, None), "b_kk": (1, None), "c_rms": (1, None)},
    "start_read": {"a_s0": (1, None), "b_s0": (1, None)},
    "start_reduced": {"a_s0": (1, None), "b_s0": (1, None)},
    "tail_rows": {"a_convout": (1, None), "b_shiftout": (1, None)},
    "tails": {"a_convout": (1, None), "b_shiftout": (1, None)},
    "tails_t": {"a_convout": (1, None), "b_shiftout": (1, None)},
    "tri_i0": {"tri": (1, None)},
    "tri_t0": {"tri": (1, None)},
    "tri_tr": {"tri": (1, None)},
    "tri_up": {"lev": (1, None)},
    "tri_y": {"lev": (2, None)},
    "tri_ys": {"lev": (2, None)},
    "tri_zt": {"lev": (1, None)},
    "tri_z": {"lev": (1, lambda st: st[3] < (NLEV - 1 if st[2] < 2 else 1))},
    "tri_iup": {"lev": (1, lambda st: st[3] < (NLEV - 1 if st[2] < 2 else 1))},
    "x_next": {"p_ple": (1, None)},
    "x_t": {"x_in": (1, None)},
    "x_tr": {"x_in": (1, None)},
    "y_rows": {"finish": (1, None)},
    "y_t": {"finish": (1, None)},
    "z_tanh": {"p_z": (1, None)},
    "a_ks": {"a_w": (1, lambda st: st[2] == 1)},
    "a_w": {"a_w": (1, lambda st: st[2] > 0)},
    "a_state": {"a_o": (1, lambda st: st[2] < 2)},
    "b_state": {"b_y": (1, lambda st: st[3] < 2)},
    "c_qx": {"c_nat": (1, lambda st: st[2] == 0)},
    "merged": {"p_up": (1, lambda st: st[2] > 0)},
    "tri_lm": {"tri": (1, None), "lev": (1, lambda st: st[3] < (NLEV - 1 if st[2] < 2 else 1))},
}
PROJECTIONS = ("p_a", "p_z", "p_ba", "p_f", "p_c", "p_g", "p_up", "p_y", "p_pg", "p_ple")


class Steps:

    def __init__(self, nc, ctx, order):
        self.nc, self.ctx, self.order, self.at, self.sems, self.totals = nc, ctx, order, 0, {}, {}
        for name, where in SIGNALS.items():
            self.tally(name, [self.by(st, where) for st in order])
        projections = [int(st[0] in PROJECTIONS) for st in order]
        number = np.cumsum(projections) - 1
        for b in range(3):
            self.tally(f"bank{b}_read", [int(p and n % 3 == b) for p, n in zip(projections, number)])

    @staticmethod
    def by(st, where):
        by, when = where.get(st[0], (0, None))
        return by if by and (when is None or when(st)) else 0

    def tally(self, name, values):
        self.totals[name] = [0] + [int(v) for v in np.cumsum(values)]

    def sem(self, name):
        if name not in self.sems:
            self.sems[name] = self.ctx.enter_context(self.nc.semaphore(name))
        return self.sems[name]

    def count(self, name, upto=None):
        return self.totals[name][(self.at if upto is None else upto) + 1]


def schedule():
    order = [("x_in", 0, t) for t in range(3)]
    for l in range(DEPTH):
        spare = []

        def add(*s):
            order.append((s[0], l) + s[1:])

        def fill(n=1):
            for _ in range(min(n, len(spare))):
                add(*spare.pop(0))

        add("params")
        add("norm")
        add("a_hist")
        for m in range(NA):
            add("p_a", m)
        add("p_ba")
        spare += [("p_z", 0, m) for m in range(4)] + [("p_f", m) for m in range(NF)]
        spare += [("p_z", 1, m) for m in range(4)] + [("p_c", m) for m in range(NC3)]
        spare += [("p_z", 2, m) for m in range(4)]
        add("a_convout")
        add("a_conv")
        fill(4)
        for c in range(3):
            add("a_silu", c)
            fill(1)
        for i in range(2):
            add("a_l2", i)
            fill(2)
        add("a_rows")
        fill(1)
        parts = []

        def part():
            if parts:
                add(*parts.pop(0))

        for t in range(3):
            add("a_scale", t)
            fill(1)
            add("a_pairs", t)
            fill(1)
            add("tri", t)
            part()
            for k in range(1, NLEV if t < 2 else 2):
                add("lev", t, k)
                part()
                fill(k in (1, 4))
            if t == 2:
                for h in range(4):
                    add("a_s0", h)
                    fill(1)
                    part()
            add("a_w", t)
            add("a_u", t)
            fill(1)
            add("a_o", t)
            parts += [(f"a_norm{i}", t) for i in range(1, 5)]
        for h in range(4):
            fill(1)
            add("a_sout", h)
            part()
        fill(max(0, len(spare) - SPARE_B))
        add("b_hist")
        add("b_shiftout")
        fill(1)
        add("b_mix")
        spare += [("p_g", m) for m in range(NF)]
        fill(2)
        add("b_lora")
        fill(1)
        add("b_kk")
        fill(1)
        add("b_bonus")
        fill(1)
        for g in range(2):
            for t in range(3):
                add("b_nat", g, t)
                add("b_scale", g, t)
                add("b_pairs", g, t)
                fill(1 if t else 0)
                add("tri", t)
                part()
                for k in range(1, NLEV if t < 2 else 2):
                    add("lev", t, k)
                    part()
                if t == 2:
                    add("b_s0", g, 0)
                    part()
                    fill(1)
                    add("b_s0", g, 1)
                    part()
                    add("b_fin", g)
                add("b_w", g, t)
                fill(1 if t == 2 else 0)
                add("b_u", g, t)
                add("b_y", g, t)
                fill(1 if t == 2 else 0)
                parts += [(f"b_norm{i}", g, t) for i in range(1, 5)]
            part()
            add("b_sout", g, 0)
            part()
            add("b_sout", g, 1)
            fill(1)
            if g == 1:
                part()
                part()
        spare += [("p_g", m) for m in range(NF, 24)]
        for q in range(4):
            if q < 2:
                add("c_fetch_k", q)
            add("c_fetch_v", q)
        for i in range(2):
            add("c_rms", i)
            fill(1)
            add("c_rope", i)
            fill(1)
        add("c_nat", 0)
        add("c_nat", 1)

        def sampled(g):
            for j in range(4):
                add("c_past", g, j)
                if 4 * g + j + 2 < NSEQ:
                    add("c_fetch_k", 4 * g + j + 2)
            fill(1)
            add("c_sprob", g)
            fill(1)
            add("c_spv", g)

        sampled(0)
        for q in range(4, 8):
            add("c_fetch_v", q)
        for t in range(2):
            for g in range(2):
                add("c_score", t, g)
                if g == t:
                    fill(1)
                add("c_prob", t, g)
                add("c_pv", t, g)
            add("c_out", t)
            fill(1)
        sampled(1)
        fill(len(spare))
        for m in range(0, 8, 2):
            for n in range(3):
                add("p_up", n, m)
                add("p_up", n, m + 1)
        for m in range(8):
            add("p_y", m)
        for m in range(8):
            add("p_pg", m)
            add("p_ple", m)
    order += [("finish", DEPTH, t) for t in range(3)]
    return order


def weight_chunks(A, order):
    w_in = A["w_in"].rearrange("l (k p) n -> l p k n", p=128)
    w_br = A["w_branch"].rearrange("l b (k p) n -> l b p k n", p=128)
    w_out = A["w_out"].rearrange("l (k p) n -> l p k n", p=128)
    w_pg = A["w_pg"].rearrange("l (k p) n -> l p k n", p=128)
    w_ple = A["w_ple"].rearrange("l (k p) n -> l p k n", p=128)
    chunks, use, open_ = [], {}, {}

    def tile(step, key, view, k, col0, cols):
        if key not in open_:
            open_[key] = len(chunks)
            chunks.append([step, step, view, k, cols])
        c = chunks[open_[key]]
        c[1] = step
        use[step] = (open_[key], col0)

    for i, st in enumerate(order):
        kind, l = st[0], (st[1] if len(st) > 1 else 0)
        m = st[-1]
        if kind in ("p_a", "p_f", "p_c", "p_g", "p_z"):
            off = {"p_a": OFF_QKVA, "p_f": OFF_F, "p_c": OFF_QKVC, "p_g": OFF_G}.get(kind)
            key = (kind, l, m // 2)
            if kind == "p_z":
                off = (OFF_ZA, OFF_ZB, OFF_ZC)[st[2]]
                key = (kind, l, st[2], m // 2)
            a = off + 256 * (m // 2)
            n = 128 if (kind == "p_f" and m == NF - 1) else 256
            tile(i, key, w_in[l, :, :, a:a + n], KT_, 128 * (m % 2), n)
        elif kind == "p_ba":
            tile(i, (kind, l), w_in[l, :, :, OFF_BA:OFF_BA + 8], KT_, 0, 8)
        elif kind == "p_up":
            n = st[2]
            a = 256 * (m // 2)
            tile(i, (kind, l, n, m // 2), w_br[l, n, :, :, a:a + 256], 4, 128 * (m % 2), 256)
        elif kind in ("p_y", "p_pg"):
            a = 256 * (m // 2)
            tile(i, (kind, l, m // 2), (w_out if kind == "p_y" else w_pg)[l, :, :, a:a + 256], KT_,
                 128 * (m % 2), 256)
        elif kind == "p_ple":
            tile(i, (kind, l), w_ple[l], 2, 128 * m, 1024)
    return chunks, use


def program(nc, A, O):
    order = schedule()
    chunks, use = weight_chunks(A, order)
    steps_of = {}
    for i, st in enumerate(order):
        steps_of.setdefault(st[0], []).append(i)
    ctx = ExitStack()
    with ctx:
        S = Steps(nc, ctx, order)

        def sb(name, shape, dt=FP32):
            return ctx.enter_context(nc.sbuf_tensor(name, shape, dt))

        CN = sb("consts", [128, CONSTS.shape[1]])
        ring = sb("ring", [128, RING, SLOT])
        XA = sb("x_a", [128, 8, NTOK])
        XB = sb("x_b", [128, 8, NTOK])
        Z = sb("z", [128, 3, 4, NTOK])
        UQ = sb("conv_in", [128, NA * (UW + NSEQ * US)])
        U = UQ[:, :].rearrange("p (m n) -> p m n", m=NA)
        QC = UQ[:, 0:NC3 * NTOK].rearrange("p (m n) -> p m n", m=NC3)
        F = sb("shift_in", [128, NF, FW + NSEQ * FS])
        PT = sb("params", [128, NPAR])
        PH = sb("params_half", [128, NPAR])
        HP = sb("head_params", [4, 4])
        PLT = sb("ple_t", [128, 2, NTOK])
        TH = sb("tanh_z", [128, 2, NTOK])
        TMP = sb("tmp", [128, 4, NTOK])
        PLN = TMP[:, :, :].rearrange("p a n -> p (a n)")[:, 0:3 * D_PLE].rearrange("p (a n) -> p a n", a=3)
        CT = sb("tails", [128, NA * 27])
        ROWS = sb("rows", [27, SHIFT_B])
        PRN = sb("param_rows", [128, 2, 128])
        PTAB = sb("pages", [1, NSEQ * 2], I32)
        LT = sb("tri_lower_t", [128, 4, 128])
        LM = sb("tri_level_t", [128, 4, 128])
        TI = sb("tri_inv", [128, 4, 128])
        TT = sb("tri_inv_t", [128, 4, 128])
        Y = sb("tri_mid", [128, 4, 128])
        WLO = Y[:, :, :].rearrange("p a n -> p (a n)")
        ARW = 18432
        arena = sb("arena", [128, ARW])
        PS = ctx.enter_context(nc.psum_tensor("psum", [128, 8, 512], FP32))
        M = [PS[:, 3 + b, :] for b in range(5)]

        top = [0]

        def part(*shape):
            n = int(np.prod(shape))
            a = arena[:, top[0]:top[0] + n]
            top[0] += n
            assert top[0] <= ARW, top[0]
            names = "abcd"[:len(shape)]
            if len(shape) > 1:
                a = a.rearrange("p (%s) -> p %s" % (" ".join(names), " ".join(names)),
                                **{c: int(k) for c, k in zip(names[1:], shape[1:])})
            return a

        UC = part(NA, NTOK)
        SD = part(4, NSEQ, 128)
        AEG, AGB, ADI, AKB, AVB, AKD = (part(4, 128) for _ in range(6))
        AKQ = part(1024)
        AVN, AKN, AQK, AW, AU, AST, AR = (part(4, 128) for _ in range(7))
        AEX = part(NSEQ, 128)
        ABG = part(2, NTOK)
        ATM = AEX.rearrange("p a b -> p (a b)")[:, 0:3 * NTOK].rearrange("p (a b) -> p a b", a=3)
        AGC = part(3, 4)
        ASM = part(2, 4)
        top[0] = 0
        FM = part(NF, NTOK)
        LW, AA, LC, KK = (part(4, NTOK) for _ in range(4))
        BON = TMP
        BE = part(3, 2, 128)
        BAR, BBK = part(512), part(512)
        BN = part(2, 2, 128)
        BVN = part(2, 128)
        BRB = part(4, 128)
        BKK = part(1024)
        BW, BU, BY, BSO = (part(2, 128) for _ in range(4))
        BQ = BW
        BSM = part(3, 4)
        BST = part(2, 128)
        BSB = part(2, NSEQ, 128)
        BX = part(2, NSEQ, 128)
        BR = part(2, 128)
        BM = part(4, 12)
        top[0] = 0
        CSQ = part(4, NTOK)
        CKN, CVN = part(3, W), part(3, W)
        CP = part(4, 256)
        CPT = part(2, 4, 128)
        CON = part(W)
        CMX = part(3, 4)
        CQX = part(4, NSEQ, 32)
        CKR = part(2, 2, W)
        CVR = part(4, 2, W)
        CKT = part(2, 4, 256)
        GTC = part(8, NTOK)
        CPS = CP.rearrange("p a b -> p (a b)")[:, 0:NTOK]
        CPTS = CPT.rearrange("p a b c -> p (a b c)")[:, 0:384].rearrange("p (a b) -> p a b", a=3)
        top[0] = 0
        STG = part(3, D_MODEL)
        MG = QC
        XN = arena[:, 0:3 * D_MODEL].rearrange("p (t n) -> p t n", t=3)

        def C(name, rows=128):
            a, n = CONST_LAYOUT[name]
            return CN[0:rows, a:a + n]

        def P(name, i=0, rows=128):
            c = PAT[name] + i
            return PT[0:rows, c:c + 1]

        def gate(m):
            return F[:, m, 0:NTOK] if m < NF else GTC[:, m - NF, :] if m < NF + 8 else CSQ[:, m - NF - 8, :]

        def Phalf(name, i=0):
            c = PAT[name] + i
            return PH[:, c:c + 1]

        def bc(ap, axis, shape):
            return ap.unsqueeze(axis).to_broadcast(shape)

        def v4(b, w, rows=128):
            return b[0:rows, 0:4 * w].rearrange("p (h n) -> p h n", h=4)

        def vx(buf, n, w, rows=128):
            return buf[0:rows, 0:2 * n * w].rearrange("p (h x n) -> p h x n", h=n, x=2)

        def of_half(buf, hh):
            return buf[:, :, :].rearrange("p (q h) n -> p q h n", h=2)[:, :, hh, :]

        def seqs(ap):
            return ap.rearrange("p (s c) -> p s c", c=LS)

        ident = C("ident")
        Us = U[:, :, UW:].rearrange("p m (s c) -> p m s c", c=US)
        Fs = F[:, :, FW:].rearrange("p m (s c) -> p m s c", c=FS)
        X = lambda l: (XA, XB)[l % 2]
        H = lambda l: (XB, XA)[l % 2]
        tok = lambda t: slice(TILES[t][0], TILES[t][0] + TILES[t][1])
        wid = lambda t: TILES[t][1]
        last_level = lambda t: NLEV - 1 if t < 2 else 1

        proj_at = [i for i, st in enumerate(order) if st[0].startswith("p_")]
        proj_no = {i: n for n, i in enumerate(proj_at)}

        def bank():
            return PS[:, proj_no[S.at] % 3, :]

        def freed(i=None):
            return f"bank{proj_no[S.at if i is None else i] % 3}_read"

        def before(kind, n=1):
            past = [i for i in steps_of[kind] if i < S.at]
            return past[-n] if len(past) >= n else None

        block = ctx.enter_context(nc.Block())

        @block.sync
        def _(sp):
            loaded = [0]

            def load_chunk():
                c = loaded[0]
                if c >= len(chunks):
                    return
                loaded[0] += 1
                first, last, view, k, cols = chunks[c]
                if c >= RING:
                    sp.wait_ge(S.sem("projected"), S.count("projected", chunks[c - RING][1]))
                dst = ring[:, c % RING, 0:k * cols].rearrange("p (k n) -> p k n", k=k)
                sp.dma_start(dst, view).then_inc(S.sem(f"ring{c % RING}_loaded"), 16)

            def x_in(l, t):
                if t:
                    return
                sp.dma_start(CN[:, :], A["const_table"]).then_inc(S.sem("consts_loaded"), 16)
                sp.dma_start(XN[:, 0, :], A["x_prompt"][0, 0:128, :]).then_inc(S.sem("x_loaded"), 16)
                sp.dma_start(XN[:, 1, :], A["x_prompt"][0, 128:256, :]).then_inc(S.sem("x_loaded"), 16)
                sp.dma_start(XN[0:32, 2, :], A["x_sample"].rearrange("s t d -> (s t) d")).then_inc(S.sem("x_loaded"), 16)
                sp.dma_start(PTAB[:, :], A["page_table"].rearrange("s n -> (s n)")
                                  .rearrange("(o n) -> o n", o=1)).then_inc(S.sem("pages_loaded"), 16)
                for _ in range(RING):
                    load_chunk()

            def params(l):
                if l:
                    sp.wait_ge(S.sem("param_t"), S.count("param_t", S.at - 1))
                    sp.wait_ge(S.sem("a_g"), S.count("a_g", S.at - 1))
                    sp.wait_ge(S.sem("x_next"), S.count("x_next", S.at - 1))
                for name, k in PROWS:
                    r = PAT[name]
                    if name in ("qn_c", "kn_c"):
                        for half in range(2):
                            sp.dma_start(PRN[r:r + 1, 0, 64 * half:64 * half + 64], A[name][l:l + 1, :]).then_inc(S.sem("param_rows_loaded"), 16)
                    else:
                        src = A[name][l].rearrange("h n -> (h n)") if name == "rk_b" else A[name][l]
                        sp.dma_start(PRN[r:r + k, 0, :], src.rearrange("(k n) -> k n", n=128)).then_inc(S.sem("param_rows_loaded"), 16)
                sp.dma_start(PRN[0:48, 1, :], A["conv_a"][l].rearrange("j (m n) -> (j m) n", n=128)).then_inc(S.sem("param_rows_loaded"), 16)
                sp.dma_start(HP[:, 0:1], A["dt_bias"][l].rearrange("(h o) -> h o", o=1)).then_inc(S.sem("heads_loaded"), 16)
                sp.dma_start(HP[:, 1:2], A["a_log"][l].rearrange("(h o) -> h o", o=1)).then_inc(S.sem("heads_loaded"), 16)
                for t, (a, n) in enumerate(TILES):
                    src = A["p_prompt"][l, 0, a:a + n, :] if t < 2 else A["p_sample"][l].rearrange("s t d -> (s t) d")
                    sp.dma_start(PLN[0:n, t, :], src).then_inc(S.sem("ple_rows_loaded"), 16)

            def a_hist(l):
                if l:
                    sp.wait_ge(S.sem("tail_rows_stored"), S.count("tail_rows_stored", S.at - 1))
                sp.dma_start(ROWS[0:24, 0:QKV_A], A["state_dn_conv"][l].rearrange("s c n -> (s c) n")).then_inc(S.sem("hist_loaded"), 16)

            def a_conv(l):
                if l:
                    sp.wait_ge(S.sem("x_next"), S.count("x_next", S.at - 1))
                sp.wait_ge(S.sem("x_t"), S.count("x_t"))
                for h in range(4):
                    sp.dma_start(SD[:, h, :, :], A["state_dn"][l, :, h].rearrange("s k v -> k s v")).then_inc(S.sem("dn_state_loaded"), 16)

            def b_hist(l):
                sp.wait_ge(S.sem("tail_rows_stored"), S.count("tail_rows_stored"))
                sp.dma_start(ROWS[0:8, :], A["state_rwkv_shift"][l]).then_inc(S.sem("hist_loaded"), 16)
                sp.wait_ge(S.sem("tri_up"), S.count("tri_up"))
                for half, name in enumerate(("w2_b", "a2_b")):
                    sp.dma_start(WLO[64 * half:64 * half + 64, :], A[name][l]).then_inc(S.sem("lora_loaded"), 16)

            def b_scale(l, g, t):
                if t != 0:
                    return
                if g == 0:
                    sp.wait_ge(S.sem("b_cleared"), S.count("b_cleared"))
                else:
                    sp.wait_ge(S.sem("states_stored"), S.count("states_stored"))
                for pr in range(2):
                    for hh in range(2):
                        r = slice(64 * hh, 64 * hh + 64)
                        sp.dma_start(BSB[r, pr, :, r],
                                          A["state_rwkv"][l, :, 4 * g + 2 * pr + hh].rearrange("s v k -> v s k")).then_inc(S.sem("rw_state_loaded"), 16)

            def fetch(cache, l, s, dst, name):
                for pg in range(2):
                    r = sp.value_load(PTAB[0:1, 2 * s + pg:2 * s + pg + 1], min_val=0,
                                      max_val=A["cache_k"].shape[1] - 1)
                    src = cache[l, bass.ds(r, 1), :, :, :].rearrange("o p h d -> (o p) (h d)")
                    sp.dma_start(dst[:, pg, :], src).then_inc(S.sem(name), 16)

            def c_fetch_k(l, s):
                if s == 0:
                    sp.wait_ge(S.sem("pages_loaded"), S.count("pages_loaded"))
                    sp.wait_ge(S.sem("b_done"), S.count("b_done"))
                    sp.wait_ge(S.sem("b_snew"), S.count("b_snew"))
                    sp.wait_ge(S.sem("states_stored"), S.count("states_stored"))
                if s >= 2:
                    sp.wait_ge(S.sem("past_k_t"), S.count("past_k_t"))
                fetch(A["cache_k"], l, s, CKR[:, s % 2], f"past_k{s % 2}_loaded")

            def c_fetch_v(l, s):
                if s >= 4:
                    sp.wait_ge(S.sem("c_so"), S.count("c_so"))
                fetch(A["cache_v"], l, s, CVR[:, s % 4], f"past_v{s // 4}_loaded")

            do = dict(x_in=x_in, params=params, a_hist=a_hist, a_conv=a_conv, b_hist=b_hist, b_scale=b_scale,
                      c_fetch_k=c_fetch_k, c_fetch_v=c_fetch_v)
            for i, st in enumerate(order):
                S.at = i
                if st[0] in do:
                    do[st[0]](*st[1:])
                if i in use and chunks[use[i][0]][1] == i:
                    load_chunk()

        @block.tensor
        def _(pe):
            mm = pe.matmul

            def tr(out, in_, w=128):
                return pe.transpose(out, in_, ident[0:w, 0:w])

            def x_in(l, t):
                w = wid(t)
                if t == 0:
                    pe.wait_ge(S.sem("consts_loaded"), S.count("consts_loaded"))
                    pe.wait_ge(S.sem("x_loaded"), S.count("x_loaded"))
                if t == 2:
                    pe.wait_ge(S.sem("x_t"), S.count("x_t", S.at - 2))
                for k in range(8):
                    ins = tr(M[2 * (t % 2) + k // 4][:, (k % 4) * w:(k % 4) * w + w], XN[0:w, t, 128 * k:128 * k + 128], w)
                ins.then_inc(S.sem("x_tr"), 1)

            def params(l):
                pe.wait_ge(S.sem("param_rows_loaded"), S.count("param_rows_loaded"))
                pe.wait_ge(S.sem("ple_rows_loaded"), S.count("ple_rows_loaded"))
                pe.wait_ge(S.sem("x_t"), S.count("x_t", S.at - 1))
                if l:
                    pe.wait_ge(S.sem("c_sdone"), S.count("c_sdone", S.at - 1))
                tr(M[0][:, 0:NP1], PRN[0:NP1, 0, :], NP1)
                tr(M[0][:, NP1:NPAR], PRN[0:48, 1, :], 48)
                for t in range(3):
                    for k in range(2):
                        ins = tr(M[1 + k][:, tok(t)], PLN[0:wid(t), t, 128 * k:128 * k + 128], wid(t))
                ins.then_inc(S.sem("param_t"), 1)

            def norm(l):
                pe.wait_ge(S.sem("squares"), S.count("squares"))
                pe.wait_ge(S.sem("param_done"), S.count("param_done"))
                for k in range(8):
                    ins = mm(M[0][:, 0:NTOK], C("ones"), H(l)[:, k, :], start=k == 0, stop=k == 7)
                ins.then_inc(S.sem("square_sums"), 1)

            def project(k_tiles, rhs, m_cols=128):
                c, col = use[S.at]
                n = proj_no[S.at]
                cols = chunks[c][4]
                pe.wait_ge(S.sem(f"ring{c % RING}_loaded"), 16 * (c // RING + 1))
                if n >= 3:
                    pe.wait_ge(S.sem(freed()), S.count(freed(), proj_at[n - 3]))
                for k in range(k_tiles):
                    lhs = ring[:, c % RING, k * cols + col:k * cols + col + m_cols]
                    ins = mm(bank()[0:m_cols, 0:NTOK], lhs, rhs(k), start=k == 0, stop=k == k_tiles - 1)
                return ins

            def p_h(l, *m):
                pe.wait_ge(S.sem("h_ready"), S.count("h_ready"))
                project(KT_, lambda k: H(l)[:, k, :]).then_inc(S.sem("projected"), 1)

            def p_ba(l):
                c, _ = use[S.at]
                pe.wait_ge(S.sem("h_ready"), S.count("h_ready"))
                project(KT_, lambda k: H(l)[:, k, :], 4)
                pe.wait_ge(S.sem("b_done"), S.count("b_done"))
                pe.wait_ge(S.sem("c_spts"), S.count("c_spts"))
                for k in range(KT_):
                    ins = mm(M[4][0:4, 0:NTOK], ring[:, c % RING, k * 8 + 4:k * 8 + 8], H(l)[:, k, :],
                             start=k == 0, stop=k == KT_ - 1)
                ins.then_inc(S.sem("projected"), 1)

            def p_up(l, n, m):
                pe.wait_ge(S.sem(("a_done", "b_done", "c_sdone")[n]), S.count(("a_done", "b_done", "c_sdone")[n]))
                pe.wait_ge(S.sem("c_done"), S.count("c_done"))
                project(4, lambda k: Z[:, n, k, :]).then_inc(S.sem("projected"), 1)

            def p_y(l, m):
                pe.wait_ge(S.sem("merged"), S.count("merged"))
                project(8, lambda k: MG[:, k, :]).then_inc(S.sem("projected"), 1)

            def p_pg(l, m):
                for b in range(3):
                    pe.wait_ge(S.sem(f"bank{b}_read"), S.count(f"bank{b}_read", before("p_y")))
                project(8, lambda k: X(l)[:, k, :]).then_inc(S.sem("projected"), 1)

            def p_ple(l, m):
                project(2, lambda k: PLT[:, k, :]).then_inc(S.sem("projected"), 1)

            def a_hist(l):
                pe.wait_ge(S.sem("hist_loaded"), S.count("hist_loaded"))
                pe.wait_ge(S.sem("inv_roots"), S.count("inv_roots"))
                for m in range(NA):
                    ins = tr(M[0][:, 24 * m:24 * m + 24], ROWS[0:24, 128 * m:128 * m + 128], 24)
                ins.then_inc(S.sem("hist_t"), 1)

            def a_convout(l):
                pe.wait_ge(S.sem("tails"), S.count("tails"))
                for m in range(NA):
                    ins = tr(M[1 + m // 4][0:27, (m % 4) * 128:(m % 4) * 128 + 128], CT[:, 27 * m:27 * m + 27])
                ins.then_inc(S.sem("tails_t"), 1)

            def ones4(src, weights, name):
                for h in range(4):
                    ins = mm(M[h][:, 0:NTOK], weights, src[:, h, :], start=True, stop=True)
                ins.then_inc(S.sem(name), 1)

            def a_l2(l, i):
                pe.wait_ge(S.sem("squares"), S.count("squares"))
                pe.wait_ge(S.sem("tail_rows"), S.count("tail_rows"))
                ones4(TMP, C("ones"), "square_sums")

            def a_rows(l):
                pe.wait_ge(S.sem("a_g"), S.count("a_g"))
                for t in range(3):
                    ins = tr(M[4][0:wid(t), 4 * t:4 * t + 4], ABG[0:4, 1, tok(t)], 4)
                ins.then_inc(S.sem("a_gcol_t"), 1)

            def a_scale(l, t):
                w = wid(t)
                pe.wait_ge(S.sem("a_unit"), S.count("a_unit"))
                pe.wait_ge(S.sem("a_state"), S.count("a_state"))
                pe.wait_ge(S.sem("a_nat"), S.count("a_nat"))
                for i in range(2):
                    for h in range(4):
                        ins = mm(v4(M[i], w)[:, h, :], C("pick_head", 4)[:, 128 * h:128 * h + 128],
                                 ABG[0:4, 1 - i, tok(t)], start=True, stop=True)
                ins.then_inc(S.sem("a_gb"), 1)

            def a_pairs(l, t):
                w = wid(t)
                pe.wait_ge(S.sem("a_scaled"), S.count("a_scaled"))
                for h in range(4):
                    mm(v4(M[2], w, w)[:, h, :], UC[:, 4 + h, tok(t)], AKB[:, h, 0:w], start=True, stop=True)
                for h in range(4):
                    mm(v4(M[3], w, w)[:, h, :], UC[:, 4 + h, tok(t)], UC[:, h, tok(t)], start=True, stop=True)
                for h in range(4):
                    tr(v4(M[4], 128, w)[:, h, :], AVB[:, h, 0:w])
                for h in range(4):
                    ins = tr(v4(M[0], 128, w)[:, h, :], AKD[:, h, 0:w])
                ins.then_inc(S.sem("a_kk"), 1)

            def tri(l, t):
                w = wid(t)
                pe.wait_ge(S.sem("tri_t0"), S.count("tri_t0"))
                pe.wait_ge(S.sem("a_nat"), S.count("a_nat"))
                pe.wait_ge(S.sem("b_vs"), S.count("b_vs"))
                for h in range(4):
                    ins = tr(v4(M[0], w, w)[:, h, :], TT[0:w, h, 0:w], w)
                ins.then_inc(S.sem("tri_tr"), 1)

            def lev(l, t, k):
                w = wid(t)
                pe.wait_ge(S.sem("tri_lm"), S.count("tri_lm", S.at - 1))
                pe.wait_ge(S.sem("tri_i0"), S.count("tri_i0"))
                pe.wait_ge(S.sem("tri_iup"), S.count("tri_iup", S.at - 1))
                for h in range(4):
                    ins = mm(v4(M[h // 2], w, w)[:, h, :], LM[0:w, h, 0:w], TI[0:w, h, 0:w], start=True, stop=True)
                    if h % 2:
                        ins.then_inc(S.sem("tri_y"), 1)
                pe.wait_ge(S.sem("tri_up"), S.count("tri_up", S.at - 1))
                pe.wait_ge(S.sem("tri_ys"), S.count("tri_ys") - 1)
                if k < last_level(t):
                    for h in range(4):
                        if h == 2:
                            pe.wait_ge(S.sem("tri_ys"), S.count("tri_ys"))
                        ins = mm(v4(M[2], w, w)[:, h, :], TT[0:w, h, 0:w], Y[0:w, h, 0:w], start=True, stop=True)
                    ins.then_inc(S.sem("tri_z"), 1)
                for h in range(4):
                    if h == 2:
                        pe.wait_ge(S.sem("tri_ys"), S.count("tri_ys"))
                    ins = mm(v4(M[3], w, w)[:, h, :], Y[0:w, h, 0:w], TT[0:w, h, 0:w], start=True, stop=True)
                ins.then_inc(S.sem("tri_zt"), 1)

            def a_s0(l, h):
                pe.wait_ge(S.sem("dn_state_loaded"), S.count("dn_state_loaded"))
                pe.wait_ge(S.sem("tri_up"), S.count("tri_up"))
                if h >= 2:
                    pe.wait_ge(S.sem("start_reduced"), S.count("start_reduced", S.at - 2))
                b = 2 * (h % 2)
                for c in range(2):
                    ins = mm(M[b + c][0:64, :], AKQ[:, 64 * h:64 * h + 64], SD[:, h, 4 * c:4 * c + 4, :],
                             start=True, stop=True)
                ins.then_inc(S.sem("start_read"), 1)

            def a_w(l, t):
                if t == 1:
                    pe.wait_ge(S.sem("tri_up"), S.count("tri_up"))
                    for h in range(4):
                        ins = mm(v4(M[0], 128)[:, h, :], vx(AKQ, 4, 128)[:, h, 0, :], AST[:, h, :], start=True, stop=True)
                    ins.then_inc(S.sem("a_ks"), 1)

            def a_u(l, t):
                w = wid(t)
                pe.wait_ge(S.sem("tri_up"), S.count("tri_up"))
                pe.wait_ge(S.sem("a_w" if t else "a_nat"), S.count("a_w" if t else "a_nat"))
                pe.wait_ge(S.sem("start_reduced"), S.count("start_reduced"))
                for h in range(4):
                    rhs = (AW if t else AVN)[0:w, h, :]
                    ins = mm(v4(M[1], 128, w)[:, h, :], TT[0:w, h, 0:w], rhs, start=True, stop=True)
                ins.then_inc(S.sem("corrected"), 1)

            def a_o(l, t):
                w = wid(t)
                pe.wait_ge(S.sem("corrected_s"), S.count("corrected_s"))
                for h in range(4):
                    out = v4(M[2], 128, w)[:, h, :]
                    if t == 1:
                        mm(out, vx(AKQ, 4, 128)[:, h, 1, :], AST[:, h, :], start=True, stop=False)
                    ins = mm(out, AQK[0:w, h, 0:w], AU[0:w, h, :], start=t != 1, stop=True)
                if t == 2:
                    ins.then_inc(S.sem("a_o"), 1)
                    return
                for h in range(4):
                    ins = mm(v4(M[3], 128)[:, h, :], AKN[0:w, h, :], AU[0:w, h, :], start=True, stop=True)
                ins.then_inc(S.sem("a_o"), 1)

            def a_norm3(l, t):
                w = wid(t)
                pe.wait_ge(S.sem("a_nat"), S.count("a_nat"))
                pe.wait_ge(S.sem("out_normed"), S.count("out_normed"))
                for h in range(4):
                    ins = tr(v4(M[4], w)[:, h, :], AW[0:w, h, :], w)
                ins.then_inc(S.sem("out_t"), 1)

            def a_sout(l, h):
                pe.wait_ge(S.sem("a_uex"), S.count("a_uex"))
                b = 2 * (h % 2)
                for c in range(2):
                    ins = mm(M[b + c], AKN[0:32, h, :], AEX[0:32, 4 * c:4 * c + 4, :], start=True, stop=True)
                ins.then_inc(S.sem("a_dst"), 1)

            def b_hist(l):
                pe.wait_ge(S.sem("hist_loaded"), S.count("hist_loaded"))
                pe.wait_ge(S.sem("a_sst"), S.count("a_sst"))
                for m in range(NF):
                    ins = tr(M[0][:, 8 * m:8 * m + 8], ROWS[0:8, 128 * m:128 * m + 128], 8)
                ins.then_inc(S.sem("hist_t"), 1)

            def b_shiftout(l):
                pe.wait_ge(S.sem("tails"), S.count("tails"))
                pe.wait_ge(S.sem("hist_in"), S.count("hist_in"))
                for m in range(NF):
                    ins = tr(M[m // 4][0:9, (m % 4) * 128:(m % 4) * 128 + 128], CT[:, 9 * m:9 * m + 9])
                ins.then_inc(S.sem("tails_t"), 1)

            def b_lora(l):
                pe.wait_ge(S.sem("lora_loaded"), S.count("lora_loaded"))
                pe.wait_ge(S.sem("b_lt"), S.count("b_lt"))
                for h in range(4):
                    ins = mm(M[h][:, 0:NTOK], WLO[0:64, 128 * h:128 * h + 128], FM[0:64, NF - 1, :], start=True, stop=True)
                ins.then_inc(S.sem("b_wraw"), 1)
                pe.wait_ge(S.sem("b_wt"), S.count("b_wt"))
                for h in range(4):
                    ins = mm(M[h][:, 0:NTOK], WLO[64:128, 128 * h:128 * h + 128], FM[64:128, NF - 1, :], start=True, stop=True)
                ins.then_inc(S.sem("b_araw"), 1)

            def b_kk(l):
                pe.wait_ge(S.sem("squares"), S.count("squares"))
                ones4(TMP, C("ones_head"), "square_sums")

            def b_bonus(l):
                pe.wait_ge(S.sem("b_rkm"), S.count("b_rkm"))
                ones4(TMP, C("ones_head"), "square_sums")

            def b_pairs(l, g, t):
                w = wid(t)
                pe.wait_ge(S.sem("b_scaled"), S.count("b_scaled"))
                pe.wait_ge(S.sem("b_vs"), S.count("b_vs"))
                ar, bk = vx(BAR, 2, w), vx(BBK, 2, w)
                for x in range(2):
                    for hd in range(4):
                        pr, r = hd // 2, slice(64 * (hd % 2), 64 * (hd % 2) + 64)
                        out = M[2 * x + hd % 2][0:w, 2 * w * pr:2 * w * pr + 2 * w]
                        mm(out, bk[r, pr, x, :], BAR[r, 2 * w * pr:2 * w * pr + 2 * w], start=True, stop=True)
                for pr in range(2):
                    for x in range(2):
                        ins = tr(M[4][0:w, (2 * pr + x) * 128:(2 * pr + x) * 128 + 128], bk[:, pr, x, :])
                ins.then_inc(S.sem("b_m"), 1)

            def b_nat(l, g, t):
                w = wid(t)
                pe.wait_ge(S.sem("b_masked"), S.count("b_masked"))
                pe.wait_ge(S.sem("corrected_s"), S.count("corrected_s"))
                pe.wait_ge(S.sem("b_snew"), S.count("b_snew"))
                pe.wait_ge(S.sem("b_bonus_done"), S.count("b_bonus_done"))
                for pr in range(2):
                    ins = tr(M[1][0:w, 128 * pr:128 * pr + 128], FM[:, 8 + 2 * g + pr, tok(t)])
                ins.then_inc(S.sem("b_vt"), 1)

            def b_s0(l, g, pr):
                pe.wait_ge(S.sem("rw_state_loaded"), S.count("rw_state_loaded"))
                pe.wait_ge(S.sem("tri_up"), S.count("tri_up"))
                pe.wait_ge(S.sem("start_reduced"), S.count("start_reduced", S.at - 1))
                for s in range(NSEQ):
                    ins = tr(M[s // 4][:, (s % 4) * 128:(s % 4) * 128 + 128], BSB[:, pr, s, :])
                ins.then_inc(S.sem("b_s_t"), 1)
                pe.wait_ge(S.sem("b_s_ts"), S.count("b_s_ts"))
                for c in range(2):
                    ins = mm(M[2 + c][0:64, :], BAR[:, 64 * pr:64 * pr + 64], BX[:, 0, 4 * c:4 * c + 4, :], start=True, stop=True)
                ins.then_inc(S.sem("start_read"), 1)

            def b_w(l, g, t):
                w = wid(t)
                pe.wait_ge(S.sem("b_vs"), S.count("b_vs"))
                pe.wait_ge(S.sem("tri_up"), S.count("tri_up"))
                pe.wait_ge(S.sem("start_reduced"), S.count("start_reduced"))
                for hd in range(4):
                    pr, hh = hd // 2, hd % 2
                    if t == 1 and hh == 0:
                        mm(M[0][:, 128 * pr:128 * pr + 128], vx(BAR, 2, w)[:, pr, 0, :], BST[:, pr, :], start=True, stop=False,
                           skip_group_check=True)
                    ins = mm(M[0][0:w, 64 * hd:64 * hd + 64], vx(BKK, 4, w, w)[:, hd, 0, :],
                             BVN[0:w, pr, 64 * hh:64 * hh + 64], start=t != 1, stop=True, skip_group_check=True)
                ins.then_inc(S.sem("b_wp"), 1)

            def b_u(l, g, t):
                w = wid(t)
                pe.wait_ge(S.sem("b_ws"), S.count("b_ws"))
                for hd in range(4):
                    pr, hh = hd // 2, hd % 2
                    ins = mm(M[1][0:w, 64 * hd:64 * hd + 64], TT[0:w, hd, 0:w], BW[0:w, pr, 64 * hh:64 * hh + 64],
                             start=True, stop=True)
                ins.then_inc(S.sem("corrected"), 1)

            def b_y(l, g, t):
                w = wid(t)
                pe.wait_ge(S.sem("corrected_s"), S.count("corrected_s"))
                for hd in range(4):
                    pr, hh = hd // 2, hd % 2
                    cols = slice(64 * hh, 64 * hh + 64)
                    out = M[2][0:w, 64 * hd:64 * hd + 64]
                    if t == 1 and hh == 0:
                        mm(M[2][:, 128 * pr:128 * pr + 128], vx(BAR, 2, w)[:, pr, 1, :], BST[:, pr, :], start=True, stop=False,
                           skip_group_check=True)
                    mm(out, BRB[0:w, hd, 0:w], BU[0:w, pr, cols], start=t != 1, stop=False, skip_group_check=True)
                    ins = mm(out, vx(BKK, 4, w, w)[:, hd, 1, :], BVN[0:w, pr, cols], start=False, stop=True,
                             skip_group_check=True)
                if t < 2:
                    for pr in range(2):
                        mm(M[3][:, 128 * pr:128 * pr + 128], BN[0:w, pr, 0, :], BU[0:w, pr, :], start=True, stop=False)
                        ins = mm(M[3][:, 128 * pr:128 * pr + 128], BN[0:w, pr, 1, :], BVN[0:w, pr, :], start=False, stop=True)
                ins.then_inc(S.sem("b_y"), 1)

            def b_fin(l, g):
                pe.wait_ge(S.sem("b_state"), S.count("b_state"))
                pe.wait_ge(S.sem("b_done"), S.count("b_done"))
                for pr in range(2):
                    ins = tr(M[4][:, 128 * pr:128 * pr + 128], BST[:, pr, :])
                ins.then_inc(S.sem("b_fin_t"), 1)

            def b_norm3(l, g, t):
                w = wid(t)
                pe.wait_ge(S.sem("b_nats"), S.count("b_nats"))
                pe.wait_ge(S.sem("b_snew"), S.count("b_snew"))
                pe.wait_ge(S.sem("out_normed"), S.count("out_normed"))
                for pr in range(2):
                    ins = tr(M[4][:, w * pr:w * pr + w], BY[0:w, pr, :], w)
                ins.then_inc(S.sem("out_t"), 1)

            def b_sout(l, g, pr):
                pe.wait_ge(S.sem("b_bex"), S.count("b_bex"))
                pe.wait_ge(S.sem("b_ys"), S.count("b_ys"))
                for c in range(2):
                    for src, x in ((BU, 0), (BVN, 1)):
                        mm(M[c], src[0:32, pr, :], BX[0:32, x, 4 * c:4 * c + 4, :], start=x == 0, stop=x == 1)
                ins = tr(M[2][0:8, 0:128], BM[:, 2 * g + pr, 4:12])
                ins.then_inc(S.sem("b_ds"), 1)
                pe.wait_ge(S.sem("b_pcx"), S.count("b_pcx"))
                pe.wait_ge(S.sem("b_fin_s"), S.count("b_fin_s"))
                for c in range(2):
                    ins = mm(M[3 + c], C("ones", 8), BX[0:8, 1, 4 * c:4 * c + 4, :], start=True, stop=True)
                ins.then_inc(S.sem("b_pcb"), 1)

            def c_rms(l, i):
                pe.wait_ge(S.sem("squares"), S.count("squares"))
                pe.wait_ge(S.sem("b_snew"), S.count("b_snew"))
                ones4(CSQ, C("ones_head"), "square_sums")

            def c_rope(l, i):
                pe.wait_ge(S.sem("inv_roots"), S.count("inv_roots"))
                pe.wait_ge(S.sem("c_n"), S.count("c_n"))
                for h in range(4):
                    ins = mm(M[h][:, 0:NTOK], C("swap"), QC[:, 4 * i + h, :], start=True, stop=True)
                ins.then_inc(S.sem("c_sw"), 1)

            def c_nat(l, i):
                pe.wait_ge(S.sem("c_rope"), S.count("c_rope"))
                if i == 0:
                    for b in range(3):
                        pe.wait_ge(S.sem(f"bank{b}_read"), S.count(f"bank{b}_read"))
                else:
                    pe.wait_ge(S.sem("c_ns"), S.count("c_ns", S.at - 1))
                for t in range(3):
                    w = wid(t)
                    for m in range(4):
                        ins = tr(M[t][0:w, 128 * m:128 * m + 128], QC[:, 4 + 4 * i + m, tok(t)])
                ins.then_inc(S.sem("c_nt"), 1)

            def c_score(l, t, g):
                if t == 0 and g == 0:
                    pe.wait_ge(S.sem("c_ns"), S.count("c_ns"))
                    pe.wait_ge(S.sem("c_sdone"), S.count("c_sdone"))
                pe.wait_ge(S.sem("c_max"), S.count("c_max", S.at - 1))
                for hd in range(4):
                    pair, r = 2 * g + hd // 2, slice(64 * (hd % 2), 64 * (hd % 2) + 64)
                    n = 128 * (t + 1)
                    out = M[hd % 2][:, n * (hd // 2):n * (hd // 2) + n]
                    ins = mm(out, QC[r, pair, tok(t)], QC[r, 4 + pair, 0:n], start=True, stop=True)
                ins.then_inc(S.sem("c_s"), 1)

            def c_prob(l, t, g):
                pe.wait_ge(S.sem("c_e"), S.count("c_e"))
                pe.wait_ge(S.sem("c_done"), S.count("c_done"))
                for st in range(t + 1):
                    for hd in range(4):
                        ins = tr(M[2 + st][:, 128 * hd:128 * hd + 128], CP[:, hd, 128 * st:128 * st + 128])
                ins.then_inc(S.sem("c_pt"), 1)

            def c_pv(l, t, g):
                pe.wait_ge(S.sem("c_pts"), S.count("c_pts"))
                pe.wait_ge(S.sem("c_os"), S.count("c_os", S.at - 1))
                for hd in range(4):
                    for st in range(t + 1):
                        ins = mm(M[4][:, 64 * hd:64 * hd + 64], CPT[:, st, hd, :], CVN[:, st, 64 * (4 * g + hd):64 * (4 * g + hd) + 64],
                                 start=st == 0, stop=st == t)
                ins.then_inc(S.sem("c_o"), 1)

            def c_out(l, t):
                pe.wait_ge(S.sem("c_os"), S.count("c_os"))
                for m in range(4):
                    ins = tr(M[2][:, 128 * m:128 * m + 128], CON[:, 128 * m:128 * m + 128])
                ins.then_inc(S.sem("c_ot"), 1)

            def c_past(l, g, j):
                s = 4 * g + j
                pe.wait_ge(S.sem(f"past_k{s % 2}_loaded"), S.count(f"past_k{s % 2}_loaded"))
                pe.wait_ge(S.sem("past_k_ts"), S.count("past_k_ts", S.at - 1))
                pe.wait_ge(S.sem("c_ns"), S.count("c_ns"))
                pe.wait_ge(S.sem("c_qx"), S.count("c_qx"))
                pe.wait_ge(S.sem("c_done"), S.count("c_done"))
                pe.wait_ge(S.sem("c_sdone"), S.count("c_sdone", S.at - 1))
                pe.wait_ge(S.sem("c_max"), S.count("c_max", S.at - 1))
                for pg in range(2):
                    for pr in range(4):
                        ins = tr(M[pg][:, 128 * pr:128 * pr + 128], CKR[:, s % 2, pg, 128 * pr:128 * pr + 128])
                ins.then_inc(S.sem("past_k_t"), 1)
                pe.wait_ge(S.sem("past_k_ts"), S.count("past_k_ts"))
                rows = slice(32 * j, 32 * j + 32)
                for pr in range(4):
                    mm(M[2 + g][rows, 0:256], CQX[:, pr, s, :], CKT[:, s % 2, pr, :], start=pr == 0, stop=pr == 3,
                       skip_group_check=True)
                for pr in range(4):
                    ins = mm(M[2 + g][rows, 256:288], CQX[:, pr, s, :], QC[:, 4 + pr, SEQ:NTOK], start=pr == 0, stop=pr == 3,
                             skip_group_check=True)
                ins.then_inc(S.sem("c_ssc"), 1)

            def c_sprob(l, g):
                pe.wait_ge(S.sem("c_sp"), S.count("c_sp"))
                for st in range(3):
                    n = 128 if st < 2 else 32
                    ins = tr(M[4][0:n, 128 * st:128 * st + 128], CPS[:, 128 * st:128 * st + n])
                ins.then_inc(S.sem("c_spt"), 1)

            def c_spv(l, g):
                pe.wait_ge(S.sem("c_spts"), S.count("c_spts"))
                pe.wait_ge(S.sem(f"past_v{g}_loaded"), S.count(f"past_v{g}_loaded"))
                for j in range(4):
                    for pr in range(4):
                        out = M[0][:, (4 * j + pr) * 8:(4 * j + pr) * 8 + 8]
                        cols = slice(32 * j + 8 * pr, 32 * j + 8 * pr + 8)
                        for pg in range(2):
                            mm(out, CVR[:, j, pg, 128 * pr:128 * pr + 128], CPTS[:, pg, cols], start=pg == 0, stop=False)
                        ins = mm(out, CVN[0:32, 2, 128 * pr:128 * pr + 128], CPTS[0:32, 2, cols], start=False, stop=True)
                ins.then_inc(S.sem("c_so"), 1)

            def finish(l, t):
                w = wid(t)
                pe.wait_ge(S.sem("x_next"), S.count("x_next"))
                if t == 2:
                    pe.wait_ge(S.sem("y_rows"), S.count("y_rows", S.at - 2))
                for k in range(8):
                    ins = tr(M[2 * (t % 2) + k // 4][0:w, (k % 4) * 128:(k % 4) * 128 + 128], X(l)[:, k, tok(t)])
                ins.then_inc(S.sem("y_t"), 1)

            do = dict(x_in=x_in, params=params, norm=norm, p_a=p_h, p_f=p_h, p_c=p_h, p_g=p_h, p_z=p_h, p_ba=p_ba,
                      p_up=p_up, p_y=p_y, p_pg=p_pg, p_ple=p_ple, a_hist=a_hist, a_convout=a_convout, a_l2=a_l2,
                      a_rows=a_rows, a_scale=a_scale, a_pairs=a_pairs, tri=tri, lev=lev, a_s0=a_s0, a_w=a_w, a_u=a_u,
                      a_o=a_o, a_norm3=a_norm3, a_sout=a_sout, b_hist=b_hist, b_shiftout=b_shiftout, b_lora=b_lora,
                      b_kk=b_kk, b_bonus=b_bonus, b_pairs=b_pairs, b_nat=b_nat, b_s0=b_s0, b_w=b_w, b_u=b_u, b_y=b_y,
                      b_fin=b_fin, b_norm3=b_norm3, b_sout=b_sout, c_rms=c_rms, c_rope=c_rope, c_nat=c_nat, c_score=c_score,
                      c_prob=c_prob, c_pv=c_pv, c_out=c_out, c_past=c_past, c_sprob=c_sprob, c_spv=c_spv, finish=finish)
            for i, st in enumerate(order):
                S.at = i
                if st[0] in do:
                    do[st[0]](*st[1:])

        @block.scalar
        def _(act):
            own = [0]

            def link(ins):
                own[0] += 1
                ins.then_inc(S.sem("act_link"), 1)
                act.wait_ge(S.sem("act_link"), own[0])

            fn = act.activation

            def params(l):
                act.wait_ge(S.sem("heads_loaded"), S.count("heads_loaded"))
                fn(HP[:, 2:3], HP[:, 1:2], ACT.Exp).then_inc(S.sem("decay_rate"), 1)
                act.wait_ge(S.sem("decay_rate"), S.count("decay_rate"))

            def norm(l):
                act.wait_ge(S.sem("x_t" if l == 0 else "x_next"), S.count("x_t" if l == 0 else "x_next"))
                if l:
                    for b in range(3):
                        act.wait_ge(S.sem(f"bank{b}_read"), S.count(f"bank{b}_read", S.at - 1))
                act.wait_ge(S.sem("param_done"), S.count("param_done"))
                fn(H(l)[:, :, :], X(l)[:, :, :], ACT.Square).then_inc(S.sem("squares"), 1)
                act.wait_ge(S.sem("squares"), S.count("squares"))
                act.wait_ge(S.sem("square_sums"), S.count("square_sums"))
                link(fn(TMP[:, 0, :], M[0][:, 0:NTOK], ACT.Ln, bias=C("c_eps"), scale=1.0 / D_MODEL))
                fn(TMP[:, 1, :], TMP[:, 0, :], ACT.Exp, scale=-0.5).then_inc(S.sem("inv_roots"), 1)
                act.wait_ge(S.sem("inv_roots"), S.count("inv_roots"))

            def p_a(l, m):
                act.wait_ge(S.sem("projected"), S.count("projected"))
                act.wait_ge(S.sem("c_ns"), S.count("c_ns", S.at - 1))
                fn(U[:, m, CONV_W - 1:UW], bank()[:, 0:SEQ], ACT.Copy)
                fn(Us[:, m, :, CONV_W - 1:], seqs(bank()[:, SEQ:NTOK]), ACT.Copy).then_inc(S.sem(freed()), 1)
                act.wait_ge(S.sem(freed()), S.count(freed()))

            def p_f(l, m):
                act.wait_ge(S.sem("projected"), S.count("projected"))
                fn(F[:, m, 1:FW], bank()[:, 0:SEQ], ACT.Copy)
                fn(Fs[:, m, :, 1:], seqs(bank()[:, SEQ:NTOK]), ACT.Copy).then_inc(S.sem(freed()), 1)
                act.wait_ge(S.sem(freed()), S.count(freed()))

            def p_c(l, m):
                act.wait_ge(S.sem("projected"), S.count("projected"))
                act.wait_ge(S.sem("a_conv_p"), S.count("a_conv_p"))
                act.wait_ge(S.sem("a_conv_s"), S.count("a_conv_s"))
                fn(QC[:, m, :], bank()[:, 0:NTOK], ACT.Copy).then_inc(S.sem(freed()), 1)
                act.wait_ge(S.sem(freed()), S.count(freed()))

            def p_z(l, n, m):
                act.wait_ge(S.sem("projected"), S.count("projected"))
                if before("p_z", 2) is not None:
                    act.wait_ge(S.sem(freed(before("p_z", 2))), S.count(freed(before("p_z", 2)), before("p_z", 2)))
                if l and n == 0:
                    for b in range(3):
                        act.wait_ge(S.sem(f"bank{b}_read"), S.count(f"bank{b}_read", before("p_ple")))
                fn(TH[:, m % 2, :], bank()[:, 0:NTOK], ACT.Tanh, scale=0.5).then_inc(S.sem("z_tanh"), 1)
                act.wait_ge(S.sem("z_tanh"), S.count("z_tanh"))

            def p_g(l, m):
                act.wait_ge(S.sem("projected"), S.count("projected"))
                act.wait_ge(S.sem("b_mixed"), S.count("b_mixed"))
                act.wait_ge(S.sem("b_mixed_s"), S.count("b_mixed_s"))
                act.wait_ge(S.sem("tails"), S.count("tails"))
                if m >= NF:
                    act.wait_ge(S.sem("b_done"), S.count("b_done"))
                    act.wait_ge(S.sem("b_snew"), S.count("b_snew"))
                    act.wait_ge(S.sem("states_stored"), S.count("states_stored"))
                if m >= NF + 8:
                    act.wait_ge(S.sem("c_rope"), S.count("c_rope"))
                fn(gate(m), bank()[:, 0:NTOK], ACT.Tanh, scale=0.5, bias=Phalf("b_gate", m)).then_inc(S.sem(freed()), 1)
                act.wait_ge(S.sem(freed()), S.count(freed()))

            def p_pg(l, m):
                act.wait_ge(S.sem("projected"), S.count("projected"))
                if m >= 2:
                    act.wait_ge(S.sem(freed(before("p_ple", 2))), S.count(freed(before("p_ple", 2)), before("p_ple", 2)))
                else:
                    for b in range(3):
                        act.wait_ge(S.sem(f"bank{b}_read"), S.count(f"bank{b}_read", before("p_z")))
                fn(TH[:, m % 2, :], bank()[:, 0:NTOK], ACT.Tanh, scale=0.5, bias=Phalf("b_pg", m)).then_inc(S.sem(freed()), 1)
                act.wait_ge(S.sem(freed()), S.count(freed()))

            def p_ba(l):
                act.wait_ge(S.sem("projected"), S.count("projected"))
                if l:
                    act.wait_ge(S.sem("x_next"), S.count("x_next", S.at - 1))
                fn(ATM[0:4, 0, :], bank()[0:4, 0:NTOK], ACT.Tanh, scale=0.5)
                fn(ATM[0:4, 1, :], M[4][0:4, 0:NTOK], ACT.Identity, bias=HP[:, 0:1]).then_inc(S.sem(freed()), 1)
                act.wait_ge(S.sem(freed()), S.count(freed()))

            def a_convout(l):
                act.wait_ge(S.sem("tails_t"), S.count("tails_t"))
                act.wait_ge(S.sem("tail_rows_stored"), S.count("tail_rows_stored", S.at - 1))
                fn(ROWS[0:27, 0:QKV_A], PS[0:27, 4:7, :].rearrange("p b n -> p (b n)"), ACT.Copy).then_inc(S.sem("tail_rows"), 1)
                act.wait_ge(S.sem("tail_rows"), S.count("tail_rows"))

            def a_silu(l, c):
                act.wait_ge(S.sem("a_conv_p"), S.count("a_conv_p"))
                act.wait_ge(S.sem("a_conv_s"), S.count("a_conv_s"))
                act.wait_ge(S.sem("a_silu"), S.count("a_silu", S.at - 1))
                fn(TMP[:, :, :], UC[:, 4 * c:4 * c + 4, :], ACT.Tanh, scale=0.5).then_inc(S.sem("a_tanh"), 1)
                act.wait_ge(S.sem("a_tanh"), S.count("a_tanh"))

            def inv_root(dst, src, mean, eps, scale_log=None, rows=128):
                link(fn(dst, src, ACT.Ln, bias=C(eps, rows), scale=mean))
                return fn(dst, dst, ACT.Exp, scale=-0.5, bias=C(scale_log or "c_0", rows))

            def a_l2(l, i):
                act.wait_ge(S.sem("a_silu"), S.count("a_silu"))
                act.wait_ge(S.sem("a_unit"), S.count("a_unit", S.at - 1))
                fn(TMP[:, :, :], UC[:, 4 * i:4 * i + 4, :], ACT.Square).then_inc(S.sem("squares"), 1)
                act.wait_ge(S.sem("squares"), S.count("squares"))
                act.wait_ge(S.sem("square_sums"), S.count("square_sums"))
                inv_root(TMP[:, :, :], PS[:, 3:7, 0:NTOK], 1.0, "c_4eps", None if i else "c_lndk").then_inc(S.sem("inv_roots"), 1)
                act.wait_ge(S.sem("inv_roots"), S.count("inv_roots"))

            def a_rows(l):
                act.wait_ge(S.sem("ba_neg"), S.count("ba_neg"))
                link(fn(ATM[0:4, 2, :], ATM[0:4, 2, :], ACT.Exp))
                fn(ATM[0:4, 2, :], ATM[0:4, 2, :], ACT.Ln, bias=C("c_1", 4)).then_inc(S.sem("ba_ln"), 1)
                act.wait_ge(S.sem("ba_ln"), S.count("ba_ln"))

            def a_scale(l, t):
                w = wid(t)
                act.wait_ge(S.sem("a_klast"), S.count("a_klast"))
                fn(AEG[:, :, 0:w], AGB[:, :, 0:w], ACT.Exp)
                fn(ADI[0:w, :, 0:w], ADI[0:w, :, 0:w], ACT.Exp)
                fn(AKD[:, :, 0:w], AKD[:, :, 0:w], ACT.Exp).then_inc(S.sem("a_exps"), 1)
                act.wait_ge(S.sem("a_exps"), S.count("a_exps"))

            def a_pairs(l, t):
                w = wid(t)
                act.wait_ge(S.sem("a_kk"), S.count("a_kk"))
                fn(AVN[0:w, :, :], v4(M[4], 128, w), ACT.Copy)
                fn(AKN[0:w, :, :], v4(M[0], 128, w), ACT.Copy).then_inc(S.sem("a_nat"), 1)
                act.wait_ge(S.sem("a_nat"), S.count("a_nat"))

            def tri(l, t):
                w = wid(t)
                act.wait_ge(S.sem("tri_tr"), S.count("tri_tr"))
                fn(TI[0:w, :, 0:w], v4(M[0], w, w), ACT.Copy).then_inc(S.sem("tri_i0"), 1)
                act.wait_ge(S.sem("tri_i0"), S.count("tri_i0"))

            def lev(l, t, k):
                w = wid(t)
                for i in range(2):
                    q = slice(2 * i, 2 * i + 2)
                    act.wait_ge(S.sem("tri_y"), S.count("tri_y") - 1 + i)
                    fn(Y[0:w, q, 0:w], v4(M[i], w, w)[:, q, :], ACT.Copy).then_inc(S.sem("tri_ys"), 1)
                act.wait_ge(S.sem("tri_ys"), S.count("tri_ys"))

            def a_u(l, t):
                w = wid(t)
                act.wait_ge(S.sem("corrected"), S.count("corrected"))
                fn(AU[0:w, :, :], v4(M[1], 128, w), ACT.Copy).then_inc(S.sem("corrected_s"), 1)
                act.wait_ge(S.sem("corrected_s"), S.count("corrected_s"))

            def a_norm1(l, t):
                w = wid(t)
                act.wait_ge(S.sem("a_os"), S.count("a_os"))
                act.wait_ge(S.sem("a_kk"), S.count("a_kk"))
                fn(AKB[0:w, :, :], AW[0:w, :, :], ACT.Square).then_inc(S.sem("out_squares"), 1)
                act.wait_ge(S.sem("out_squares"), S.count("out_squares"))

            def a_norm2(l, t):
                w = wid(t)
                act.wait_ge(S.sem("out_sums"), S.count("out_sums"))
                link(fn(ASM[0:w, 1, :], ASM[0:w, 0, :], ACT.Ln, bias=C("c_eps", w), scale=1.0 / 128))
                fn(ASM[0:w, 1, :], ASM[0:w, 1, :], ACT.Exp, scale=-0.5, bias=C("c_lnhalf", w)).then_inc(S.sem("out_roots"), 1)
                act.wait_ge(S.sem("out_roots"), S.count("out_roots"))

            def b_shiftout(l):
                act.wait_ge(S.sem("tails_t"), S.count("tails_t"))
                fn(ROWS[0:9, :], PS[0:9, 3:7, :].rearrange("p b n -> p (b n)")[:, 0:SHIFT_B], ACT.Copy).then_inc(S.sem("tail_rows"), 1)
                act.wait_ge(S.sem("tail_rows"), S.count("tail_rows"))

            def b_lora(l):
                act.wait_ge(S.sem("b_mixed"), S.count("b_mixed"))
                act.wait_ge(S.sem("b_mixed_s"), S.count("b_mixed_s"))
                fn(FM[0:64, NF - 1, :], FM[0:64, NF - 1, :], ACT.Tanh).then_inc(S.sem("b_lt"), 1)
                act.wait_ge(S.sem("b_lt"), S.count("b_lt"))
                for src, dst, par, name in (("b_wraw", LW, "w0_b", "b_wt"), ("b_araw", AA, "a0_b", "b_at")):
                    act.wait_ge(S.sem(src), S.count(src))
                    for h in range(4):
                        ins = fn(dst[:, h, :], M[h][:, 0:NTOK], ACT.Tanh, scale=0.5, bias=Phalf(par, h))
                    ins.then_inc(S.sem(name), 1)
                    act.wait_ge(S.sem(name), S.count(name))

            def b_kk(l):
                act.wait_ge(S.sem("b_kraw"), S.count("b_kraw"))
                fn(TMP[:, :, :], KK[:, :, :], ACT.Square).then_inc(S.sem("squares"), 1)
                act.wait_ge(S.sem("squares"), S.count("squares"))
                act.wait_ge(S.sem("square_sums"), S.count("square_sums"))
                inv_root(TMP[:, :, :], PS[:, 3:7, 0:NTOK], 1.0, "c_eps").then_inc(S.sem("inv_roots"), 1)
                act.wait_ge(S.sem("inv_roots"), S.count("inv_roots"))
                act.wait_ge(S.sem("b_prep"), S.count("b_prep"))
                fn(BM[:, :, :], BM[:, :, :], ACT.Exp).then_inc(S.sem("b_bm"), 1)
                act.wait_ge(S.sem("b_bm"), S.count("b_bm"))

            def b_scale(l, g, t):
                w = wid(t)
                act.wait_ge(S.sem("b_done"), S.count("b_done", S.at - 1))
                q = slice(2 * g, 2 * g + 2)
                fn(BE[:, 0, :, 0:w], LC[:, q, tok(t)], ACT.Exp)
                fn(BE[:, 1, :, 0:w], LC[:, q, tok(t)], ACT.Exp, scale=-1.0)
                fn(BE[:, 2, :, 0:w], LW[:, q, tok(t)], ACT.Exp).then_inc(S.sem("b_exps"), 1)
                act.wait_ge(S.sem("b_exps"), S.count("b_exps"))

            def b_pairs(l, g, t):
                w = wid(t)
                act.wait_ge(S.sem("b_m"), S.count("b_m"))
                fn(BN[0:w, :, :, :].rearrange("p a b c -> p (a b c)"), M[4][0:w, :], ACT.Copy).then_inc(S.sem("b_nats"), 1)
                act.wait_ge(S.sem("b_nats"), S.count("b_nats"))

            def b_nat(l, g, t):
                w = wid(t)
                act.wait_ge(S.sem("b_vt"), S.count("b_vt"))
                fn(BVN[0:w, :, :].rearrange("p a b -> p (a b)"), M[1][0:w, 0:256], ACT.Copy).then_inc(S.sem("b_vs"), 1)
                act.wait_ge(S.sem("b_vs"), S.count("b_vs"))

            def b_s0(l, g, pr):
                act.wait_ge(S.sem("b_s_t"), S.count("b_s_t"))
                fn(BX[:, 0, :, :], PS[:, 3:5, :].rearrange("p b (s n) -> p (b s) n", n=128), ACT.Copy).then_inc(S.sem("b_s_ts"), 1)
                act.wait_ge(S.sem("b_s_ts"), S.count("b_s_ts"))

            def b_u(l, g, t):
                w = wid(t)
                act.wait_ge(S.sem("corrected"), S.count("corrected"))
                fn(BU[0:w, :, :].rearrange("p a b -> p (a b)"), M[1][0:w, 0:256], ACT.Copy).then_inc(S.sem("corrected_s"), 1)
                act.wait_ge(S.sem("corrected_s"), S.count("corrected_s"))

            def b_fin(l, g):
                act.wait_ge(S.sem("b_fin_t"), S.count("b_fin_t"))
                act.wait_ge(S.sem("states_stored"), S.count("states_stored", S.at - 1))
                fn(BSO[:, :, :].rearrange("p a b -> p (a b)"), M[4][:, 0:256], ACT.Copy).then_inc(S.sem("b_fin_s"), 1)
                act.wait_ge(S.sem("b_fin_s"), S.count("b_fin_s"))

            def b_norm1(l, g, t):
                w = wid(t)
                act.wait_ge(S.sem("b_yc"), S.count("b_yc"))
                fn(BQ[0:w, :, :], BY[0:w, :, :], ACT.Square).then_inc(S.sem("out_squares"), 1)
                act.wait_ge(S.sem("out_squares"), S.count("out_squares"))

            def b_norm2(l, g, t):
                w = wid(t)
                act.wait_ge(S.sem("out_sums"), S.count("out_sums"))
                inv_root(BSM[0:w, 1, :], BSM[0:w, 1, :], 1.0 / 64, "c_gneps", rows=w).then_inc(S.sem("out_roots"), 1)
                act.wait_ge(S.sem("out_roots"), S.count("out_roots"))

            def c_rms(l, i):
                for b in range(3):
                    act.wait_ge(S.sem(f"bank{b}_read"), S.count(f"bank{b}_read"))
                act.wait_ge(S.sem("b_done"), S.count("b_done"))
                act.wait_ge(S.sem("b_snew"), S.count("b_snew"))
                act.wait_ge(S.sem("c_rope"), S.count("c_rope", S.at - 1))
                fn(CSQ[:, :, :], QC[:, 4 * i:4 * i + 4, :], ACT.Square).then_inc(S.sem("squares"), 1)
                act.wait_ge(S.sem("squares"), S.count("squares"))
                act.wait_ge(S.sem("square_sums"), S.count("square_sums"))
                inv_root(CSQ[:, :, :], PS[:, 3:7, 0:NTOK], 1.0 / 64, "c_eps").then_inc(S.sem("inv_roots"), 1)
                act.wait_ge(S.sem("inv_roots"), S.count("inv_roots"))

            def c_nat(l, i):
                act.wait_ge(S.sem("c_nt"), S.count("c_nt"))
                dst = (CKN, CVN)[i]
                for t in range(3):
                    ins = fn(dst[0:wid(t), t, :], M[t][0:wid(t), :], ACT.Copy)
                ins.then_inc(S.sem("c_ns"), 1)
                act.wait_ge(S.sem("c_ns"), S.count("c_ns"))

            def probs(dst, i, row):
                return fn(dst, dst, ACT.Exp, scale=0.125, bias=CMX[:, 0, i:i + 1], accum_out=CMX[:, 1, i:i + 1])

            def c_prob(l, t, g):
                act.wait_ge(S.sem("c_max"), S.count("c_max"))
                for hd in range(4):
                    ins = probs(CP[:, hd, 0:128 * (t + 1)], hd, 128)
                ins.then_inc(S.sem("c_e"), 1)
                act.wait_ge(S.sem("c_e"), S.count("c_e"))
                act.wait_ge(S.sem("c_pt"), S.count("c_pt"))
                for st in range(t + 1):
                    ins = fn(CPT[:, st, :, :].rearrange("p a b -> p (a b)"), M[2 + st], ACT.Copy)
                ins.then_inc(S.sem("c_pts"), 1)
                act.wait_ge(S.sem("c_pts"), S.count("c_pts"))

            def c_past(l, g, j):
                s = 4 * g + j
                act.wait_ge(S.sem("past_k_t"), S.count("past_k_t"))
                if before("c_past", 2) is not None:
                    act.wait_ge(S.sem("c_ssc"), S.count("c_ssc", before("c_past", 2)))
                for pg in range(2):
                    ins = fn(CKT[:, s % 2, :, 128 * pg:128 * pg + 128], v4(M[pg], 128), ACT.Copy)
                ins.then_inc(S.sem("past_k_ts"), 1)
                act.wait_ge(S.sem("past_k_ts"), S.count("past_k_ts"))

            def c_sprob(l, g):
                act.wait_ge(S.sem("c_max"), S.count("c_max"))
                probs(CPS, 0, 128).then_inc(S.sem("c_e"), 1)
                act.wait_ge(S.sem("c_e"), S.count("c_e"))
                act.wait_ge(S.sem("c_spt"), S.count("c_spt"))
                fn(CPTS[:, 0:2, :].rearrange("p a b -> p (a b)"), M[4][:, 0:256], ACT.Copy)
                fn(CPTS[0:32, 2, :], M[4][0:32, 256:384], ACT.Copy).then_inc(S.sem("c_spts"), 1)
                act.wait_ge(S.sem("c_spts"), S.count("c_spts"))

            do = dict(params=params, norm=norm, p_a=p_a, p_f=p_f, p_c=p_c, p_z=p_z, p_g=p_g, p_pg=p_pg, p_ba=p_ba,
                      a_convout=a_convout, a_silu=a_silu, a_l2=a_l2, a_rows=a_rows, a_scale=a_scale, a_pairs=a_pairs,
                      tri=tri, lev=lev, a_u=a_u, a_norm1=a_norm1, a_norm2=a_norm2, b_shiftout=b_shiftout, b_lora=b_lora, b_kk=b_kk,
                      b_scale=b_scale, b_pairs=b_pairs, b_nat=b_nat, b_s0=b_s0, b_u=b_u, b_fin=b_fin, b_norm1=b_norm1, b_norm2=b_norm2,
                      c_rms=c_rms, c_nat=c_nat, c_prob=c_prob, c_past=c_past, c_sprob=c_sprob)
            for i, st in enumerate(order):
                S.at = i
                if st[0] in do:
                    do[st[0]](*st[1:])

        @block.vector
        def _(dve):
            own = [0]

            def link(ins):
                own[0] += 1
                ins.then_inc(S.sem("dve_link"), 1)
                dve.wait_ge(S.sem("dve_link"), own[0])

            tt, ts, stt, cp = dve.tensor_tensor, dve.tensor_scalar, dve.scalar_tensor_tensor, dve.tensor_copy
            MUL, ADD, SUB = ALU.mult, ALU.add, ALU.subtract

            def x_in(l, t):
                dve.wait_ge(S.sem("x_tr"), S.count("x_tr"))
                for k in range(2):
                    ins = cp(XA[:, 4 * k:4 * k + 4, tok(t)], v4(M[2 * (t % 2) + k], wid(t)))
                ins.then_inc(S.sem("x_t"), 1)
                dve.wait_ge(S.sem("x_t"), S.count("x_t"))

            def params(l):
                dve.wait_ge(S.sem("param_t"), S.count("param_t"))
                dve.wait_ge(S.sem("decay_rate"), S.count("decay_rate"))
                if l:
                    for b in range(3):
                        dve.wait_ge(S.sem(f"bank{b}_read"), S.count(f"bank{b}_read", S.at - 1))
                cp(PT[:, :], M[0][:, 0:NPAR])
                cp(PLT[:, 0, :], M[1][:, 0:NTOK])
                link(cp(PLT[:, 1, :], M[2][:, 0:NTOK]))
                ts(HP[:, 3:4], HP[:, 2:3], -1.0, None, MUL)
                ts(PH[:, :], PT[:, :], 0.5, None, MUL).then_inc(S.sem("param_done"), 1)
                dve.wait_ge(S.sem("param_done"), S.count("param_done"))

            def norm(l):
                dve.wait_ge(S.sem("inv_roots"), S.count("inv_roots"))
                for k in range(8):
                    ins = stt(H(l)[:, k, :], X(l)[:, k, :], P("norm_g", k), TMP[:, 1, :], MUL, MUL)
                ins.then_inc(S.sem("h_ready"), 1)
                dve.wait_ge(S.sem("h_ready"), S.count("h_ready"))

            def p_z(l, n, m):
                dve.wait_ge(S.sem("z_tanh"), S.count("z_tanh"))
                stt(Z[:, n, m, :], TH[:, m % 2, :], 1.0, bank()[:, 0:NTOK], ADD, MUL).then_inc(S.sem(freed()), 1)
                dve.wait_ge(S.sem(freed()), S.count(freed()))

            def p_up(l, n, m):
                dve.wait_ge(S.sem("projected"), S.count("projected"))
                for b in range(3):
                    dve.wait_ge(S.sem(f"bank{b}_read"), S.count(f"bank{b}_read", before("p_g")))
                dve.wait_ge(S.sem("kv_stored"), S.count("kv_stored"))
                if n == 0:
                    stt(MG[:, m, :], gate(m), 1.0, bank()[:, 0:NTOK], ADD, MUL).then_inc(S.sem(freed()), 1)
                    dve.wait_ge(S.sem(freed()), S.count(freed()))
                    return
                stt(TMP[:, 0, :], gate(8 * n + m), 1.0, bank()[:, 0:NTOK], ADD, MUL).then_inc(S.sem(freed()), 1)
                dve.wait_ge(S.sem(freed()), S.count(freed()))
                tt(MG[:, m, :], MG[:, m, :], TMP[:, 0, :], ADD).then_inc(S.sem("merged"), 1)
                dve.wait_ge(S.sem("merged"), S.count("merged"))

            def p_y(l, m):
                dve.wait_ge(S.sem("projected"), S.count("projected"))
                stt(X(l)[:, m, :], bank()[:, 0:NTOK], 0.5, X(l)[:, m, :], MUL, ADD).then_inc(S.sem(freed()), 1)
                dve.wait_ge(S.sem(freed()), S.count(freed()))

            def p_ple(l, m):
                dve.wait_ge(S.sem("projected"), S.count("projected"))
                for b in range(3):
                    dve.wait_ge(S.sem(f"bank{b}_read"), S.count(f"bank{b}_read", S.at - 1))
                stt(TMP[:, m % 2, :], TH[:, m % 2, :], 1.0, bank()[:, 0:NTOK], ADD, MUL).then_inc(S.sem(freed()), 1)
                dve.wait_ge(S.sem(freed()), S.count(freed()))
                stt(H(l)[:, m, :], TMP[:, m % 2, :], 0.5, X(l)[:, m, :], MUL, ADD).then_inc(S.sem("x_next"), 1)
                dve.wait_ge(S.sem("x_next"), S.count("x_next"))

            def a_hist(l):
                dve.wait_ge(S.sem("hist_t"), S.count("hist_t"))
                if l:
                    for b in range(3):
                        dve.wait_ge(S.sem(f"bank{b}_read"), S.count(f"bank{b}_read", S.at - 1))
                dve.memset(U[:, :, 0:CONV_W - 1], 0.0)
                cp(Us[:, :, :, 0:CONV_W - 1], M[0][:, 0:24 * NA].rearrange("p (m s c) -> p m s c", m=NA, s=NSEQ)).then_inc(S.sem("hist_in"), 1)
                dve.wait_ge(S.sem("hist_in"), S.count("hist_in"))

            def tails(width, prompt, sampled, n):
                v = CT[:, 0:n * width].rearrange("p (m c) -> p m c", c=width)
                for b in range(3):
                    dve.wait_ge(S.sem(f"bank{b}_read"), S.count(f"bank{b}_read"))
                k = width - prompt.shape[2]
                cp(v[:, :, 0:width - k], prompt)
                return cp(v[:, :, width - k:].rearrange("p m (s c) -> p m s c", s=NSEQ), sampled)

            def a_convout(l):
                dve.wait_ge(S.sem("hist_in"), S.count("hist_in"))
                dve.wait_ge(S.sem("tails_t"), S.count("tails_t", S.at - 1))
                tails(27, U[:, :, UW - 3:UW], Us[:, :, :, US - 3:], NA).then_inc(S.sem("tails"), 1)
                dve.wait_ge(S.sem("tails"), S.count("tails"))

            def conv_w(j, m):
                c = NP1 + NA * j + m
                return PT[:, c:c + 1]

            def a_conv(l):
                for b in range(3):
                    dve.wait_ge(S.sem(f"bank{b}_read"), S.count(f"bank{b}_read"))
                dve.wait_ge(S.sem("tails_t"), S.count("tails_t"))
                for j in range(CONV_W):
                    for m in range(NA):
                        if j == 0:
                            ins = ts(UC[:, m, 0:SEQ], U[:, m, 0:SEQ], conv_w(0, m), None, MUL)
                        else:
                            ins = stt(UC[:, m, 0:SEQ], U[:, m, j:j + SEQ], conv_w(j, m), UC[:, m, 0:SEQ], MUL, ADD)
                    if j < CONV_W - 1:
                        link(ins)
                ins.then_inc(S.sem("a_conv_p"), 1)
                dve.wait_ge(S.sem("a_conv_p"), S.count("a_conv_p"))

            def a_silu(l, c):
                dve.wait_ge(S.sem("a_tanh"), S.count("a_tanh"))
                stt(UC[:, 4 * c:4 * c + 4, :], TMP[:, :, :], 1.0, UC[:, 4 * c:4 * c + 4, :], ADD, MUL).then_inc(S.sem("a_silu"), 1)
                dve.wait_ge(S.sem("a_silu"), S.count("a_silu"))

            def a_l2(l, i):
                dve.wait_ge(S.sem("inv_roots"), S.count("inv_roots"))
                tt(UC[:, 4 * i:4 * i + 4, :], UC[:, 4 * i:4 * i + 4, :], TMP[:, :, :], MUL).then_inc(S.sem("a_unit"), 1)
                dve.wait_ge(S.sem("a_unit"), S.count("a_unit"))

            def a_rows(l):
                for b in range(3):
                    dve.wait_ge(S.sem(f"bank{b}_read"), S.count(f"bank{b}_read"))
                ts(ABG[0:4, 0, :], ATM[0:4, 0, :], 0.5, 0.5, MUL, ADD)
                link(ts(ATM[0:4, 2, :], ATM[0:4, 1, :], -1.0, None, MUL))
                tt(ATM[0:4, 2, :], ATM[0:4, 1, :], ATM[0:4, 2, :], ALU.min).then_inc(S.sem("ba_neg"), 1)
                dve.wait_ge(S.sem("ba_neg"), S.count("ba_neg"))
                dve.wait_ge(S.sem("ba_ln"), S.count("ba_ln"))
                link(stt(ATM[0:4, 1, :], ATM[0:4, 1, :], 0.0, ATM[0:4, 2, :], ALU.max, ADD))
                link(ts(ATM[0:4, 1, :], ATM[0:4, 1, :], HP[:, 3:4], None, MUL))
                dve.tensor_tensor_scan(ABG[0:4, 1, :], C("keep", 4), ATM[0:4, 1, :], 0.0, MUL, ADD).then_inc(S.sem("a_g"), 1)
                dve.wait_ge(S.sem("a_g"), S.count("a_g"))
                dve.wait_ge(S.sem("a_gcol_t"), S.count("a_gcol_t"))
                for t in range(3):
                    ins = cp(AGC[0:wid(t), t, :], M[4][0:wid(t), 4 * t:4 * t + 4])
                link(ins)

            def a_scale(l, t):
                w = wid(t)
                dve.wait_ge(S.sem("a_gb"), S.count("a_gb"))
                link(cp(AGB[:, :, 0:w], v4(M[0], w)))
                link(tt(ADI[0:w, :, 0:w], AGB[0:w, :, 0:w], bc(AGC[0:w, t, :], 2, [w, 4, w]), SUB))
                ts(ADI[0:w, :, 0:w], ADI[0:w, :, 0:w], 0.0, None, ALU.min)
                if t < 2:
                    last = AGB[:, :, w - 1:w].to_broadcast([128, 4, w])
                    ins = tt(AKD[:, :, 0:w], last, AGB[:, :, 0:w], SUB)
                else:
                    for h in range(4):
                        last = seqs(AGB[:, h, 0:w])[:, :, LS - 1:LS].to_broadcast([128, NSEQ, LS])
                        ins = tt(seqs(AKD[:, h, 0:w]), last, seqs(AGB[:, h, 0:w]), SUB)
                ins.then_inc(S.sem("a_klast"), 1)
                dve.wait_ge(S.sem("a_klast"), S.count("a_klast"))
                tt(AKB[:, :, 0:w], UC[:, 4:8, tok(t)], v4(M[1], w), MUL)
                link(stt(AVB[:, :, 0:w], UC[:, 8:12, tok(t)], 0.5, v4(M[1], w), MUL, MUL))
                dve.wait_ge(S.sem("a_exps"), S.count("a_exps"))
                kq = vx(AKQ, 4, w)
                tt(kq[:, :, 0, :], AKB[:, :, 0:w], AEG[:, :, 0:w], MUL)
                tt(kq[:, :, 1, :], UC[:, 0:4, tok(t)], AEG[:, :, 0:w], MUL)
                tt(AKD[:, :, 0:w], UC[:, 4:8, tok(t)], AKD[:, :, 0:w], MUL)
                m = C("strict_incl")[:, 128:256] if t < 2 else C("strict_incl_s", 32)[:, 32:64]
                tt(ADI[0:w, :, 0:w], ADI[0:w, :, 0:w], bc(m, 1, [w, 4, w]), MUL).then_inc(S.sem("a_scaled"), 1)
                dve.wait_ge(S.sem("a_scaled"), S.count("a_scaled"))

            def a_pairs(l, t):
                w = wid(t)
                dve.wait_ge(S.sem("a_kk"), S.count("a_kk"))
                tt(LT[0:w, :, 0:w], v4(M[2], w, w), ADI[0:w, :, 0:w], MUL)
                tt(AQK[0:w, :, 0:w], v4(M[3], w, w), ADI[0:w, :, 0:w], MUL).then_inc(S.sem("a_lt"), 1)
                dve.wait_ge(S.sem("a_lt"), S.count("a_lt"))

            def tri(l, t):
                w = wid(t)
                link(tt(LM[0:w, :, 0:w], LT[0:w, :, 0:w], bc(C("level0", w)[:, 0:w], 1, [w, 4, w]), MUL))
                tt(TT[0:w, :, 0:w], bc(ident[0:w, 0:w], 1, [w, 4, w]), LM[0:w, :, 0:w], SUB).then_inc(S.sem("tri_t0"), 1)
                dve.wait_ge(S.sem("tri_t0"), S.count("tri_t0"))

            def lev(l, t, k):
                w = wid(t)
                if k < last_level(t):
                    dve.wait_ge(S.sem("tri_z"), S.count("tri_z"))
                    tt(TI[0:w, :, 0:w], TI[0:w, :, 0:w], v4(M[2], w, w), SUB).then_inc(S.sem("tri_iup"), 1)
                dve.wait_ge(S.sem("tri_zt"), S.count("tri_zt"))
                tt(TT[0:w, :, 0:w], TT[0:w, :, 0:w], v4(M[3], w, w), SUB).then_inc(S.sem("tri_up"), 1)
                dve.wait_ge(S.sem("tri_up"), S.count("tri_up"))

            def own_seq(rows):
                return C("own_seq", rows).unsqueeze(2).to_broadcast([rows, NSEQ, 128])

            def both(b):
                return PS[:, 3 + b:5 + b, :].rearrange("p b (s n) -> p (b s) n", n=128)

            def a_s0(l, h):
                dve.wait_ge(S.sem("start_read"), S.count("start_read"))
                link(tt(AEX[0:64], both(2 * (h % 2))[0:64], own_seq(64), MUL))
                dve.tensor_reduce(AR[0:64, h, :], AEX[0:64].rearrange("p s v -> p v s"), AXX, ADD).then_inc(S.sem("start_reduced"), 1)
                dve.wait_ge(S.sem("start_reduced"), S.count("start_reduced"))

            def a_w(l, t):
                if t == 1:
                    dve.wait_ge(S.sem("a_ks"), S.count("a_ks"))
                    tt(AW[:, :, :], AVN[:, :, :], v4(M[0], 128), SUB).then_inc(S.sem("a_w"), 1)
                    dve.wait_ge(S.sem("a_w"), S.count("a_w"))
                if t == 2:
                    dve.wait_ge(S.sem("a_nat"), S.count("a_nat"))
                    tt(AW[0:32, :, :], AVN[0:32, :, :], AR[0:32, :, :], SUB).then_inc(S.sem("a_w"), 1)
                    dve.wait_ge(S.sem("a_w"), S.count("a_w"))

            def a_o(l, t):
                w = wid(t)
                dve.wait_ge(S.sem("a_o"), S.count("a_o"))
                if t == 2:
                    tt(AW[0:32, :, :], v4(M[2], 128, 32), AR[32:64, :, :], ADD).then_inc(S.sem("a_os"), 1)
                    dve.wait_ge(S.sem("a_os"), S.count("a_os"))
                    return
                cp(AW[:, :, :], v4(M[2], 128)).then_inc(S.sem("a_os"), 1)
                dve.wait_ge(S.sem("a_os"), S.count("a_os"))
                if t == 0:
                    cp(AST[:, :, :], v4(M[3], 128)).then_inc(S.sem("a_state"), 1)
                    dve.wait_ge(S.sem("a_state"), S.count("a_state"))
                else:
                    for h in range(4):
                        ins = stt(AST[:, h, :], AST[:, h, :], AEG[:, h, w - 1:w], v4(M[3], 128)[:, h, :], MUL, ADD)
                    ins.then_inc(S.sem("a_state"), 1)
                    dve.wait_ge(S.sem("a_state"), S.count("a_state"))

            def a_norm2(l, t):
                w = wid(t)
                dve.wait_ge(S.sem("out_squares"), S.count("out_squares"))
                dve.tensor_reduce(ASM[0:w, 0, :], AKB[0:w, :, :], AXX, ADD).then_inc(S.sem("out_sums"), 1)
                dve.wait_ge(S.sem("out_sums"), S.count("out_sums"))

            def a_norm3(l, t):
                w = wid(t)
                dve.wait_ge(S.sem("out_roots"), S.count("out_roots"))
                tt(AW[0:w, :, :], AW[0:w, :, :], bc(ASM[0:w, 1, :], 2, [w, 4, 128]), MUL).then_inc(S.sem("out_normed"), 1)
                dve.wait_ge(S.sem("out_normed"), S.count("out_normed"))

            def a_norm4(l, t):
                w = wid(t)
                dve.wait_ge(S.sem("out_t"), S.count("out_t"))
                stt(Z[:, 0, :, tok(t)], v4(M[4], w), P("onorm_a"), Z[:, 0, :, tok(t)], MUL, MUL).then_inc(S.sem("a_done"), 1)
                dve.wait_ge(S.sem("a_done"), S.count("a_done"))

            def a_sout(l, h):
                if h >= 1:
                    dve.wait_ge(S.sem("a_dst"), S.count("a_dst", S.at - 1))
                tt(AEX[0:32], bc(AU[0:32, h, :], 1, [32, NSEQ, 128]), own_seq(32), MUL).then_inc(S.sem("a_uex"), 1)
                dve.wait_ge(S.sem("a_uex"), S.count("a_uex"))
                dve.wait_ge(S.sem("a_dst"), S.count("a_dst"))
                last = seqs(AEG[:, h, 0:32])[:, :, LS - 1:LS].to_broadcast([128, NSEQ, 128])
                link(tt(SD[:, h], SD[:, h], last, MUL))
                tt(SD[:, h], SD[:, h], both(2 * (h % 2)), ADD).then_inc(S.sem("a_sst"), 1)
                dve.wait_ge(S.sem("a_sst"), S.count("a_sst"))

            def b_hist(l):
                dve.wait_ge(S.sem("hist_t"), S.count("hist_t"))
                dve.memset(F[:, :, 0:1], 0.0)
                cp(Fs[:, :, :, 0], M[0][:, 0:8 * NF].rearrange("p (m s) -> p m s", m=NF)).then_inc(S.sem("hist_in"), 1)
                dve.wait_ge(S.sem("hist_in"), S.count("hist_in"))

            def b_shiftout(l):
                dve.wait_ge(S.sem("tails_t"), S.count("tails_t", S.at - 1))
                tails(9, F[:, :, FW - 1:FW], Fs[:, :, :, FS - 1:FS], NF).then_inc(S.sem("tails"), 1)
                dve.wait_ge(S.sem("tails"), S.count("tails"))

            def b_mix(l):
                dve.wait_ge(S.sem("states_stored"), S.count("states_stored"))
                dve.wait_ge(S.sem("states_stored"), S.count("states_stored"))
                link(tt(FM[:, :, 0:SEQ], F[:, :, 0:SEQ], F[:, :, 1:FW], SUB))
                for m in range(NF):
                    ins = stt(FM[:, m, 0:SEQ], FM[:, m, 0:SEQ], P("mu_b", m), F[:, m, 1:FW], MUL, ADD)
                ins.then_inc(S.sem("b_mixed"), 1)
                dve.wait_ge(S.sem("b_mixed"), S.count("b_mixed"))

            def b_lora(l):
                dve.wait_ge(S.sem("b_wt"), S.count("b_wt"))
                half = -0.5 * math.exp(-0.5)
                link(ts(LW[:, :, :], LW[:, :, :], half, half, MUL, ADD))
                for h in range(4):
                    dve.tensor_tensor_scan(LC[:, h, :], C("keep"), LW[:, h, :], 0.0, MUL, ADD)
                dve.wait_ge(S.sem("b_at"), S.count("b_at"))
                ts(AA[:, :, :], AA[:, :, :], 0.5, 0.5, MUL, ADD).then_inc(S.sem("b_lc"), 1)
                dve.wait_ge(S.sem("b_lc"), S.count("b_lc"))

            def b_kk(l):
                for h in range(4):
                    ins = ts(KK[:, h, :], FM[:, 4 + h, :], P("kk_b", h), None, MUL)
                ins.then_inc(S.sem("b_kraw"), 1)
                dve.wait_ge(S.sem("b_kraw"), S.count("b_kraw"))
                mid = LC[:, :, 0:SEQ].rearrange("p h (c n) -> p h c n", c=2)
                link(cp(BM[:, :, 0:2], mid[:, :, :, 63]))
                link(tt(mid, mid, bc(BM[:, :, 0:2], 3, [128, 4, 2, 128]), SUB))
                cp(BM[:, :, 2:4], mid[:, :, :, 127])
                cp(BM[:, :, 4:12], LC[:, :, SEQ:NTOK].rearrange("p h (s c) -> p h s c", c=LS)[:, :, :, LS - 1])
                tt(LW[:, :, :], LC[:, :, :], LW[:, :, :], SUB)
                dve.wait_ge(S.sem("inv_roots"), S.count("inv_roots"))
                link(tt(KK[:, :, :], KK[:, :, :], TMP[:, :, :], MUL))
                for h in range(4):
                    ins = ts(TMP[:, h, :], AA[:, h, :], -1.0, P("ka_b", h), ADD, MUL)
                link(ins)
                stt(FM[:, 4:8, :], TMP[:, :, :], 1.0, FM[:, 4:8, :], ADD, MUL)
                tt(AA[:, :, :], AA[:, :, :], KK[:, :, :], MUL).then_inc(S.sem("b_prep"), 1)
                dve.wait_ge(S.sem("b_prep"), S.count("b_prep"))

            def b_bonus(l):
                for h in range(4):
                    ins = stt(TMP[:, h, :], FM[:, h, :], P("rk_b", h), FM[:, 4 + h, :], MUL, MUL)
                ins.then_inc(S.sem("b_rkm"), 1)
                dve.wait_ge(S.sem("b_rkm"), S.count("b_rkm"))
                dve.wait_ge(S.sem("square_sums"), S.count("square_sums"))
                tt(BON[:, :, :], PS[:, 3:7, 0:NTOK], FM[:, 8:12, :], MUL).then_inc(S.sem("b_bonus_done"), 1)
                dve.wait_ge(S.sem("b_bonus_done"), S.count("b_bonus_done"))

            def b_scale(l, g, t):
                w = wid(t)
                q, q4 = slice(2 * g, 2 * g + 2), slice(4 + 2 * g, 6 + 2 * g)
                dve.wait_ge(S.sem("b_exps"), S.count("b_exps"))
                ar, bk = vx(BAR, 2, w), vx(BBK, 2, w)
                stt(ar[:, :, 0, :], KK[:, q, tok(t)], -1.0, BE[:, 2, :, 0:w], MUL, MUL)
                tt(ar[:, :, 1, :], FM[:, q, tok(t)], BE[:, 0, :, 0:w], MUL)
                tt(bk[:, :, 0, :], AA[:, q, tok(t)], BE[:, 1, :, 0:w], MUL)
                tt(bk[:, :, 1, :], FM[:, q4, tok(t)], BE[:, 1, :, 0:w], MUL).then_inc(S.sem("b_scaled"), 1)
                dve.wait_ge(S.sem("b_scaled"), S.count("b_scaled"))

            def b_pairs(l, g, t):
                w = wid(t)
                dve.wait_ge(S.sem("b_m"), S.count("b_m"))
                si = C("strict_incl") if t < 2 else C("strict_incl_s", 32)
                kk = BKK[0:w, 0:8 * w].rearrange("p (q h n) -> p q h n", q=2, h=2)
                for hh in range(2):
                    m = M[hh][0:w, 0:4 * w].rearrange("p (q x n) -> p q x n", q=2, x=2)
                    ts(of_half(LT, hh)[0:w, :, 0:w], m[:, :, 0, :], -1.0, None, MUL)
                    tt(of_half(BRB, hh)[0:w, :, 0:w], m[:, :, 1, :], bc(si[0:w, w:2 * w], 1, [w, 2, w]), MUL)
                    ins = tt(kk[:, :, hh, :], M[2 + hh][0:w, 0:4 * w].rearrange("p (q n) -> p q n", q=2),
                             bc(si[0:w, 0:2 * w], 1, [w, 2, 2 * w]), MUL)
                ins.then_inc(S.sem("b_masked"), 1)
                dve.wait_ge(S.sem("b_masked"), S.count("b_masked"))

            def b_s0(l, g, pr):
                dve.wait_ge(S.sem("start_read"), S.count("start_read"))
                link(tt(BX[0:64, 1], both(2)[0:64], own_seq(64), MUL))
                dve.tensor_reduce(BR[0:64, pr, :], BX[0:64, 1].rearrange("p s v -> p v s"), AXX, ADD).then_inc(S.sem("start_reduced"), 1)
                dve.wait_ge(S.sem("start_reduced"), S.count("start_reduced"))

            def flat(ap):
                return ap.rearrange("p a b -> p (a b)")

            def b_w(l, g, t):
                w = wid(t)
                dve.wait_ge(S.sem("b_wp"), S.count("b_wp"))
                if t == 2:
                    tt(flat(BW[0:w]), M[0][0:w, 0:256], flat(BR[0:32]), ADD).then_inc(S.sem("b_ws"), 1)
                    dve.wait_ge(S.sem("b_ws"), S.count("b_ws"))
                else:
                    cp(flat(BW[0:w]), M[0][0:w, 0:256]).then_inc(S.sem("b_ws"), 1)
                    dve.wait_ge(S.sem("b_ws"), S.count("b_ws"))

            def b_y(l, g, t):
                w = wid(t)
                dve.wait_ge(S.sem("b_y"), S.count("b_y"))
                if t == 2:
                    tt(flat(BY[0:w]), M[2][0:w, 0:256], flat(BR[32:64]), ADD).then_inc(S.sem("b_ys"), 1)
                    dve.wait_ge(S.sem("b_ys"), S.count("b_ys"))
                    return
                cp(flat(BY[0:w]), M[2][0:w, 0:256]).then_inc(S.sem("b_ys"), 1)
                dve.wait_ge(S.sem("b_ys"), S.count("b_ys"))
                dve.wait_ge(S.sem("b_bm"), S.count("b_bm"))
                new = M[3][:, 0:256].rearrange("p (a b) -> p a b", a=2)
                bd = bc(C("bd"), 1, [128, 2, 128])
                if t == 0:
                    link(tt(BST[:, :, :], new, bd, MUL))
                    for pr in range(2):
                        q = 2 * g + pr
                        ins = ts(BST[:, pr, :], BST[:, pr, :], BM[:, q, 2:3], BM[:, q, 1:2], MUL, MUL)
                else:
                    link(tt(BW[:, :, :], new, bd, MUL))
                    link(tt(BST[:, :, :], BST[:, :, :], BW[:, :, :], ADD))
                    for pr in range(2):
                        ins = ts(BST[:, pr, :], BST[:, pr, :], BM[:, 2 * g + pr, 3:4], None, MUL)
                ins.then_inc(S.sem("b_state"), 1)
                dve.wait_ge(S.sem("b_state"), S.count("b_state"))

            def b_norm1(l, g, t):
                w = wid(t)
                y = flat(BY[0:w]).rearrange("p (h n) -> p h n", h=4)
                link(dve.tensor_reduce(BSM[0:w, 0, :], y, AXX, ADD))
                link(ts(BSM[0:w, 0, :], BSM[0:w, 0, :], 1.0 / 64, None, MUL))
                tt(y, y, bc(BSM[0:w, 0, :], 2, [w, 4, 64]), SUB).then_inc(S.sem("b_yc"), 1)
                dve.wait_ge(S.sem("b_yc"), S.count("b_yc"))

            def b_norm2(l, g, t):
                w = wid(t)
                sq = flat(BQ[0:w]).rearrange("p (h n) -> p h n", h=4)
                dve.wait_ge(S.sem("out_squares"), S.count("out_squares"))
                dve.tensor_reduce(BSM[0:w, 1, :], sq, AXX, ADD).then_inc(S.sem("out_sums"), 1)
                dve.wait_ge(S.sem("out_sums"), S.count("out_sums"))

            def b_norm3(l, g, t):
                w = wid(t)
                y = flat(BY[0:w]).rearrange("p (h n) -> p h n", h=4)
                dve.wait_ge(S.sem("out_roots"), S.count("out_roots"))
                tt(y, y, bc(BSM[0:w, 1, :], 2, [w, 4, 64]), MUL).then_inc(S.sem("out_normed"), 1)
                dve.wait_ge(S.sem("out_normed"), S.count("out_normed"))

            def b_norm4(l, g, t):
                w = wid(t)
                dve.wait_ge(S.sem("out_t"), S.count("out_t"))
                q = slice(2 * g, 2 * g + 2)
                for pr in range(2):
                    ins = ts(BE[:, 0, pr, 0:w], M[4][:, w * pr:w * pr + w], P("gn_g_b", 2 * g + pr), P("gn_b_b", 2 * g + pr),
                             MUL, ADD)
                link(ins)
                link(tt(BE[:, 0, :, 0:w], BE[:, 0, :, 0:w], BON[:, q, tok(t)], ADD))
                stt(Z[:, 1, q, tok(t)], BE[:, 0, :, 0:w], 0.5, Z[:, 1, q, tok(t)], MUL, MUL).then_inc(S.sem("b_done"), 1)
                dve.wait_ge(S.sem("b_done"), S.count("b_done"))

            def b_sout(l, g, pr):
                dve.wait_ge(S.sem("b_pcb"), S.count("b_pcb", S.at - 1))
                for x in range(2):
                    ins = tt(BX[0:32, x], bc(BN[0:32, pr, x, :], 1, [32, NSEQ, 128]), own_seq(32), MUL)
                ins.then_inc(S.sem("b_bex"), 1)
                dve.wait_ge(S.sem("b_bex"), S.count("b_bex"))
                dve.wait_ge(S.sem("b_ds"), S.count("b_ds"))
                tt(BX[0:8, 1], bc(M[2][0:8, 0:128], 1, [8, NSEQ, 128]),
                      C("eye8", 8).unsqueeze(2).to_broadcast([8, NSEQ, 128]), MUL).then_inc(S.sem("b_pcx"), 1)
                dve.wait_ge(S.sem("b_pcx"), S.count("b_pcx"))
                for hh in range(2):
                    r = slice(64 * hh, 64 * hh + 64)
                    ins = tt(BSB[r, pr, :, r], both(0)[r, :, r], BSB[r, pr, :, r], ADD)
                link(ins)
                dve.wait_ge(S.sem("b_pcb"), S.count("b_pcb"))
                for hh in range(2):
                    r = slice(64 * hh, 64 * hh + 64)
                    ins = tt(BSB[r, pr, :, r], both(3)[r, :, r], BSB[r, pr, :, r], MUL)
                ins.then_inc(S.sem("b_snew"), 1)
                dve.wait_ge(S.sem("b_snew"), S.count("b_snew"))

            def c_rms(l, i):
                dve.wait_ge(S.sem("inv_roots"), S.count("inv_roots"))
                q = QC[:, 4 * i:4 * i + 4, :]
                stt(q, q, P(("qn_c", "kn_c")[i]), CSQ[:, :, :], MUL, MUL).then_inc(S.sem("c_n"), 1)
                dve.wait_ge(S.sem("c_n"), S.count("c_n"))

            def c_rope(l, i):
                q = QC[:, 4 * i:4 * i + 4, :]
                dve.wait_ge(S.sem("c_sw"), S.count("c_sw"))
                tt(CSQ[:, :, :], PS[:, 3:7, 0:NTOK], bc(C("sin"), 1, [128, 4, NTOK]), MUL)
                link(tt(q, q, bc(C("cos"), 1, [128, 4, NTOK]), MUL))
                tt(q, q, CSQ[:, :, :], ADD).then_inc(S.sem("c_rope"), 1)
                dve.wait_ge(S.sem("c_rope"), S.count("c_rope"))

            def row_max(out, src):
                link(dve.tensor_reduce(out, src, AXX, ALU.max))
                ts(out, out, -0.125, None, MUL).then_inc(S.sem("c_max"), 1)
                dve.wait_ge(S.sem("c_max"), S.count("c_max"))

            def c_score(l, t, g):
                dve.wait_ge(S.sem("c_s"), S.count("c_s"))
                dve.wait_ge(S.sem("c_pt"), S.count("c_pt", S.at - 1))
                dve.wait_ge(S.sem("c_spt"), S.count("c_spt"))
                mask = C("causal")
                n = 128 * (t + 1)
                for hh in range(2):
                    sc = M[hh][:, 0:2 * n].rearrange("p (q n) -> p q n", q=2)
                    dst = of_half(CP, hh)
                    if t:
                        cp(dst[:, :, 0:128], sc[:, :, 0:128])
                    ins = tt(dst[:, :, n - 128:n], sc[:, :, n - 128:n], bc(mask, 1, [128, 2, 128]), ADD)
                link(ins)
                row_max(CMX[:, 0, :], CP[:, :, 0:128 * (t + 1)])

            def c_prob(l, t, g):
                dve.wait_ge(S.sem("c_e"), S.count("c_e"))
                link(dve.reciprocal(CMX[:, 2, :], CMX[:, 1, :]))

            def c_pv(l, t, g):
                dve.wait_ge(S.sem("c_o"), S.count("c_o"))
                dve.wait_ge(S.sem("c_ot"), S.count("c_ot", S.at - 1))
                tt(CON[:, 256 * g:256 * g + 256].rearrange("p (h n) -> p h n", h=4),
                      M[4][:, 0:256].rearrange("p (h n) -> p h n", h=4), bc(CMX[:, 2, :], 2, [128, 4, 64]), MUL).then_inc(S.sem("c_os"), 1)
                dve.wait_ge(S.sem("c_os"), S.count("c_os"))

            def c_out(l, t):
                dve.wait_ge(S.sem("c_ot"), S.count("c_ot"))
                stt(Z[:, 2, :, tok(t)], v4(M[2], 128), 0.5, Z[:, 2, :, tok(t)], MUL, MUL).then_inc(S.sem("c_done"), 1)
                dve.wait_ge(S.sem("c_done"), S.count("c_done"))

            def c_sprob(l, g):
                dve.wait_ge(S.sem("c_ssc"), S.count("c_ssc"))
                cp(CPS[:, 0:256], M[2 + g][:, 0:256])
                link(tt(CPS[:, 256:NTOK], M[2 + g][:, 256:NTOK], C("causal_new")[:, 32 * g:32 * g + 32], ADD))
                row_max(CMX[:, 0, 0:1], CPS)
                dve.wait_ge(S.sem("c_e"), S.count("c_e"))
                link(dve.reciprocal(CMX[:, 2, 0:1], CMX[:, 1, 0:1]))
                ts(CPS, CPS, CMX[:, 2, 0:1], None, MUL).then_inc(S.sem("c_sp"), 1)
                dve.wait_ge(S.sem("c_sp"), S.count("c_sp"))

            def c_spv(l, g):
                dve.wait_ge(S.sem("c_so"), S.count("c_so"))
                for hh in range(2):
                    r = slice(64 * hh, 64 * hh + 64)
                    o = M[0][r, 0:128].rearrange("p (j q h t) -> p q j h t", j=4, q=4, h=2)[:, :, :, hh, :]
                    z = Z[r, 2, :, SEQ + 16 * g:SEQ + 16 * g + 16].rearrange("p q (j t) -> p q j t", j=4)
                    for q in range(4):
                        ins = stt(z[:, q], o[:, q], 0.5, z[:, q], MUL, MUL)
                ins.then_inc(S.sem("c_sdone"), 1)
                dve.wait_ge(S.sem("c_sdone"), S.count("c_sdone"))

            def finish(l, t):
                dve.wait_ge(S.sem("y_t"), S.count("y_t"))
                for k in range(2):
                    ins = cp(STG[0:wid(t), t, 512 * k:512 * k + 512], M[2 * (t % 2) + k][0:wid(t), :])
                ins.then_inc(S.sem("y_rows"), 1)
                dve.wait_ge(S.sem("y_rows"), S.count("y_rows"))

            do = dict(x_in=x_in, params=params, norm=norm, p_z=p_z, p_up=p_up, p_y=p_y, p_ple=p_ple, a_hist=a_hist,
                      a_convout=a_convout, a_conv=a_conv, a_silu=a_silu, a_l2=a_l2, a_rows=a_rows, a_scale=a_scale,
                      a_pairs=a_pairs, tri=tri, lev=lev, a_s0=a_s0, a_w=a_w, a_o=a_o, a_norm2=a_norm2, a_norm3=a_norm3, a_norm4=a_norm4, a_sout=a_sout,
                      b_hist=b_hist, b_shiftout=b_shiftout, b_mix=b_mix, b_lora=b_lora, b_kk=b_kk, b_bonus=b_bonus,
                      b_scale=b_scale, b_pairs=b_pairs, b_s0=b_s0, b_w=b_w, b_y=b_y, b_norm1=b_norm1, b_norm2=b_norm2, b_norm3=b_norm3, b_norm4=b_norm4, b_sout=b_sout,
                      c_rms=c_rms, c_rope=c_rope, c_score=c_score, c_prob=c_prob, c_pv=c_pv, c_out=c_out, c_sprob=c_sprob, c_spv=c_spv,
                      finish=finish)
            for i, st in enumerate(order):
                S.at = i
                if st[0] in do:
                    do[st[0]](*st[1:])

        @block.gpsimd
        def _(pool):
            own = [0]

            def link(ins):
                own[0] += 1
                ins.then_inc(S.sem("pool_link"), 1)
                pool.wait_ge(S.sem("pool_link"), own[0])

            tt = pool.tensor_tensor
            MUL, ADD, SUB = ALU.mult, ALU.add, ALU.subtract

            def store(out, src, name):
                pool.dma_start(out, src).then_inc(S.sem(name), 16)

            def a_convout(l):
                pool.wait_ge(S.sem("tail_rows"), S.count("tail_rows"))
                store(O["dn_conv_prompt"][l, 0], ROWS[0:3, 0:QKV_A], "tail_rows_stored")
                store(O["dn_conv_sample"][l].rearrange("s c n -> (s c) n"), ROWS[3:27, 0:QKV_A], "tail_rows_stored")

            def a_conv(l):
                for b in range(3):
                    pool.wait_ge(S.sem(f"bank{b}_read"), S.count(f"bank{b}_read"))
                pool.wait_ge(S.sem("hist_in"), S.count("hist_in"))
                pool.wait_ge(S.sem("param_done"), S.count("param_done"))
                if l:
                    pool.wait_ge(S.sem("x_next"), S.count("x_next", S.at - 1))
                out = UC[:, :, SEQ:NTOK].rearrange("p m (s c) -> p m s c", c=LS)
                tmp = TMP[:, 0:2, :].rearrange("p a n -> p (a n)")[:, 0:NA * NS].rearrange("p (m s c) -> p m s c", m=NA, s=NSEQ)
                pool.wait_ge(S.sem("h_ready"), S.count("h_ready"))
                for j in range(CONV_W):
                    w = PT[:, NP1 + NA * j:NP1 + NA * j + NA].unsqueeze(2).unsqueeze(3).to_broadcast([128, NA, NSEQ, LS])
                    link(tt(out if j == 0 else tmp, Us[:, :, :, j:j + LS], w, MUL))
                    if j:
                        ins = tt(out, out, tmp, ADD)
                        if j < CONV_W - 1:
                            link(ins)
                ins.then_inc(S.sem("a_conv_s"), 1)
                pool.wait_ge(S.sem("a_conv_s"), S.count("a_conv_s"))

            def level(t, k, name="tri_lm"):
                w = wid(t)
                tt(LM[0:w, :, 0:w], LT[0:w, :, 0:w], bc(C(f"level{k}", w)[:, 0:w], 1, [w, 4, w]), MUL).then_inc(S.sem(name), 1)
                pool.wait_ge(S.sem(name), S.count(name))

            def tri(l, t):
                pool.wait_ge(S.sem("tri_t0"), S.count("tri_t0"))
                level(t, 1)

            def lev(l, t, k):
                if k < last_level(t):
                    pool.wait_ge(S.sem("tri_y"), S.count("tri_y"))
                    level(t, k + 1)

            def a_o(l, t):
                if t == 1:
                    pool.wait_ge(S.sem("a_state"), S.count("a_state"))
                    store(O["dn_prompt"][l, 0].rearrange("h k v -> k h v"), AST[:, :, :], "states_stored")

            def a_sout(l, h):
                pool.wait_ge(S.sem("a_sst"), S.count("a_sst"))
                store(O["dn_sample"][l, :, h].rearrange("s k v -> k s v"), SD[:, h], "states_stored")

            def b_shiftout(l):
                pool.wait_ge(S.sem("tail_rows"), S.count("tail_rows"))
                store(O["rwkv_shift_prompt"][l], ROWS[0:1, :], "tail_rows_stored")
                store(O["rwkv_shift_sample"][l], ROWS[1:9, :], "tail_rows_stored")

            def b_mix(l):
                for b in range(3):
                    pool.wait_ge(S.sem(f"bank{b}_read"), S.count(f"bank{b}_read"))
                pool.wait_ge(S.sem("hist_in"), S.count("hist_in"))
                pool.wait_ge(S.sem("states_stored"), S.count("states_stored"))
                pool.wait_ge(S.sem("a_done"), S.count("a_done"))
                v = FM[:, :, SEQ:NTOK].rearrange("p m (s c) -> p m s c", c=LS)
                mu = PT[:, PAT["mu_b"]:PAT["mu_b"] + NF].unsqueeze(2).unsqueeze(3).to_broadcast([128, NF, NSEQ, LS])
                link(tt(v, Fs[:, :, :, 0:LS], Fs[:, :, :, 1:], SUB))
                link(tt(v, v, mu, MUL))
                tt(v, v, Fs[:, :, :, 1:], ADD).then_inc(S.sem("b_mixed_s"), 1)
                pool.wait_ge(S.sem("b_mixed_s"), S.count("b_mixed_s"))
                pool.memset(BSB[:, :, :, :], 0.0).then_inc(S.sem("b_cleared"), 1)
                pool.wait_ge(S.sem("b_cleared"), S.count("b_cleared"))

            def b_fin(l, g):
                pool.wait_ge(S.sem("b_fin_s"), S.count("b_fin_s"))
                for pr in range(2):
                    for hh in range(2):
                        r = slice(64 * hh, 64 * hh + 64)
                        store(O["rwkv_prompt"][l, 0, 4 * g + 2 * pr + hh], BSO[r, pr, r], "states_stored")

            def b_sout(l, g, pr):
                pool.wait_ge(S.sem("b_snew"), S.count("b_snew"))
                for hh in range(2):
                    r = slice(64 * hh, 64 * hh + 64)
                    store(O["rwkv_sample"][l, :, 4 * g + 2 * pr + hh].rearrange("s v k -> v s k"), BSB[r, pr, :, r],
                          "states_stored")

            def c_nat(l, i):
                if i == 0:
                    pool.wait_ge(S.sem("c_rope"), S.count("c_rope"))
                    pool.wait_ge(S.sem("b_snew"), S.count("b_snew"))
                    link(pool.memset(CQX[:, :, :, :], 0.0))
                    for pr in range(4):
                        for hh in range(2):
                            r = slice(64 * hh, 64 * hh + 64)
                            h = 2 * pr + hh
                            ins = pool.tensor_copy(CQX[r, pr, :, 4 * h:4 * h + 4], seqs(QC[r, pr, SEQ:NTOK]))
                    ins.then_inc(S.sem("c_qx"), 1)
                    pool.wait_ge(S.sem("c_qx"), S.count("c_qx"))
                pool.wait_ge(S.sem("c_ns"), S.count("c_ns"))
                src, name = ((CKN, "k"), (CVN, "v"))[i]
                store(O[f"{name}_prompt"][l, 0].rearrange("(t p) h d -> p t (h d)", p=128), src[:, 0:2, :], "kv_stored")
                store(O[f"{name}_sample"][l].rearrange("s t h d -> (s t) (h d)"), src[0:32, 2, :], "kv_stored")

            def finish(l, t):
                pool.wait_ge(S.sem("y_rows"), S.count("y_rows"))
                a, n = TILES[t]
                if t < 2:
                    store(O["y_prompt"][0, a:a + n, :], STG[0:n, t, :], "y_stored")
                else:
                    store(O["y_sample"].rearrange("s t d -> (s t) d"), STG[0:n, t, :], "y_stored")
                    for name in ("y_stored", "kv_stored", "states_stored", "tail_rows_stored"):
                        pool.wait_ge(S.sem(name), S.count(name))

            do = dict(a_convout=a_convout, a_conv=a_conv, tri=tri, lev=lev, a_o=a_o, a_sout=a_sout, b_shiftout=b_shiftout,
                      b_mix=b_mix, b_fin=b_fin, b_sout=b_sout, c_nat=c_nat, finish=finish)
            for i, st in enumerate(order):
                S.at = i
                if st[0] in do:
                    do[st[0]](*st[1:])


IN_NAMES = ["x_prompt", "x_sample", "cache_k", "cache_v", "state_dn", "state_dn_conv", "state_rwkv",
            "state_rwkv_shift", "page_table", "p_prompt", "p_sample", "norm_g", "w_in", "conv_a", "a_log", "dt_bias",
            "onorm_a", "mu_b", "w0_b", "w2_b", "a0_b", "a2_b", "kk_b", "ka_b", "rk_b", "gn_g_b", "gn_b_b", "qn_c",
            "kn_c", "w_branch", "b_gate", "w_out", "w_ple", "w_pg", "b_pg"]
OUT_SHAPES = [("y_prompt", (1, 256, 1024)), ("y_sample", (8, 4, 1024)), ("k_prompt", (2, 1, 256, 8, 64)),
              ("v_prompt", (2, 1, 256, 8, 64)), ("dn_prompt", (2, 1, 4, 128, 128)), ("dn_conv_prompt", (2, 1, 3, 1536)),
              ("rwkv_prompt", (2, 1, 8, 64, 64)), ("rwkv_shift_prompt", (2, 1, 1664)), ("k_sample", (2, 8, 4, 8, 64)),
              ("v_sample", (2, 8, 4, 8, 64)), ("dn_sample", (2, 8, 4, 128, 128)), ("dn_conv_sample", (2, 8, 3, 1536)),
              ("rwkv_sample", (2, 8, 8, 64, 64)), ("rwkv_shift_sample", (2, 8, 1664))]


def kernel(**inputs):
    import concourse.bacc as bacc
    from concourse.bass_utils import run_bass_kernel_spmd
    arrays = {n: np.ascontiguousarray(inputs[n]) for n in IN_NAMES}
    arrays["const_table"] = CONSTS
    nc = bacc.Bacc("TRN2", target_bir_lowering=False, num_devices=1)
    A = {n: nc.dram_tensor(f"in_{n}", a.shape, mybir.dt.from_np(a.dtype), kind="ExternalInput").ap()
         for n, a in arrays.items()}
    O = {n: nc.dram_tensor(f"out_{n}", s, FP32, kind="ExternalOutput").ap() for n, s in OUT_SHAPES}
    program(nc, A, O)
    r = run_bass_kernel_spmd(nc, [{f"in_{n}": a for n, a in arrays.items()}], core_ids=[0])
    return tuple(r.results[0][f"out_{n}"] for n, _ in OUT_SHAPES)
```

```python
import math

import numpy as np
import concourse.bass as bass
from concourse import mybir
from contextlib import ExitStack

FP32 = mybir.dt.float32
I32 = mybir.dt.int32
ALU = mybir.AluOpType
ACT = mybir.ActivationFunctionType
AXX = mybir.AxisListType.X

D_MODEL, SEQ, DEPTH, NSEQ, LS, PAST, PAGE = 1024, 256, 2, 8, 4, 256, 128
D_PLE, W = 256, 512
KT_ = D_MODEL // 128
NTOK = SEQ + NSEQ * LS
NS = NSEQ * LS
QKV_A, CONV_W, SHIFT_B = 1536, 4, 1664
NA, NF, NC3 = QKV_A // 128, SHIFT_B // 128, 1536 // 128
OFF_QKVA, OFF_ZA, OFF_BA, OFF_F, OFF_ZB, OFF_QKVC, OFF_ZC, OFF_G = 0, 1536, 2048, 2056, 3720, 4232, 5768, 6280
UW = CONV_W - 1 + SEQ
US = CONV_W - 1 + LS
FW = 1 + SEQ
FS = 1 + LS
NEG = -1.0e30
NLEV = 7
TILES = [(0, 128), (128, 128), (256, 32)]
RING = 4
SPARE_B = 9
SLOT = 2048

CONST_LAYOUT = {}


def constants():
    cols, at = [], 0

    def put(name, a):
        nonlocal at
        full = np.zeros((128, a.shape[1]), np.float32)
        full[:a.shape[0]] = a
        CONST_LAYOUT[name] = (at, a.shape[1])
        at += a.shape[1]
        cols.append(full)

    p = np.arange(128)
    s, t = p[:, None], p[None, :]
    put("ident", np.eye(128))
    put("ones", np.ones((128, 128)))
    put("ones_head", (s // 64 == t // 64) * 1.0)
    swap = np.zeros((128, 128))
    for h in range(2):
        for j in range(8):
            swap[64 * h + 8 + j, 64 * h + j] = -1.0
            swap[64 * h + j, 64 * h + 8 + j] = 1.0
    put("swap", swap)
    for k in range(NLEV):
        b = 2 ** k
        put(f"level{k}", ((s // (2 * b) == t // (2 * b)) & ((s // b) % 2 == 0) & ((t // b) % 2 == 1)) * 1.0)
    put("strict_incl", np.concatenate([(s < t) * 1.0, (s <= t) * 1.0], 1))
    same = (s // LS == t // LS)[:32, :32]
    put("strict_incl_s", np.concatenate([(same & (s < t)[:32, :32]) * 1.0, (same & (s <= t)[:32, :32]) * 1.0], 1))
    put("causal", np.where(t <= s, 0.0, NEG))
    new = np.full((128, 2, 32), NEG)
    for q in range(128):
        j, tt = q // 32, q % 4
        for g in range(2):
            new[q, g, (4 * g + j) * 4:(4 * g + j) * 4 + tt + 1] = 0.0
    put("causal_new", new.reshape(128, 64))
    put("own_seq", ((p % 32)[:, None] // LS == np.arange(NSEQ)[None, :])[:64] * 1.0)
    put("eye8", np.eye(8))
    sel = np.zeros((4, 4, 128))
    for h in range(4):
        sel[h, h] = 1.0
    put("pick_head", sel.reshape(4, 512))
    pos = np.concatenate([np.arange(SEQ), np.tile(PAST + np.arange(LS), NSEQ)]).astype(np.float32)
    inv = (np.float32(500000.0) ** (-np.arange(8, dtype=np.float32) / np.float32(8))).astype(np.float32)
    ang = (inv[:, None] * pos[None, :]).astype(np.float32)
    cos, sin = np.ones((128, NTOK)), np.zeros((128, NTOK))
    for h in range(2):
        for half in range(2):
            r = 64 * h + 8 * half
            cos[r:r + 8], sin[r:r + 8] = np.cos(ang), np.sin(ang)
    put("cos", cos)
    put("sin", sin)
    keep = np.ones((128, NTOK))
    keep[:, [0, 128] + list(range(SEQ, NTOK, LS))] = 0.0
    put("keep", keep)
    for name, v in [("c_1", 1.0), ("c_eps", 1e-6), ("c_4eps", 4e-6), ("c_gneps", 64e-5),
                    ("c_lndk", math.log(128.0 ** -0.5)), ("c_lnhalf", math.log(0.5)), ("c_0", 0.0)]:
        put(name, np.full((128, 1), v))
    return np.concatenate(cols, 1).astype(np.float32)


CONSTS = constants()

PROWS = [("norm_g", 8), ("mu_b", 13), ("b_gate", 24), ("w0_b", 4), ("a0_b", 4), ("kk_b", 4), ("ka_b", 4),
         ("rk_b", 4), ("gn_g_b", 4), ("gn_b_b", 4), ("b_pg", 8), ("onorm_a", 1), ("qn_c", 1), ("kn_c", 1)]
PAT, _n = {}, 0
for _name, _k in PROWS:
    PAT[_name] = _n
    _n += _k
NP1 = _n
NPAR = NP1 + 48


SIGNALS = {
    "ident_loaded": {"x_in": (16, lambda st: st[2] == 0)},
    "consts_loaded": {"x_in": (16, lambda st: st[2] == 0)},
    "x_loaded": {"x_in": (48, lambda st: st[2] == 0)},
    "pages_loaded": {"x_in": (16, lambda st: st[2] == 0)},
    "param_rows_loaded": {"params_load": (16 * (len(PROWS) + 3), None)},
    "heads_loaded": {"params_load": (32, None)},
    "ple_rows_loaded": {"params_load": (48, None)},
    "hist_loaded": {"a_hist": (16, None), "b_hist": (16, None)},
    "lora_loaded": {"b_hist": (32, None)},
    "dn_state_loaded": {"a_conv": (64, lambda st: st[2] == 0)},
    "rw_state_loaded": {"b_scale": (64, lambda st: st[3] == 0)},
    "past_k0_loaded": {"c_fetch_k": (32, lambda st: st[2] % 2 == 0)},
    "past_k1_loaded": {"c_fetch_k": (32, lambda st: st[2] % 2 == 1)},
    "past_v0_loaded": {"c_fetch_v": (32, lambda st: st[2] < 4)},
    "past_v1_loaded": {"c_fetch_v": (32, lambda st: st[2] >= 4)},
    "kv_stored": {"c_nat": (32, None)},
    "states_stored": {"a_o": (16, lambda st: st[2] == 1), "a_sout": (16, None), "b_fin": (64, None), "b_sdec": (32, None)},
    "tail_rows_stored": {"a_convout": (32, None), "b_shiftout": (32, None)},
    "y_stored": {"finish": (16, None)},
    "a_conv_p": {"a_conv": (1, None)},
    "a_conv_s": {"a_conv": (1, lambda st: st[2] == 0)},
    "a_done": {"a_norm6": (1, None)},
    "a_dst": {"a_sout": (1, None)},
    "a_exps": {"a_scale": (1, None)},
    "a_g": {"a_rows": (1, None)},
    "a_gb": {"a_scale": (1, None)},
    "a_gcol_t": {"a_rows": (1, None)},
    "a_kk0": {"a_pairs": (1, None)},
    "a_kk": {"a_pairs": (1, None)},
    "a_klast": {"a_scale": (1, None)},
    "a_lt": {"a_keys": (1, None)},
    "a_nat": {"a_pairs": (1, None)},
    "a_o": {"a_o": (1, None)},
    "a_os": {"a_o": (1, None)},
    "a_scaled": {"a_scale": (1, None)},
    "a_silu": {"a_silu": (1, None)},
    "a_sdec": {"a_sout": (1, None)},
    "a_sst": {"a_sout": (1, None)},
    "a_tanh": {"a_silu": (1, None)},
    "a_uex": {"a_sout": (1, None)},
    "a_unit": {"a_l2": (1, None)},
    "b_araw": {"b_lora": (1, None)},
    "b_at": {"b_lora": (1, None)},
    "b_bex": {"b_sout": (1, None)},
    "b_bm": {"b_kk": (1, None)},
    "b_bonus_done": {"b_bonus": (1, None)},
    "b_cleared": {"b_mix": (1, None)},
    "b_done": {"b_norm6": (1, None)},
    "b_ds": {"b_sout": (1, None)},
    "b_exps": {"b_exp": (1, None)},
    "b_fin_s": {"b_fin": (1, None)},
    "b_fin_t": {"b_fin": (1, None)},
    "b_kraw": {"b_kk": (1, None)},
    "b_lc": {"b_lora": (1, None)},
    "b_lt": {"b_lora": (1, None)},
    "b_m0": {"b_pairs": (1, None)},
    "b_m": {"b_pairs": (1, None)},
    "b_masked": {"b_keys": (1, None)},
    "b_mixed": {"b_mix": (1, None)},
    "b_mixed_s": {"b_mix": (1, None)},
    "b_nats": {"b_pairs": (1, None)},
    "b_pcb": {"b_sdec": (1, None)},
    "b_pcx": {"b_sout": (1, None)},
    "b_prep": {"b_kk": (1, None)},
    "b_rkm": {"b_bonus": (1, None)},
    "b_s_t": {"b_st": (1, None)},
    "b_s_ts": {"b_st": (1, None)},
    "b_scaled": {"b_scale": (1, None)},
    "b_snew": {"b_sdec": (1, None)},
    "b_vs": {"b_nat": (1, None)},
    "b_vt": {"b_nat": (1, None)},
    "b_wp": {"b_w": (1, None)},
    "b_wraw": {"b_lora": (1, None)},
    "b_ws": {"b_w": (1, None)},
    "b_wt": {"b_lora": (1, None)},
    "b_y": {"b_y": (1, None)},
    "b_yc": {"b_norm1": (1, None)},
    "b_ys": {"b_y": (1, None)},
    "ba_ln": {"a_rows": (1, None)},
    "ba_neg": {"a_rows": (1, None)},
    "c_done": {"c_out": (1, None)},
    "c_e": {"c_prob": (1, None), "c_sprob": (1, None)},
    "c_max": {"c_score": (1, None), "c_sprob": (1, None)},
    "c_n": {"c_rms": (1, None)},
    "c_ns": {"c_nat": (1, None)},
    "c_nt": {"c_nat": (1, None)},
    "c_o": {"c_pv": (1, None)},
    "c_os": {"c_pv": (1, None)},
    "c_ot": {"c_out": (1, None)},
    "c_pt": {"c_prob": (1, None)},
    "c_pts": {"c_prob": (1, None)},
    "c_rope": {"c_rope": (1, None)},
    "c_s": {"c_score": (1, None)},
    "c_sdone": {"c_spv": (1, None)},
    "c_so": {"c_spv": (1, None)},
    "c_sp": {"c_sprob": (1, None)},
    "c_spt": {"c_sprob": (1, None)},
    "c_spts": {"c_sprob": (1, None)},
    "c_ssc": {"c_past": (1, None)},
    "c_sw": {"c_rope": (1, None)},
    "corrected": {"a_u": (1, None), "b_u": (1, None)},
    "corrected_s": {"a_u": (1, None), "b_u": (1, None)},
    "decay_rate": {"params": (1, None)},
    "h_ready": {"norm": (8, None)},
    "hist_in": {"a_hist": (1, None), "b_hist": (1, None)},
    "hist_t": {"a_hist": (1, None), "b_hist": (1, None)},
    "inv_roots": {"norm": (1, None), "a_l2": (1, None), "b_kk": (1, None), "c_rms": (1, None)},
    "out_normed": {"a_norm5": (1, None), "b_norm5": (1, None)},
    "out_roots": {"a_norm4": (1, None), "b_norm4": (1, None)},
    "out_squares": {"a_norm2": (1, None), "b_norm2": (1, None)},
    "out_sums": {"a_norm3": (1, None), "b_norm3": (1, None)},
    "out_t": {"a_norm5": (1, None), "b_norm5": (1, None)},
    "param_done": {"params": (1, None)},
    "param_t": {"params_t": (1, None)},
    "past_k_t": {"c_keys": (1, None)},
    "past_k_ts": {"c_keys": (1, None)},
    "projected": {"p_a": (1, None), "p_z": (1, None), "p_ba": (1, None), "p_f": (1, None), "p_c": (1, None), "p_g": (1, None), "p_up": (1, None), "p_y": (1, None), "p_pg": (1, None), "p_ple": (1, None)},
    "square_sums": {"norm": (1, None), "a_l2": (1, None), "b_kk": (1, None), "b_bonus": (1, None), "c_rms": (1, None)},
    "squares": {"norm": (2, None), "a_l2": (1, None), "b_kk": (1, None), "c_rms": (1, None)},
    "start_read": {"a_s0": (1, None), "b_s0": (1, None)},
    "start_reduced": {"a_s0": (1, None), "b_s0": (1, None)},
    "tail_rows": {"a_convout": (1, None), "b_shiftout": (1, None)},
    "tails": {"a_convout": (1, None), "b_shiftout": (1, None)},
    "tails_t": {"a_convout": (1, None), "b_shiftout": (1, None)},
    "tri_i0": {"tri": (1, None)},
    "tri_t0": {"tri": (1, None)},
    "tri_tr": {"tri": (1, None)},
    "tri_up": {"lev": (1, None)},
    "tri_y": {"lev": (2, None)},
    "tri_ys": {"lev": (2, None)},
    "tri_zt": {"lev": (1, None)},
    "tri_z": {"lev": (1, lambda st: st[3] < (NLEV - 1 if st[2] < 2 else 1))},
    "tri_iup": {"lev": (1, lambda st: st[3] < (NLEV - 1 if st[2] < 2 else 1))},
    "x_next": {"p_ple": (1, None)},
    "x_t": {"x_in": (1, None)},
    "x_tr": {"x_in": (1, None)},
    "y_rows": {"finish": (1, None)},
    "y_t": {"finish": (1, None)},
    "z_tanh": {"p_z": (1, None)},
    "a_ks": {"a_w": (1, lambda st: st[2] == 1)},
    "a_w": {"a_w": (1, lambda st: st[2] > 0)},
    "a_state": {"a_o": (1, lambda st: st[2] < 2)},
    "b_state": {"b_y": (1, lambda st: st[3] < 2)},
    "c_qx": {"c_nat": (1, lambda st: st[2] == 0)},
    "merged": {"p_up": (1, lambda st: st[2] > 0)},
    "tri_lm": {"tri": (1, None), "lev": (1, lambda st: st[3] < (NLEV - 1 if st[2] < 2 else 1))},
}
PROJECTIONS = ("p_a", "p_z", "p_ba", "p_f", "p_c", "p_g", "p_up", "p_y", "p_pg", "p_ple")


class Steps:

    def __init__(self, nc, ctx, order):
        self.nc, self.ctx, self.order, self.at, self.sems, self.totals = nc, ctx, order, 0, {}, {}
        for name, where in SIGNALS.items():
            self.tally(name, [self.by(st, where) for st in order])
        projections = [int(st[0] in PROJECTIONS) for st in order]
        number = np.cumsum(projections) - 1
        for b in range(3):
            self.tally(f"bank{b}_read", [int(p and n % 3 == b) for p, n in zip(projections, number)])

    @staticmethod
    def by(st, where):
        by, when = where.get(st[0], (0, None))
        return by if by and (when is None or when(st)) else 0

    def tally(self, name, values):
        self.totals[name] = [0] + [int(v) for v in np.cumsum(values)]

    def sem(self, name):
        if name not in self.sems:
            self.sems[name] = self.ctx.enter_context(self.nc.semaphore(name))
        return self.sems[name]

    def count(self, name, upto=None):
        return self.totals[name][(self.at if upto is None else upto) + 1]


def mixer_steps():
    steps, parts = [], []

    def add(*s):
        steps.append(s)

    def part():
        if parts:
            add(*parts.pop(0))

    add("a_convout")
    add("a_rows")
    add("a_conv", 0)
    for c in range(3):
        if c < 2:
            add("a_conv", c + 1)
        add("a_silu", c)
    for i in range(2):
        add("a_l2", i)
    for t in range(3):
        add("a_scale", t)
        add("a_pairs", t)
        add("tri", t)
        add("a_keys", t)
        part()
        for k in range(1, NLEV if t < 2 else 2):
            if k == NLEV - 1:
                add("a_w", t)
            add("lev", t, k)
            part()
        if t == 2:
            for h in range(4):
                add("a_s0", h)
                part()
            part()
            add("a_w", t)
        add("a_u", t)
        add("a_o", t)
        parts += [(f"a_norm{i}", t) for i in range(2, 7)]
    for h in range(4):
        add("a_sout", h)
        part()
    part()
    add("b_hist")
    add("b_shiftout")
    add("b_mix")
    add("b_lora")
    add("b_kk")
    add("b_bonus")
    units = [(g, t) for g in range(2) for t in range(3)]
    add("b_exp", 0, 0)
    for g in range(2):
        for t in range(3):
            add("b_nat", g, t)
            add("b_scale", g, t)
            add("b_pairs", g, t)
            add("tri", t)
            add("b_keys", g, t)
            part()
            for k in range(1, NLEV if t < 2 else 2):
                if k == NLEV - 1:
                    add("b_w", g, t)
                add("lev", t, k)
                part()
            if t == 2:
                add("b_st", g, 0)
                part()
                add("b_s0", g, 0)
                part()
                add("b_st", g, 1)
                part()
                add("b_s0", g, 1)
                part()
                add("b_w", g, t)
            if (g, t) != units[-1]:
                add("b_exp", *units[3 * g + t + 1])
            add("b_u", g, t)
            add("b_y", g, t)
            parts += [(f"b_norm{i}", g, t) for i in range(1, 7)]
        part()
        add("b_fin", g)
        add("b_sout", g, 0)
        part()
        add("b_sdec", g, 0)
        if g:
            part()
        add("b_sout", g, 1)
        if g:
            part()
        add("b_sdec", g, 1)
    part()
    part()
    for q in range(4):
        if q < 2:
            add("c_fetch_k", q)
        add("c_fetch_v", q)
    add("c_rms", 0)
    add("c_rms", 1)
    add("c_rope", 0)
    add("c_rope", 1)
    add("c_nat", 0)
    add("c_nat", 1)

    def sampled(g):
        for j in range(5):
            if j < 4:
                add("c_keys", g, j)
                if 4 * g + j + 2 < NSEQ:
                    add("c_fetch_k", 4 * g + j + 2)
            if j:
                add("c_past", g, j - 1)
        add("c_sprob", g)
        add("c_spv", g)

    sampled(0)
    for q in range(4, 8):
        add("c_fetch_v", q)
    blocks = [(t, g) for t in range(2) for g in range(2)]
    add("c_score", *blocks[0])
    for i, (t, g) in enumerate(blocks):
        add("c_prob", t, g)
        if i + 1 < len(blocks):
            add("c_score", *blocks[i + 1])
        add("c_pv", t, g)
        if g == 1:
            add("c_out", t)
    sampled(1)
    return steps


def spare_projections():
    spare = [("p_f", m) for m in range(6)] + [("p_z", 0, m) for m in range(4)] + [("p_f", m) for m in range(6, NF)]
    spare += [("p_z", 1, m) for m in range(4)] + [("p_c", m) for m in range(NC3)]
    spare += [("p_z", 2, m) for m in range(4)]
    spare += [("p_g", m) for m in range(8)]
    for m in range(8, 16):
        spare += [("p_up", 0, m - 8), ("p_g", m)]
    for m in range(8):
        spare += [("p_up", 1, m), ("p_g", 16 + m)]
    return spare


PLACES = [3, 4, 5, 5, 7, 7, 9, 9, 9, 10, 10, 10, 11, 12, 15, 18, 22, 24, 24, 28, 34, 39, 41, 42, 47, 49, 51, 53, 55,
          55, 58, 61, 63, 65, 69, 70, 70, 72, 72, 76, 80, 108, 117, 125, 132, 145, 158, 184, 188, 190, 192,
          192, 192, 196, 196, 201, 217, 223, 226, 230, 232, 247, 253, 254, 256, 259, 261, 262, 262, 262,
          262, 262, 262, 263, 263, 263, 263]


def schedule():
    order = [("x_in", 0, 0), ("params_load", 0), ("x_in", 0, 1), ("x_in", 0, 2), ("params_t", 0)]
    for l in range(DEPTH):
        def add(*s):
            order.append((s[0], l) + s[1:])

        add("params")
        add("norm")
        add("p_a", 0)
        add("a_hist")
        for m in range(1, NA):
            add("p_a", m)
        add("p_ba")
        spare = list(zip(PLACES, spare_projections()))
        for i, step in enumerate(mixer_steps()):
            while spare and spare[0][0] <= i:
                add(*spare.pop(0)[1])
            add(*step)
        for _, s in spare:
            add(*s)
        if l + 1 < DEPTH:
            order.append(("params_load", l + 1))
        for m in range(8):
            add("p_up", 2, m)
        for m in range(8):
            add("p_y", m)
        if l + 1 < DEPTH:
            order.append(("params_t", l + 1))
        for m in range(8):
            add("p_pg", m)
            add("p_ple", m)
    order += [("finish", DEPTH, t) for t in range(3)]
    return order


def weight_chunks(A, order):
    w_in = A["w_in"].rearrange("l (k p) n -> l p k n", p=128)
    w_br = A["w_branch"].rearrange("l b (k p) n -> l b p k n", p=128)
    w_out = A["w_out"].rearrange("l (k p) n -> l p k n", p=128)
    w_pg = A["w_pg"].rearrange("l (k p) n -> l p k n", p=128)
    w_ple = A["w_ple"].rearrange("l (k p) n -> l p k n", p=128)
    chunks, use, open_ = [], {}, {}

    def tile(step, key, view, k, col0, cols):
        if key not in open_:
            open_[key] = len(chunks)
            chunks.append([step, step, view, k, cols])
        c = chunks[open_[key]]
        c[1] = step
        use[step] = (open_[key], col0)

    for i, st in enumerate(order):
        kind, l = st[0], (st[1] if len(st) > 1 else 0)
        m = st[-1]
        if kind in ("p_a", "p_f", "p_c", "p_g", "p_z"):
            off = {"p_a": OFF_QKVA, "p_f": OFF_F, "p_c": OFF_QKVC, "p_g": OFF_G}.get(kind)
            key = (kind, l, m // 2)
            if kind == "p_z":
                off = (OFF_ZA, OFF_ZB, OFF_ZC)[st[2]]
                key = (kind, l, st[2], m // 2)
            a = off + 256 * (m // 2)
            n = 128 if (kind == "p_f" and m == NF - 1) else 256
            tile(i, key, w_in[l, :, :, a:a + n], KT_, 128 * (m % 2), n)
        elif kind == "p_ba":
            tile(i, (kind, l), w_in[l, :, :, OFF_BA:OFF_BA + 8], KT_, 0, 8)
        elif kind == "p_up":
            n = st[2]
            a = 256 * (m // 2)
            tile(i, (kind, l, n, m // 2), w_br[l, n, :, :, a:a + 256], 4, 128 * (m % 2), 256)
        elif kind in ("p_y", "p_pg"):
            a = 256 * (m // 2)
            tile(i, (kind, l, m // 2), (w_out if kind == "p_y" else w_pg)[l, :, :, a:a + 256], KT_,
                 128 * (m % 2), 256)
        elif kind == "p_ple":
            tile(i, (kind, l), w_ple[l], 2, 128 * m, 1024)
    return chunks, use


def program(nc, A, O):
    order = schedule()
    chunks, use = weight_chunks(A, order)
    steps_of = {}
    for i, st in enumerate(order):
        steps_of.setdefault(st[0], []).append(i)
    ctx = ExitStack()
    with ctx:
        S = Steps(nc, ctx, order)

        def sb(name, shape, dt=FP32):
            return ctx.enter_context(nc.sbuf_tensor(name, shape, dt))

        CN = sb("consts", [128, CONSTS.shape[1]])
        ring = sb("ring", [128, RING, SLOT])
        XA = sb("x_a", [128, 8, NTOK])
        XB = sb("x_b", [128, 8, NTOK])
        Z = sb("z", [128, 3, 4, NTOK])
        UQ = sb("conv_in", [128, NA * (UW + NSEQ * US)])
        U = UQ[:, :].rearrange("p (m n) -> p m n", m=NA)
        QC = UQ[:, 0:NC3 * NTOK].rearrange("p (m n) -> p m n", m=NC3)
        F = sb("shift_in", [128, NF, FW + NSEQ * FS])
        PT = sb("params", [128, NPAR])
        PH = sb("params_half", [128, NPAR])
        HP = sb("head_params", [4, 4])
        PLT = sb("ple_t", [128, 2, NTOK])
        TH = sb("tanh_z", [128, 2, NTOK])
        TMP = sb("tmp", [128, 4, NTOK])
        PRN = sb("param_rows", [128, 2, 128])
        PTAB = sb("pages", [1, NSEQ * 2], I32)
        TRI = sb("triangles", [128, 5 * 512])
        LT, LM, TI, TT, Y = (TRI[:, 512 * i:512 * i + 512].rearrange("p (h n) -> p h n", h=4) for i in range(5))
        ROWS = TRI[0:27, 0:SHIFT_B]
        CT = TRI[:, SHIFT_B:SHIFT_B + NA * 27]
        WLO = TRI[:, 2048:2560]
        MG = sb("merged", [128, 8, NTOK])
        ARW = 18144
        arena = sb("arena", [128, ARW])
        PS = ctx.enter_context(nc.psum_tensor("psum", [128, 8, 512], FP32))
        M = [PS[:, 3 + b, :] for b in range(5)]

        top = [0]

        def part(*shape):
            n = int(np.prod(shape))
            a = arena[:, top[0]:top[0] + n]
            top[0] += n
            assert top[0] <= ARW, top[0]
            names = "abcd"[:len(shape)]
            if len(shape) > 1:
                a = a.rearrange("p (%s) -> p %s" % (" ".join(names), " ".join(names)),
                                **{c: int(k) for c, k in zip(names[1:], shape[1:])})
            return a

        UC = part(NA, NTOK)
        SD = part(4, NSEQ, 128)
        AEG, AGB, ADI, AKB, AVB, AKD = (part(4, 128) for _ in range(6))
        AKQ = part(1024)
        AVN, AKN, AQK, AW, AU, AST, AR = (part(4, 128) for _ in range(7))
        AEX = part(NSEQ, 128)
        ABG = part(2, NTOK)
        ATM = AEX.rearrange("p a b -> p (a b)")[:, 0:3 * NTOK].rearrange("p (a b) -> p a b", a=3)
        AGC = part(3, 4)
        ASM = part(2, 4)
        top[0] = 0
        FM = part(NF, NTOK)
        LW, AA, LC, KK = (part(4, NTOK) for _ in range(4))
        BON = TMP
        BE = part(3, 2, 128)
        BAR, BBK = part(512), part(512)
        BN = part(2, 2, 128)
        BVN = part(2, 128)
        BRB = part(4, 128)
        BKK = part(1024)
        BW, BU, BY, BSO = (part(2, 128) for _ in range(4))
        BQ = BW
        BSM = part(3, 4)
        BST = part(2, 128)
        BSB = part(2, NSEQ, 128)
        BX = part(2, NSEQ, 128)
        BR = part(2, 128)
        BM = part(4, 12)
        top[0] = 0
        CSQ = part(4, NTOK)
        CKN, CVN = part(3, W), part(3, W)
        SQ = (CSQ, CVN[:, :, :].rearrange("p a n -> p (a n)")[:, 0:4 * NTOK].rearrange("p (a n) -> p a n", a=4))
        CP = part(4, 256)
        CPT = part(2, 4, 128)
        CON = part(W)
        CMX = part(3, 4)
        CQX = part(4, NSEQ, 32)
        CKR = part(2, 2, W)
        CVR = part(4, 2, W)
        CKT = part(2, 4, 256)
        GTC = part(7, NTOK)
        PLN = CKT[:, :, :, :].rearrange("p a b n -> p (a b n)")[:, 0:3 * D_PLE].rearrange("p (a n) -> p a n", a=3)
        CPS = CP.rearrange("p a b -> p (a b)")[:, 0:NTOK]
        CPTS = CPT.rearrange("p a b c -> p (a b c)")[:, 0:384].rearrange("p (a b) -> p a b", a=3)
        top[0] = 0
        STG = part(3, D_MODEL)
        XN = arena[:, 0:3 * D_MODEL].rearrange("p (t n) -> p t n", t=3)

        def C(name, rows=128):
            a, n = CONST_LAYOUT[name]
            return CN[0:rows, a:a + n]

        def P(name, i=0, rows=128):
            c = PAT[name] + i
            return PT[0:rows, c:c + 1]

        def gate(m):
            return F[:, m, 0:NTOK] if m < NF else GTC[:, m - NF, :] if m < NF + 7 else CSQ[:, m - NF - 7, :]

        def Phalf(name, i=0):
            c = PAT[name] + i
            return PH[:, c:c + 1]

        def bc(ap, axis, shape):
            return ap.unsqueeze(axis).to_broadcast(shape)

        def v4(b, w, rows=128):
            return b[0:rows, 0:4 * w].rearrange("p (h n) -> p h n", h=4)

        def vx(buf, n, w, rows=128):
            return buf[0:rows, 0:2 * n * w].rearrange("p (h x n) -> p h x n", h=n, x=2)

        def of_half(buf, hh):
            return buf[:, :, :].rearrange("p (q h) n -> p q h n", h=2)[:, :, hh, :]

        def seqs(ap):
            return ap.rearrange("p (s c) -> p s c", c=LS)

        ident = C("ident")
        Us = U[:, :, UW:].rearrange("p m (s c) -> p m s c", c=US)
        Fs = F[:, :, FW:].rearrange("p m (s c) -> p m s c", c=FS)
        X = lambda l: (XA, XB)[l % 2]
        H = lambda l: (XB, XA)[l % 2]
        tok = lambda t: slice(TILES[t][0], TILES[t][0] + TILES[t][1])
        wid = lambda t: TILES[t][1]
        last_level = lambda t: NLEV - 1 if t < 2 else 1
        level_width = lambda t, k: 64 if k == NLEV - 1 else wid(t)

        proj_at = [i for i, st in enumerate(order) if st[0].startswith("p_")]
        proj_no = {i: n for n, i in enumerate(proj_at)}

        def bank():
            return PS[:, proj_no[S.at] % 3, :]

        def freed(i=None):
            return f"bank{proj_no[S.at if i is None else i] % 3}_read"

        def before(kind, n=1):
            past = [i for i in steps_of[kind] if i < S.at]
            return past[-n] if len(past) >= n else None

        block = ctx.enter_context(nc.Block())

        @block.sync
        def _(sp):
            loaded = [0]

            def load_chunk():
                c = loaded[0]
                if c >= len(chunks):
                    return
                loaded[0] += 1
                first, last, view, k, cols = chunks[c]
                if c >= RING:
                    sp.wait_ge(S.sem("projected"), S.count("projected", chunks[c - RING][1]))
                dst = ring[:, c % RING, 0:k * cols].rearrange("p (k n) -> p k n", k=k)
                sp.dma_start(dst, view).then_inc(S.sem(f"ring{c % RING}_loaded"), 16)

            def x_in(l, t):
                if t:
                    return
                sp.dma_start(CN[:, 0:128], A["const_table"][:, 0:128]).then_inc(S.sem("ident_loaded"), 16)
                sp.dma_start(XN[:, 0, :], A["x_prompt"][0, 0:128, :]).then_inc(S.sem("x_loaded"), 16)
                sp.dma_start(XN[:, 1, :], A["x_prompt"][0, 128:256, :]).then_inc(S.sem("x_loaded"), 16)
                sp.dma_start(XN[0:32, 2, :], A["x_sample"].rearrange("s t d -> (s t) d")).then_inc(S.sem("x_loaded"), 16)
                sp.dma_start(PTAB[:, :], A["page_table"].rearrange("s n -> (s n)")
                                  .rearrange("(o n) -> o n", o=1)).then_inc(S.sem("pages_loaded"), 16)
                sp.dma_start(CN[:, 128:], A["const_table"][:, 128:]).then_inc(S.sem("consts_loaded"), 16)

            def params_load(l):
                if l:
                    sp.wait_ge(S.sem("param_t"), S.count("param_t"))
                    sp.wait_ge(S.sem("a_g"), S.count("a_g"))
                    sp.wait_ge(S.sem("c_sdone"), S.count("c_sdone"))
                for name, k in PROWS:
                    r = PAT[name]
                    if name in ("qn_c", "kn_c"):
                        for half in range(2):
                            sp.dma_start(PRN[r:r + 1, 0, 64 * half:64 * half + 64], A[name][l:l + 1, :]).then_inc(S.sem("param_rows_loaded"), 16)
                    else:
                        src = A[name][l].rearrange("h n -> (h n)") if name == "rk_b" else A[name][l]
                        sp.dma_start(PRN[r:r + k, 0, :], src.rearrange("(k n) -> k n", n=128)).then_inc(S.sem("param_rows_loaded"), 16)
                sp.dma_start(PRN[0:48, 1, :], A["conv_a"][l].rearrange("j (m n) -> (j m) n", n=128)).then_inc(S.sem("param_rows_loaded"), 16)
                sp.dma_start(HP[:, 0:1], A["dt_bias"][l].rearrange("(h o) -> h o", o=1)).then_inc(S.sem("heads_loaded"), 16)
                sp.dma_start(HP[:, 1:2], A["a_log"][l].rearrange("(h o) -> h o", o=1)).then_inc(S.sem("heads_loaded"), 16)
                for t, (a, n) in enumerate(TILES):
                    src = A["p_prompt"][l, 0, a:a + n, :] if t < 2 else A["p_sample"][l].rearrange("s t d -> (s t) d")
                    sp.dma_start(PLN[0:n, t, :], src).then_inc(S.sem("ple_rows_loaded"), 16)
                if l == 0:
                    for _ in range(RING):
                        load_chunk()

            def a_hist(l):
                sp.wait_ge(S.sem("corrected"), S.count("corrected"))
                sp.wait_ge(S.sem("tail_rows_stored"), S.count("tail_rows_stored", S.at - 1))
                sp.dma_start(ROWS[0:24, 0:QKV_A], A["state_dn_conv"][l].rearrange("s c n -> (s c) n")).then_inc(S.sem("hist_loaded"), 16)

            def a_conv(l, c):
                if c:
                    return
                if l:
                    sp.wait_ge(S.sem("x_next"), S.count("x_next", S.at - 1))
                sp.wait_ge(S.sem("x_t"), S.count("x_t"))
                for h in range(4):
                    sp.dma_start(SD[:, h, :, :], A["state_dn"][l, :, h].rearrange("s k v -> k s v")).then_inc(S.sem("dn_state_loaded"), 16)

            def b_hist(l):
                sp.wait_ge(S.sem("tail_rows_stored"), S.count("tail_rows_stored"))
                sp.wait_ge(S.sem("corrected"), S.count("corrected"))
                sp.dma_start(ROWS[0:8, :], A["state_rwkv_shift"][l]).then_inc(S.sem("hist_loaded"), 16)
                sp.wait_ge(S.sem("tri_up"), S.count("tri_up"))
                for half, name in enumerate(("w2_b", "a2_b")):
                    sp.dma_start(WLO[64 * half:64 * half + 64, :], A[name][l]).then_inc(S.sem("lora_loaded"), 16)

            def b_scale(l, g, t):
                if t != 0:
                    return
                if g == 0:
                    sp.wait_ge(S.sem("b_cleared"), S.count("b_cleared"))
                else:
                    sp.wait_ge(S.sem("states_stored"), S.count("states_stored"))
                for pr in range(2):
                    for hh in range(2):
                        r = slice(64 * hh, 64 * hh + 64)
                        sp.dma_start(BSB[r, pr, :, r],
                                          A["state_rwkv"][l, :, 4 * g + 2 * pr + hh].rearrange("s v k -> v s k")).then_inc(S.sem("rw_state_loaded"), 16)

            def fetch(cache, l, s, dst, name):
                for pg in range(2):
                    r = sp.value_load(PTAB[0:1, 2 * s + pg:2 * s + pg + 1], min_val=0,
                                      max_val=A["cache_k"].shape[1] - 1)
                    src = cache[l, bass.ds(r, 1), :, :, :].rearrange("o p h d -> (o p) (h d)")
                    sp.dma_start(dst[:, pg, :], src).then_inc(S.sem(name), 16)

            def c_fetch_k(l, s):
                if s == 0:
                    sp.wait_ge(S.sem("pages_loaded"), S.count("pages_loaded"))
                    sp.wait_ge(S.sem("b_done"), S.count("b_done"))
                    sp.wait_ge(S.sem("b_snew"), S.count("b_snew"))
                    sp.wait_ge(S.sem("states_stored"), S.count("states_stored"))
                if s >= 2:
                    sp.wait_ge(S.sem("past_k_t"), S.count("past_k_t"))
                fetch(A["cache_k"], l, s, CKR[:, s % 2], f"past_k{s % 2}_loaded")

            def c_fetch_v(l, s):
                if s >= 4:
                    sp.wait_ge(S.sem("c_so"), S.count("c_so"))
                fetch(A["cache_v"], l, s, CVR[:, s % 4], f"past_v{s // 4}_loaded")

            do = dict(x_in=x_in, params_load=params_load, a_hist=a_hist, a_conv=a_conv, b_hist=b_hist, b_scale=b_scale,
                      c_fetch_k=c_fetch_k, c_fetch_v=c_fetch_v)
            for i, st in enumerate(order):
                S.at = i
                if st[0] in do:
                    do[st[0]](*st[1:])
                if i in use and chunks[use[i][0]][1] == i:
                    load_chunk()

        @block.tensor
        def _(pe):
            mm = pe.matmul

            def tr(out, in_, w=128):
                return pe.transpose(out, in_, ident[0:w, 0:w])

            def x_in(l, t):
                w = wid(t)
                if t == 0:
                    pe.wait_ge(S.sem("ident_loaded"), S.count("ident_loaded"))
                    pe.wait_ge(S.sem("x_loaded"), S.count("x_loaded"))
                if t == 2:
                    pe.wait_ge(S.sem("x_t"), S.count("x_t", S.at - 2))
                for k in range(8):
                    ins = tr(M[2 * (t % 2) + k // 4][:, (k % 4) * w:(k % 4) * w + w], XN[0:w, t, 128 * k:128 * k + 128], w)
                ins.then_inc(S.sem("x_tr"), 1)

            def params_t(l):
                pe.wait_ge(S.sem("consts_loaded"), S.count("consts_loaded"))
                pe.wait_ge(S.sem("param_rows_loaded"), S.count("param_rows_loaded"))
                pe.wait_ge(S.sem("ple_rows_loaded"), S.count("ple_rows_loaded"))
                pe.wait_ge(S.sem("x_t"), S.count("x_t", S.at - 1))
                if l:
                    pe.wait_ge(S.sem("c_sdone"), S.count("c_sdone", S.at - 1))
                tr(M[0][:, 0:NP1], PRN[0:NP1, 0, :], NP1)
                tr(M[0][:, NP1:NPAR], PRN[0:48, 1, :], 48)
                for t in range(3):
                    for k in range(2):
                        ins = tr(M[1 + k][:, tok(t)], PLN[0:wid(t), t, 128 * k:128 * k + 128], wid(t))
                ins.then_inc(S.sem("param_t"), 1)

            def norm(l):
                pe.wait_ge(S.sem("squares"), S.count("squares") - 1)
                pe.wait_ge(S.sem("param_done"), S.count("param_done"))
                for k in range(8):
                    if k == 7:
                        pe.wait_ge(S.sem("squares"), S.count("squares"))
                    ins = mm(M[0][:, 0:NTOK], C("ones"), H(l)[:, k, :], start=k == 0, stop=k == 7)
                ins.then_inc(S.sem("square_sums"), 1)

            def project(k_tiles, rhs, m_cols=128):
                c, col = use[S.at]
                n = proj_no[S.at]
                cols = chunks[c][4]
                pe.wait_ge(S.sem(f"ring{c % RING}_loaded"), 16 * (c // RING + 1))
                if n >= 3:
                    pe.wait_ge(S.sem(freed()), S.count(freed(), proj_at[n - 3]))
                for k in range(k_tiles):
                    if order[S.at][0] == "p_a":
                        pe.wait_ge(S.sem("h_ready"), S.count("h_ready") - (KT_ - 1) + k)
                    lhs = ring[:, c % RING, k * cols + col:k * cols + col + m_cols]
                    ins = mm(bank()[0:m_cols, 0:NTOK], lhs, rhs(k), start=k == 0, stop=k == k_tiles - 1)
                return ins

            def p_h(l, *m):
                project(KT_, lambda k: H(l)[:, k, :]).then_inc(S.sem("projected"), 1)

            def p_ba(l):
                c, _ = use[S.at]
                pe.wait_ge(S.sem("h_ready"), S.count("h_ready"))
                project(KT_, lambda k: H(l)[:, k, :], 4)
                pe.wait_ge(S.sem("b_done"), S.count("b_done"))
                pe.wait_ge(S.sem("c_spts"), S.count("c_spts"))
                for k in range(KT_):
                    ins = mm(M[4][0:4, 0:NTOK], ring[:, c % RING, k * 8 + 4:k * 8 + 8], H(l)[:, k, :],
                             start=k == 0, stop=k == KT_ - 1)
                ins.then_inc(S.sem("projected"), 1)

            def p_up(l, n, m):
                if n == 0:
                    pe.wait_ge(S.sem("a_done"), S.count("a_done"))
                elif n == 1:
                    pe.wait_ge(S.sem("b_done"), S.count("b_done"))
                else:
                    pe.wait_ge(S.sem("c_done"), S.count("c_done"))
                    pe.wait_ge(S.sem("c_sdone"), S.count("c_sdone"))
                project(4, lambda k: Z[:, n, k, :]).then_inc(S.sem("projected"), 1)

            def p_y(l, m):
                pe.wait_ge(S.sem("merged"), S.count("merged"))
                project(8, lambda k: MG[:, k, :]).then_inc(S.sem("projected"), 1)

            def p_pg(l, m):
                for b in range(3):
                    pe.wait_ge(S.sem(f"bank{b}_read"), S.count(f"bank{b}_read", before("p_y")))
                project(8, lambda k: X(l)[:, k, :]).then_inc(S.sem("projected"), 1)

            def p_ple(l, m):
                project(2, lambda k: PLT[:, k, :]).then_inc(S.sem("projected"), 1)

            def a_hist(l):
                pe.wait_ge(S.sem("hist_loaded"), S.count("hist_loaded"))
                pe.wait_ge(S.sem("inv_roots"), S.count("inv_roots"))
                for m in range(NA):
                    ins = tr(M[0][:, 24 * m:24 * m + 24], ROWS[0:24, 128 * m:128 * m + 128], 24)
                ins.then_inc(S.sem("hist_t"), 1)

            def a_convout(l):
                pe.wait_ge(S.sem("tails"), S.count("tails"))
                for m in range(NA):
                    ins = tr(M[1 + m // 4][0:27, (m % 4) * 128:(m % 4) * 128 + 128], CT[:, 27 * m:27 * m + 27])
                ins.then_inc(S.sem("tails_t"), 1)

            def ones4(src, weights, name):
                for h in range(4):
                    ins = mm(M[h][:, 0:NTOK], weights, src[:, h, :], start=True, stop=True)
                ins.then_inc(S.sem(name), 1)

            def a_l2(l, i):
                pe.wait_ge(S.sem("squares"), S.count("squares"))
                pe.wait_ge(S.sem("tail_rows"), S.count("tail_rows"))
                ones4(TMP, C("ones"), "square_sums")

            def a_rows(l):
                pe.wait_ge(S.sem("a_g"), S.count("a_g"))
                for t in range(3):
                    ins = tr(M[4][0:wid(t), 4 * t:4 * t + 4], ABG[0:4, 1, tok(t)], 4)
                ins.then_inc(S.sem("a_gcol_t"), 1)

            def a_scale(l, t):
                w = wid(t)
                pe.wait_ge(S.sem("a_unit"), S.count("a_unit"))
                pe.wait_ge(S.sem("a_state"), S.count("a_state"))
                pe.wait_ge(S.sem("a_nat"), S.count("a_nat"))
                for i in range(2):
                    for h in range(4):
                        ins = mm(v4(M[i], w)[:, h, :], C("pick_head", 4)[:, 128 * h:128 * h + 128],
                                 ABG[0:4, 1 - i, tok(t)], start=True, stop=True)
                ins.then_inc(S.sem("a_gb"), 1)

            def a_pairs(l, t):
                w = wid(t)
                pe.wait_ge(S.sem("a_scaled"), S.count("a_scaled"))
                for h in range(4):
                    ins = mm(v4(M[2], w, w)[:, h, :], UC[:, 4 + h, tok(t)], AKB[:, h, 0:w], start=True, stop=True)
                ins.then_inc(S.sem("a_kk0"), 1)
                for h in range(4):
                    mm(v4(M[3], w, w)[:, h, :], UC[:, 4 + h, tok(t)], UC[:, h, tok(t)], start=True, stop=True)
                for h in range(4):
                    tr(v4(M[4], 128, w)[:, h, :], AVB[:, h, 0:w])
                for h in range(4):
                    ins = tr(v4(M[0], 128, w)[:, h, :], AKD[:, h, 0:w])
                ins.then_inc(S.sem("a_kk"), 1)

            def tri(l, t):
                w = wid(t)
                pe.wait_ge(S.sem("tri_t0"), S.count("tri_t0"))
                pe.wait_ge(S.sem("a_nat"), S.count("a_nat"))
                pe.wait_ge(S.sem("b_vs"), S.count("b_vs"))
                for h in range(4):
                    ins = tr(v4(M[0], w, w)[:, h, :], TT[0:w, h, 0:w], w)
                ins.then_inc(S.sem("tri_tr"), 1)

            def lev(l, t, k):
                w, n = wid(t), level_width(t, k)
                pe.wait_ge(S.sem("tri_lm"), S.count("tri_lm", S.at - 1))
                pe.wait_ge(S.sem("tri_i0"), S.count("tri_i0"))
                pe.wait_ge(S.sem("tri_iup"), S.count("tri_iup", S.at - 1))
                if k == 1:
                    pe.wait_ge(S.sem("a_lt"), S.count("a_lt"))
                    pe.wait_ge(S.sem("b_masked"), S.count("b_masked"))
                for h in range(4):
                    ins = mm(v4(M[h // 2], w, w)[:, h, 0:n], LM[0:w, h, 0:w], TI[0:w, h, 0:n], start=True, stop=True)
                    if h % 2:
                        ins.then_inc(S.sem("tri_y"), 1)
                pe.wait_ge(S.sem("tri_up"), S.count("tri_up", S.at - 1))
                pe.wait_ge(S.sem("tri_ys"), S.count("tri_ys") - 1)
                if k < last_level(t):
                    for h in range(4):
                        if h == 2:
                            pe.wait_ge(S.sem("tri_ys"), S.count("tri_ys"))
                        ins = mm(v4(M[2], w, w)[:, h, :], TT[0:w, h, 0:w], Y[0:w, h, 0:w], start=True, stop=True)
                    ins.then_inc(S.sem("tri_z"), 1)
                for h in range(4):
                    if h == 2:
                        pe.wait_ge(S.sem("tri_ys"), S.count("tri_ys"))
                    ins = mm(v4(M[3], w, n)[:, h, w - n:w], Y[0:w, h, 0:n], TT[0:w, h, w - n:w], start=True, stop=True)
                ins.then_inc(S.sem("tri_zt"), 1)

            def a_s0(l, h):
                pe.wait_ge(S.sem("dn_state_loaded"), S.count("dn_state_loaded"))
                pe.wait_ge(S.sem("tri_up"), S.count("tri_up"))
                if h >= 2:
                    pe.wait_ge(S.sem("start_reduced"), S.count("start_reduced", S.at - 2))
                b = 2 * (h % 2)
                for c in range(2):
                    ins = mm(M[b + c][0:64, :], AKQ[:, 64 * h:64 * h + 64], SD[:, h, 4 * c:4 * c + 4, :],
                             start=True, stop=True)
                ins.then_inc(S.sem("start_read"), 1)

            def a_w(l, t):
                if t == 1:
                    pe.wait_ge(S.sem("a_done"), S.count("a_done"))
                    for h in range(4):
                        ins = mm(v4(M[4], 128)[:, h, :], vx(AKQ, 4, 128)[:, h, 0, :], AST[:, h, :], start=True, stop=True)
                    ins.then_inc(S.sem("a_ks"), 1)

            def a_u(l, t):
                w = wid(t)
                pe.wait_ge(S.sem("tri_up"), S.count("tri_up"))
                pe.wait_ge(S.sem("a_w" if t else "a_nat"), S.count("a_w" if t else "a_nat"))
                pe.wait_ge(S.sem("start_reduced"), S.count("start_reduced"))
                for h in range(4):
                    rhs = (AW if t else AVN)[0:w, h, :]
                    ins = mm(v4(M[1], 128, w)[:, h, :], TT[0:w, h, 0:w], rhs, start=True, stop=True)
                ins.then_inc(S.sem("corrected"), 1)

            def a_o(l, t):
                w = wid(t)
                if t == 1:
                    for h in range(4):
                        mm(v4(M[2], 128)[:, h, :], vx(AKQ, 4, 128)[:, h, 1, :], AST[:, h, :], start=h == 0, stop=False,
                           skip_group_check=True)
                pe.wait_ge(S.sem("corrected_s"), S.count("corrected_s"))
                for h in range(4):
                    out = v4(M[2], 128, w)[:, h, :]
                    ins = mm(out, AQK[0:w, h, 0:w], AU[0:w, h, :], start=t != 1, stop=True, skip_group_check=True)
                if t == 2:
                    ins.then_inc(S.sem("a_o"), 1)
                    return
                for h in range(4):
                    ins = mm(v4(M[3], 128)[:, h, :], AKN[0:w, h, :], AU[0:w, h, :], start=True, stop=True)
                ins.then_inc(S.sem("a_o"), 1)

            def a_norm5(l, t):
                w = wid(t)
                pe.wait_ge(S.sem("a_nat"), S.count("a_nat"))
                pe.wait_ge(S.sem("out_normed"), S.count("out_normed"))
                for h in range(4):
                    ins = tr(v4(M[4], w)[:, h, :], AW[0:w, h, :], w)
                ins.then_inc(S.sem("out_t"), 1)

            def a_sout(l, h):
                pe.wait_ge(S.sem("a_uex"), S.count("a_uex"))
                b = 2 * (h % 2)
                for c in range(2):
                    ins = mm(M[b + c], AKN[0:32, h, :], AEX[0:32, 4 * c:4 * c + 4, :], start=True, stop=True)
                ins.then_inc(S.sem("a_dst"), 1)

            def b_hist(l):
                pe.wait_ge(S.sem("hist_loaded"), S.count("hist_loaded"))
                pe.wait_ge(S.sem("a_sst"), S.count("a_sst"))
                for m in range(NF):
                    ins = tr(M[0][:, 8 * m:8 * m + 8], ROWS[0:8, 128 * m:128 * m + 128], 8)
                ins.then_inc(S.sem("hist_t"), 1)

            def b_shiftout(l):
                pe.wait_ge(S.sem("tails"), S.count("tails"))
                pe.wait_ge(S.sem("hist_in"), S.count("hist_in"))
                for m in range(NF):
                    ins = tr(M[m // 4][0:9, (m % 4) * 128:(m % 4) * 128 + 128], CT[:, 9 * m:9 * m + 9])
                ins.then_inc(S.sem("tails_t"), 1)

            def b_lora(l):
                pe.wait_ge(S.sem("lora_loaded"), S.count("lora_loaded"))
                pe.wait_ge(S.sem("b_lt"), S.count("b_lt"))
                for h in range(4):
                    ins = mm(M[h][:, 0:NTOK], WLO[0:64, 128 * h:128 * h + 128], FM[0:64, NF - 1, :], start=True, stop=True)
                ins.then_inc(S.sem("b_wraw"), 1)
                pe.wait_ge(S.sem("b_wt"), S.count("b_wt"))
                for h in range(4):
                    ins = mm(M[h][:, 0:NTOK], WLO[64:128, 128 * h:128 * h + 128], FM[64:128, NF - 1, :], start=True, stop=True)
                ins.then_inc(S.sem("b_araw"), 1)

            def b_kk(l):
                pe.wait_ge(S.sem("squares"), S.count("squares"))
                ones4(TMP, C("ones_head"), "square_sums")

            def b_bonus(l):
                pe.wait_ge(S.sem("b_rkm"), S.count("b_rkm"))
                ones4(TMP, C("ones_head"), "square_sums")

            def b_pairs(l, g, t):
                w = wid(t)
                pe.wait_ge(S.sem("b_scaled"), S.count("b_scaled"))
                pe.wait_ge(S.sem("b_vs"), S.count("b_vs"))
                ar, bk = vx(BAR, 2, w), vx(BBK, 2, w)
                for x in range(2):
                    for hd in range(4):
                        pr, r = hd // 2, slice(64 * (hd % 2), 64 * (hd % 2) + 64)
                        out = M[2 * x + hd % 2][0:w, 2 * w * pr:2 * w * pr + 2 * w]
                        ins = mm(out, bk[r, pr, x, :], BAR[r, 2 * w * pr:2 * w * pr + 2 * w], start=True, stop=True)
                    if x == 0:
                        ins.then_inc(S.sem("b_m0"), 1)
                for pr in range(2):
                    for x in range(2):
                        ins = tr(M[4][0:w, (2 * pr + x) * 128:(2 * pr + x) * 128 + 128], bk[:, pr, x, :])
                ins.then_inc(S.sem("b_m"), 1)

            def b_nat(l, g, t):
                w = wid(t)
                pe.wait_ge(S.sem("b_masked"), S.count("b_masked"))
                pe.wait_ge(S.sem("corrected_s"), S.count("corrected_s"))
                pe.wait_ge(S.sem("b_snew"), S.count("b_snew"))
                pe.wait_ge(S.sem("b_bonus_done"), S.count("b_bonus_done"))
                for pr in range(2):
                    ins = tr(M[1][0:w, 128 * pr:128 * pr + 128], FM[:, 8 + 2 * g + pr, tok(t)])
                ins.then_inc(S.sem("b_vt"), 1)

            def b_st(l, g, pr):
                pe.wait_ge(S.sem("rw_state_loaded"), S.count("rw_state_loaded"))
                pe.wait_ge(S.sem("tri_up"), S.count("tri_up"))
                pe.wait_ge(S.sem("start_reduced"), S.count("start_reduced", S.at - 1))
                for s in range(NSEQ):
                    ins = tr(M[s // 4][:, (s % 4) * 128:(s % 4) * 128 + 128], BSB[:, pr, s, :])
                ins.then_inc(S.sem("b_s_t"), 1)

            def b_s0(l, g, pr):
                pe.wait_ge(S.sem("b_s_ts"), S.count("b_s_ts"))
                for c in range(2):
                    ins = mm(M[2 + c][0:64, :], BAR[:, 64 * pr:64 * pr + 64], BX[:, 0, 4 * c:4 * c + 4, :], start=True, stop=True)
                ins.then_inc(S.sem("start_read"), 1)

            def b_w(l, g, t):
                w = wid(t)
                pe.wait_ge(S.sem("b_vs"), S.count("b_vs"))
                pe.wait_ge(S.sem("b_masked"), S.count("b_masked"))
                pe.wait_ge(S.sem("b_done"), S.count("b_done"))
                for hd in range(4):
                    pr, hh = hd // 2, hd % 2
                    if t == 1 and hh == 0:
                        mm(M[4][:, 128 * pr:128 * pr + 128], vx(BAR, 2, w)[:, pr, 0, :], BST[:, pr, :], start=True, stop=False,
                           skip_group_check=True)
                    ins = mm(M[4][0:w, 64 * hd:64 * hd + 64], vx(BKK, 4, w, w)[:, hd, 0, :],
                             BVN[0:w, pr, 64 * hh:64 * hh + 64], start=t != 1, stop=True, skip_group_check=True)
                ins.then_inc(S.sem("b_wp"), 1)

            def b_u(l, g, t):
                w = wid(t)
                pe.wait_ge(S.sem("b_ws"), S.count("b_ws"))
                pe.wait_ge(S.sem("tri_up"), S.count("tri_up"))
                for hd in range(4):
                    pr, hh = hd // 2, hd % 2
                    ins = mm(M[1][0:w, 64 * hd:64 * hd + 64], TT[0:w, hd, 0:w], BW[0:w, pr, 64 * hh:64 * hh + 64],
                             start=True, stop=True)
                ins.then_inc(S.sem("corrected"), 1)

            def b_y(l, g, t):
                w = wid(t)
                for hd in range(4):
                    pr, hh = hd // 2, hd % 2
                    cols = slice(64 * hh, 64 * hh + 64)
                    out = M[2][0:w, 64 * hd:64 * hd + 64]
                    if t == 1 and hh == 0:
                        mm(M[2][:, 128 * pr:128 * pr + 128], vx(BAR, 2, w)[:, pr, 1, :], BST[:, pr, :], start=pr == 0, stop=False,
                           skip_group_check=True)
                    mm(out, vx(BKK, 4, w, w)[:, hd, 1, :], BVN[0:w, pr, cols], start=t != 1 and hd == 0, stop=False,
                       skip_group_check=True)
                if t < 2:
                    for pr in range(2):
                        mm(M[3][:, 128 * pr:128 * pr + 128], BN[0:w, pr, 1, :], BVN[0:w, pr, :], start=pr == 0, stop=False,
                           skip_group_check=True)
                pe.wait_ge(S.sem("corrected_s"), S.count("corrected_s"))
                for hd in range(4):
                    pr, hh = hd // 2, hd % 2
                    ins = mm(M[2][0:w, 64 * hd:64 * hd + 64], BRB[0:w, hd, 0:w], BU[0:w, pr, 64 * hh:64 * hh + 64],
                             start=False, stop=True, skip_group_check=True)
                if t < 2:
                    for pr in range(2):
                        ins = mm(M[3][:, 128 * pr:128 * pr + 128], BN[0:w, pr, 0, :], BU[0:w, pr, :], start=False,
                                 stop=True, skip_group_check=True)
                ins.then_inc(S.sem("b_y"), 1)

            def b_fin(l, g):
                pe.wait_ge(S.sem("b_state"), S.count("b_state"))
                pe.wait_ge(S.sem("b_done"), S.count("b_done"))
                for pr in range(2):
                    ins = tr(M[4][:, 128 * pr:128 * pr + 128], BST[:, pr, :])
                ins.then_inc(S.sem("b_fin_t"), 1)

            def b_norm5(l, g, t):
                w = wid(t)
                pe.wait_ge(S.sem("b_nats"), S.count("b_nats"))
                pe.wait_ge(S.sem("b_snew"), S.count("b_snew"))
                pe.wait_ge(S.sem("out_normed"), S.count("out_normed"))
                for pr in range(2):
                    ins = tr(M[4][:, w * pr:w * pr + w], BY[0:w, pr, :], w)
                ins.then_inc(S.sem("out_t"), 1)

            def b_sout(l, g, pr):
                pe.wait_ge(S.sem("b_bex"), S.count("b_bex"))
                pe.wait_ge(S.sem("b_ys"), S.count("b_ys"))
                for c in range(2):
                    for src, x in ((BU, 0), (BVN, 1)):
                        mm(M[c], src[0:32, pr, :], BX[0:32, x, 4 * c:4 * c + 4, :], start=x == 0, stop=x == 1)
                ins = tr(M[2][0:8, 0:128], BM[:, 2 * g + pr, 4:12])
                ins.then_inc(S.sem("b_ds"), 1)

            def b_sdec(l, g, pr):
                pe.wait_ge(S.sem("b_pcx"), S.count("b_pcx"))
                pe.wait_ge(S.sem("b_fin_s"), S.count("b_fin_s"))
                for c in range(2):
                    ins = mm(M[3 + c], C("ones", 8), BX[0:8, 1, 4 * c:4 * c + 4, :], start=True, stop=True)
                ins.then_inc(S.sem("b_pcb"), 1)

            def c_rms(l, i):
                pe.wait_ge(S.sem("squares"), S.count("squares"))
                pe.wait_ge(S.sem("b_snew"), S.count("b_snew"))
                pe.wait_ge(S.sem("inv_roots"), S.count("inv_roots", S.at - 1))
                ones4(SQ[i], C("ones_head"), "square_sums")

            def c_rope(l, i):
                pe.wait_ge(S.sem("inv_roots"), S.count("inv_roots"))
                pe.wait_ge(S.sem("c_rope"), S.count("c_rope", S.at - 1))
                pe.wait_ge(S.sem("c_n"), S.count("c_n"))
                for h in range(4):
                    ins = mm(M[h][:, 0:NTOK], C("swap"), QC[:, 4 * i + h, :], start=True, stop=True)
                ins.then_inc(S.sem("c_sw"), 1)

            def c_nat(l, i):
                pe.wait_ge(S.sem("c_rope"), S.count("c_rope"))
                if i == 0:
                    for b in range(3):
                        pe.wait_ge(S.sem(f"bank{b}_read"), S.count(f"bank{b}_read"))
                else:
                    pe.wait_ge(S.sem("c_ns"), S.count("c_ns", S.at - 1))
                for t in range(3):
                    w = wid(t)
                    for m in range(4):
                        ins = tr(M[t][0:w, 128 * m:128 * m + 128], QC[:, 4 + 4 * i + m, tok(t)])
                ins.then_inc(S.sem("c_nt"), 1)

            def c_score(l, t, g):
                if t == 0 and g == 0:
                    pe.wait_ge(S.sem("c_ns"), S.count("c_ns"))
                    pe.wait_ge(S.sem("c_sdone"), S.count("c_sdone"))
                pe.wait_ge(S.sem("c_max"), S.count("c_max", S.at - 1))
                for hd in range(4):
                    pair, r = 2 * g + hd // 2, slice(64 * (hd % 2), 64 * (hd % 2) + 64)
                    n = 128 * (t + 1)
                    out = M[hd % 2][:, n * (hd // 2):n * (hd // 2) + n]
                    ins = mm(out, QC[r, pair, tok(t)], QC[r, 4 + pair, 0:n], start=True, stop=True)
                ins.then_inc(S.sem("c_s"), 1)

            def c_prob(l, t, g):
                pe.wait_ge(S.sem("c_e"), S.count("c_e"))
                pe.wait_ge(S.sem("c_done"), S.count("c_done"))
                for st in range(t + 1):
                    for hd in range(4):
                        ins = tr(M[2 + st][:, 128 * hd:128 * hd + 128], CP[:, hd, 128 * st:128 * st + 128])
                ins.then_inc(S.sem("c_pt"), 1)

            def c_pv(l, t, g):
                pe.wait_ge(S.sem("c_pts"), S.count("c_pts"))
                pe.wait_ge(S.sem("c_os"), S.count("c_os", S.at - 1))
                for hd in range(4):
                    for st in range(t + 1):
                        ins = mm(M[4][:, 64 * hd:64 * hd + 64], CPT[:, st, hd, :], CVN[:, st, 64 * (4 * g + hd):64 * (4 * g + hd) + 64],
                                 start=st == 0, stop=st == t)
                ins.then_inc(S.sem("c_o"), 1)

            def c_out(l, t):
                pe.wait_ge(S.sem("c_os"), S.count("c_os"))
                for m in range(4):
                    ins = tr(M[2][:, 128 * m:128 * m + 128], CON[:, 128 * m:128 * m + 128])
                ins.then_inc(S.sem("c_ot"), 1)

            def c_keys(l, g, j):
                s = 4 * g + j
                pe.wait_ge(S.sem(f"past_k{s % 2}_loaded"), S.count(f"past_k{s % 2}_loaded"))
                pe.wait_ge(S.sem("past_k_ts"), S.count("past_k_ts", S.at - 1) - (j > 0))
                pe.wait_ge(S.sem("c_ns"), S.count("c_ns"))
                pe.wait_ge(S.sem("c_qx"), S.count("c_qx"))
                pe.wait_ge(S.sem("c_done"), S.count("c_done"))
                pe.wait_ge(S.sem("c_sdone"), S.count("c_sdone", S.at - 1))
                pe.wait_ge(S.sem("c_max"), S.count("c_max", S.at - 1))
                for pg in range(2):
                    for pr in range(4):
                        ins = tr(M[3 * (s % 2) + pg][:, 128 * pr:128 * pr + 128], CKR[:, s % 2, pg, 128 * pr:128 * pr + 128])
                ins.then_inc(S.sem("past_k_t"), 1)

            def c_past(l, g, j):
                s = 4 * g + j
                pe.wait_ge(S.sem("past_k_ts"), S.count("past_k_ts") - (j < 3))
                rows = slice(32 * j, 32 * j + 32)
                for pr in range(4):
                    mm(M[2][rows, 0:256], CQX[:, pr, s, :], CKT[:, s % 2, pr, :], start=pr == 0, stop=pr == 3,
                       skip_group_check=True)
                for pr in range(4):
                    ins = mm(M[2][rows, 256:288], CQX[:, pr, s, :], QC[:, 4 + pr, SEQ:NTOK], start=pr == 0, stop=pr == 3,
                             skip_group_check=True)
                ins.then_inc(S.sem("c_ssc"), 1)

            def c_sprob(l, g):
                pe.wait_ge(S.sem("c_sp"), S.count("c_sp"))
                for st in range(3):
                    n = 128 if st < 2 else 32
                    ins = tr(M[4][0:n, 128 * st:128 * st + 128], CPS[:, 128 * st:128 * st + n])
                ins.then_inc(S.sem("c_spt"), 1)

            def c_spv(l, g):
                pe.wait_ge(S.sem("c_spts"), S.count("c_spts"))
                pe.wait_ge(S.sem(f"past_v{g}_loaded"), S.count(f"past_v{g}_loaded"))
                for j in range(4):
                    for pr in range(4):
                        out = M[0][:, (4 * j + pr) * 8:(4 * j + pr) * 8 + 8]
                        cols = slice(32 * j + 8 * pr, 32 * j + 8 * pr + 8)
                        for pg in range(2):
                            mm(out, CVR[:, j, pg, 128 * pr:128 * pr + 128], CPTS[:, pg, cols], start=pg == 0, stop=False)
                        ins = mm(out, CVN[0:32, 2, 128 * pr:128 * pr + 128], CPTS[0:32, 2, cols], start=False, stop=True)
                ins.then_inc(S.sem("c_so"), 1)

            def finish(l, t):
                w = wid(t)
                pe.wait_ge(S.sem("x_next"), S.count("x_next"))
                if t == 2:
                    pe.wait_ge(S.sem("y_rows"), S.count("y_rows", S.at - 2))
                for k in range(8):
                    ins = tr(M[2 * (t % 2) + k // 4][0:w, (k % 4) * 128:(k % 4) * 128 + 128], X(l)[:, k, tok(t)])
                ins.then_inc(S.sem("y_t"), 1)

            do = dict(x_in=x_in, params_t=params_t, norm=norm, p_a=p_h, p_f=p_h, p_c=p_h, p_g=p_h, p_z=p_h, p_ba=p_ba,
                      p_up=p_up, p_y=p_y, p_pg=p_pg, p_ple=p_ple, a_hist=a_hist, a_convout=a_convout, a_l2=a_l2,
                      a_rows=a_rows, a_scale=a_scale, a_pairs=a_pairs, tri=tri, lev=lev, a_s0=a_s0, a_w=a_w, a_u=a_u,
                      a_o=a_o, a_norm5=a_norm5, a_sout=a_sout, b_hist=b_hist, b_shiftout=b_shiftout, b_lora=b_lora,
                      b_kk=b_kk, b_bonus=b_bonus, b_pairs=b_pairs, b_nat=b_nat, b_st=b_st, b_s0=b_s0, b_w=b_w, b_u=b_u, b_y=b_y,
                      b_fin=b_fin, b_norm5=b_norm5, b_sout=b_sout, b_sdec=b_sdec, c_rms=c_rms, c_rope=c_rope, c_nat=c_nat, c_score=c_score,
                      c_prob=c_prob, c_pv=c_pv, c_out=c_out, c_keys=c_keys, c_past=c_past, c_sprob=c_sprob, c_spv=c_spv, finish=finish)
            for i, st in enumerate(order):
                S.at = i
                if st[0] in do:
                    do[st[0]](*st[1:])

        @block.scalar
        def _(act):
            own = [0]

            def link(ins):
                own[0] += 1
                ins.then_inc(S.sem("act_link"), 1)
                act.wait_ge(S.sem("act_link"), own[0])

            fn = act.activation

            def params(l):
                act.wait_ge(S.sem("heads_loaded"), S.count("heads_loaded"))
                fn(HP[:, 2:3], HP[:, 1:2], ACT.Exp).then_inc(S.sem("decay_rate"), 1)
                act.wait_ge(S.sem("decay_rate"), S.count("decay_rate"))

            def norm(l):
                if l == 0:
                    act.wait_ge(S.sem("x_t"), S.count("x_t"))
                else:
                    act.wait_ge(S.sem("x_next"), S.count("x_next") - 1)
                fn(H(l)[:, 0:7, :], X(l)[:, 0:7, :], ACT.Square).then_inc(S.sem("squares"), 1)
                if l:
                    act.wait_ge(S.sem("x_next"), S.count("x_next"))
                fn(H(l)[:, 7, :], X(l)[:, 7, :], ACT.Square).then_inc(S.sem("squares"), 1)
                act.wait_ge(S.sem("param_done"), S.count("param_done"))
                act.wait_ge(S.sem("squares"), S.count("squares"))
                act.wait_ge(S.sem("square_sums"), S.count("square_sums"))
                link(fn(TMP[:, 0, :], M[0][:, 0:NTOK], ACT.Ln, bias=C("c_eps"), scale=1.0 / D_MODEL))
                fn(TMP[:, 1, :], TMP[:, 0, :], ACT.Exp, scale=-0.5).then_inc(S.sem("inv_roots"), 1)
                act.wait_ge(S.sem("inv_roots"), S.count("inv_roots"))

            def p_a(l, m):
                act.wait_ge(S.sem("projected"), S.count("projected"))
                act.wait_ge(S.sem("c_ns"), S.count("c_ns", S.at - 1))
                fn(U[:, m, CONV_W - 1:UW], bank()[:, 0:SEQ], ACT.Copy)
                fn(Us[:, m, :, CONV_W - 1:], seqs(bank()[:, SEQ:NTOK]), ACT.Copy).then_inc(S.sem(freed()), 1)
                act.wait_ge(S.sem(freed()), S.count(freed()))

            def p_f(l, m):
                act.wait_ge(S.sem("projected"), S.count("projected"))
                fn(F[:, m, 1:FW], bank()[:, 0:SEQ], ACT.Copy)
                fn(Fs[:, m, :, 1:], seqs(bank()[:, SEQ:NTOK]), ACT.Copy).then_inc(S.sem(freed()), 1)
                act.wait_ge(S.sem(freed()), S.count(freed()))

            def p_c(l, m):
                act.wait_ge(S.sem("projected"), S.count("projected"))
                act.wait_ge(S.sem("a_conv_p"), S.count("a_conv_p"))
                act.wait_ge(S.sem("a_conv_s"), S.count("a_conv_s"))
                fn(QC[:, m, :], bank()[:, 0:NTOK], ACT.Copy).then_inc(S.sem(freed()), 1)
                act.wait_ge(S.sem(freed()), S.count(freed()))

            def p_z(l, n, m):
                act.wait_ge(S.sem("projected"), S.count("projected"))
                if before("p_z", 2) is not None:
                    act.wait_ge(S.sem(freed(before("p_z", 2))), S.count(freed(before("p_z", 2)), before("p_z", 2)))
                if l and n == 0:
                    for b in range(3):
                        act.wait_ge(S.sem(f"bank{b}_read"), S.count(f"bank{b}_read", before("p_ple")))
                fn(TH[:, m % 2, :], bank()[:, 0:NTOK], ACT.Tanh, scale=0.5).then_inc(S.sem("z_tanh"), 1)
                act.wait_ge(S.sem("z_tanh"), S.count("z_tanh"))

            def p_g(l, m):
                act.wait_ge(S.sem("projected"), S.count("projected"))
                act.wait_ge(S.sem("b_mixed"), S.count("b_mixed"))
                act.wait_ge(S.sem("b_mixed_s"), S.count("b_mixed_s"))
                act.wait_ge(S.sem("tails"), S.count("tails"))
                if m >= NF:
                    act.wait_ge(S.sem("b_done"), S.count("b_done"))
                    act.wait_ge(S.sem("b_snew"), S.count("b_snew"))
                    act.wait_ge(S.sem("states_stored"), S.count("states_stored"))
                if m >= NF + 7:
                    act.wait_ge(S.sem("c_rope"), S.count("c_rope"))
                fn(gate(m), bank()[:, 0:NTOK], ACT.Tanh, scale=0.5, bias=Phalf("b_gate", m)).then_inc(S.sem(freed()), 1)
                act.wait_ge(S.sem(freed()), S.count(freed()))

            def p_pg(l, m):
                act.wait_ge(S.sem("projected"), S.count("projected"))
                if m >= 2:
                    act.wait_ge(S.sem(freed(before("p_ple", 2))), S.count(freed(before("p_ple", 2)), before("p_ple", 2)))
                else:
                    for b in range(3):
                        act.wait_ge(S.sem(f"bank{b}_read"), S.count(f"bank{b}_read", before("p_z")))
                fn(TH[:, m % 2, :], bank()[:, 0:NTOK], ACT.Tanh, scale=0.5, bias=Phalf("b_pg", m)).then_inc(S.sem(freed()), 1)
                act.wait_ge(S.sem(freed()), S.count(freed()))

            def p_ba(l):
                act.wait_ge(S.sem("projected"), S.count("projected"))
                if l:
                    act.wait_ge(S.sem("x_next"), S.count("x_next", S.at - 1))
                fn(ATM[0:4, 0, :], bank()[0:4, 0:NTOK], ACT.Tanh, scale=0.5)
                fn(ATM[0:4, 1, :], M[4][0:4, 0:NTOK], ACT.Identity, bias=HP[:, 0:1]).then_inc(S.sem(freed()), 1)
                act.wait_ge(S.sem(freed()), S.count(freed()))

            def a_convout(l):
                act.wait_ge(S.sem("tails_t"), S.count("tails_t"))
                act.wait_ge(S.sem("tail_rows_stored"), S.count("tail_rows_stored", S.at - 1))
                fn(ROWS[0:27, 0:QKV_A], PS[0:27, 4:7, :].rearrange("p b n -> p (b n)"), ACT.Copy).then_inc(S.sem("tail_rows"), 1)
                act.wait_ge(S.sem("tail_rows"), S.count("tail_rows"))

            def a_silu(l, c):
                act.wait_ge(S.sem("a_conv_p"), S.count("a_conv_p") - (c < 2))
                act.wait_ge(S.sem("a_conv_s"), S.count("a_conv_s"))
                act.wait_ge(S.sem("a_silu"), S.count("a_silu", S.at - 1))
                fn(TMP[:, :, :], UC[:, 4 * c:4 * c + 4, :], ACT.Tanh, scale=0.5).then_inc(S.sem("a_tanh"), 1)
                act.wait_ge(S.sem("a_tanh"), S.count("a_tanh"))

            def inv_root(dst, src, mean, eps, scale_log=None, rows=128):
                link(fn(dst, src, ACT.Ln, bias=C(eps, rows), scale=mean))
                return fn(dst, dst, ACT.Exp, scale=-0.5, bias=C(scale_log or "c_0", rows))

            def a_l2(l, i):
                act.wait_ge(S.sem("a_silu"), S.count("a_silu"))
                act.wait_ge(S.sem("a_unit"), S.count("a_unit", S.at - 1))
                fn(TMP[:, :, :], UC[:, 4 * i:4 * i + 4, :], ACT.Square).then_inc(S.sem("squares"), 1)
                act.wait_ge(S.sem("squares"), S.count("squares"))
                act.wait_ge(S.sem("square_sums"), S.count("square_sums"))
                inv_root(TMP[:, :, :], PS[:, 3:7, 0:NTOK], 1.0, "c_4eps", None if i else "c_lndk").then_inc(S.sem("inv_roots"), 1)
                act.wait_ge(S.sem("inv_roots"), S.count("inv_roots"))

            def a_rows(l):
                act.wait_ge(S.sem("ba_neg"), S.count("ba_neg"))
                link(fn(ATM[0:4, 2, :], ATM[0:4, 2, :], ACT.Exp))
                fn(ATM[0:4, 2, :], ATM[0:4, 2, :], ACT.Ln, bias=C("c_1", 4)).then_inc(S.sem("ba_ln"), 1)
                act.wait_ge(S.sem("ba_ln"), S.count("ba_ln"))

            def a_scale(l, t):
                w = wid(t)
                act.wait_ge(S.sem("a_klast"), S.count("a_klast"))
                fn(AEG[:, :, 0:w], AGB[:, :, 0:w], ACT.Exp)
                fn(ADI[0:w, :, 0:w], ADI[0:w, :, 0:w], ACT.Exp)
                fn(AKD[:, :, 0:w], AKD[:, :, 0:w], ACT.Exp).then_inc(S.sem("a_exps"), 1)
                act.wait_ge(S.sem("a_exps"), S.count("a_exps"))

            def a_pairs(l, t):
                w = wid(t)
                act.wait_ge(S.sem("a_kk"), S.count("a_kk"))
                fn(AVN[0:w, :, :], v4(M[4], 128, w), ACT.Copy)
                fn(AKN[0:w, :, :], v4(M[0], 128, w), ACT.Copy).then_inc(S.sem("a_nat"), 1)
                act.wait_ge(S.sem("a_nat"), S.count("a_nat"))

            def tri(l, t):
                w = wid(t)
                act.wait_ge(S.sem("tri_tr"), S.count("tri_tr"))
                fn(TI[0:w, :, 0:w], v4(M[0], w, w), ACT.Copy).then_inc(S.sem("tri_i0"), 1)
                act.wait_ge(S.sem("tri_i0"), S.count("tri_i0"))

            def lev(l, t, k):
                w, n = wid(t), level_width(t, k)
                for i in range(2):
                    q = slice(2 * i, 2 * i + 2)
                    act.wait_ge(S.sem("tri_y"), S.count("tri_y") - 1 + i)
                    fn(Y[0:w, q, 0:n], v4(M[i], w, w)[:, q, 0:n], ACT.Copy).then_inc(S.sem("tri_ys"), 1)
                act.wait_ge(S.sem("tri_ys"), S.count("tri_ys"))

            def a_u(l, t):
                w = wid(t)
                act.wait_ge(S.sem("corrected"), S.count("corrected"))
                fn(AU[0:w, :, :], v4(M[1], 128, w), ACT.Copy).then_inc(S.sem("corrected_s"), 1)
                act.wait_ge(S.sem("corrected_s"), S.count("corrected_s"))

            def a_norm2(l, t):
                w = wid(t)
                act.wait_ge(S.sem("a_os"), S.count("a_os"))
                act.wait_ge(S.sem("a_kk"), S.count("a_kk"))
                fn(AKB[0:w, :, :], AW[0:w, :, :], ACT.Square).then_inc(S.sem("out_squares"), 1)
                act.wait_ge(S.sem("out_squares"), S.count("out_squares"))

            def a_norm4(l, t):
                w = wid(t)
                act.wait_ge(S.sem("out_sums"), S.count("out_sums"))
                link(fn(ASM[0:w, 1, :], ASM[0:w, 0, :], ACT.Ln, bias=C("c_eps", w), scale=1.0 / 128))
                fn(ASM[0:w, 1, :], ASM[0:w, 1, :], ACT.Exp, scale=-0.5, bias=C("c_lnhalf", w)).then_inc(S.sem("out_roots"), 1)
                act.wait_ge(S.sem("out_roots"), S.count("out_roots"))

            def b_shiftout(l):
                act.wait_ge(S.sem("tails_t"), S.count("tails_t"))
                fn(ROWS[0:9, :], PS[0:9, 3:7, :].rearrange("p b n -> p (b n)")[:, 0:SHIFT_B], ACT.Copy).then_inc(S.sem("tail_rows"), 1)
                act.wait_ge(S.sem("tail_rows"), S.count("tail_rows"))

            def b_lora(l):
                act.wait_ge(S.sem("b_mixed"), S.count("b_mixed"))
                act.wait_ge(S.sem("b_mixed_s"), S.count("b_mixed_s"))
                fn(FM[0:64, NF - 1, :], FM[0:64, NF - 1, :], ACT.Tanh).then_inc(S.sem("b_lt"), 1)
                act.wait_ge(S.sem("b_lt"), S.count("b_lt"))
                for src, dst, par, name in (("b_wraw", LW, "w0_b", "b_wt"), ("b_araw", AA, "a0_b", "b_at")):
                    act.wait_ge(S.sem(src), S.count(src))
                    for h in range(4):
                        ins = fn(dst[:, h, :], M[h][:, 0:NTOK], ACT.Tanh, scale=0.5, bias=Phalf(par, h))
                    ins.then_inc(S.sem(name), 1)
                    act.wait_ge(S.sem(name), S.count(name))

            def b_kk(l):
                act.wait_ge(S.sem("b_kraw"), S.count("b_kraw"))
                fn(TMP[:, :, :], KK[:, :, :], ACT.Square).then_inc(S.sem("squares"), 1)
                act.wait_ge(S.sem("squares"), S.count("squares"))
                act.wait_ge(S.sem("square_sums"), S.count("square_sums"))
                inv_root(TMP[:, :, :], PS[:, 3:7, 0:NTOK], 1.0, "c_eps").then_inc(S.sem("inv_roots"), 1)
                act.wait_ge(S.sem("inv_roots"), S.count("inv_roots"))
                act.wait_ge(S.sem("b_prep"), S.count("b_prep"))
                fn(BM[:, :, :], BM[:, :, :], ACT.Exp).then_inc(S.sem("b_bm"), 1)
                act.wait_ge(S.sem("b_bm"), S.count("b_bm"))

            def b_exp(l, g, t):
                w = wid(t)
                act.wait_ge(S.sem("b_done"), S.count("b_done"))
                act.wait_ge(S.sem("b_scaled"), S.count("b_scaled"))
                q = slice(2 * g, 2 * g + 2)
                fn(BE[:, 0, :, 0:w], LC[:, q, tok(t)], ACT.Exp)
                fn(BE[:, 1, :, 0:w], LC[:, q, tok(t)], ACT.Exp, scale=-1.0)
                fn(BE[:, 2, :, 0:w], LW[:, q, tok(t)], ACT.Exp).then_inc(S.sem("b_exps"), 1)
                act.wait_ge(S.sem("b_exps"), S.count("b_exps"))

            def b_pairs(l, g, t):
                w = wid(t)
                act.wait_ge(S.sem("b_m"), S.count("b_m"))
                fn(BN[0:w, :, :, :].rearrange("p a b c -> p (a b c)"), M[4][0:w, :], ACT.Copy).then_inc(S.sem("b_nats"), 1)
                act.wait_ge(S.sem("b_nats"), S.count("b_nats"))

            def b_nat(l, g, t):
                w = wid(t)
                act.wait_ge(S.sem("b_vt"), S.count("b_vt"))
                fn(BVN[0:w, :, :].rearrange("p a b -> p (a b)"), M[1][0:w, 0:256], ACT.Copy).then_inc(S.sem("b_vs"), 1)
                act.wait_ge(S.sem("b_vs"), S.count("b_vs"))

            def b_st(l, g, pr):
                act.wait_ge(S.sem("b_s_t"), S.count("b_s_t"))
                fn(BX[:, 0, :, :], PS[:, 3:5, :].rearrange("p b (s n) -> p (b s) n", n=128), ACT.Copy).then_inc(S.sem("b_s_ts"), 1)
                act.wait_ge(S.sem("b_s_ts"), S.count("b_s_ts"))

            def b_u(l, g, t):
                w = wid(t)
                act.wait_ge(S.sem("corrected"), S.count("corrected"))
                fn(BU[0:w, :, :].rearrange("p a b -> p (a b)"), M[1][0:w, 0:256], ACT.Copy).then_inc(S.sem("corrected_s"), 1)
                act.wait_ge(S.sem("corrected_s"), S.count("corrected_s"))

            def b_fin(l, g):
                act.wait_ge(S.sem("b_fin_t"), S.count("b_fin_t"))
                act.wait_ge(S.sem("states_stored"), S.count("states_stored", S.at - 1))
                fn(BSO[:, :, :].rearrange("p a b -> p (a b)"), M[4][:, 0:256], ACT.Copy).then_inc(S.sem("b_fin_s"), 1)
                act.wait_ge(S.sem("b_fin_s"), S.count("b_fin_s"))

            def b_norm2(l, g, t):
                w = wid(t)
                act.wait_ge(S.sem("b_yc"), S.count("b_yc"))
                fn(BQ[0:w, :, :], BY[0:w, :, :], ACT.Square).then_inc(S.sem("out_squares"), 1)
                act.wait_ge(S.sem("out_squares"), S.count("out_squares"))

            def b_norm4(l, g, t):
                w = wid(t)
                act.wait_ge(S.sem("out_sums"), S.count("out_sums"))
                inv_root(BSM[0:w, 1, :], BSM[0:w, 1, :], 1.0 / 64, "c_gneps", rows=w).then_inc(S.sem("out_roots"), 1)
                act.wait_ge(S.sem("out_roots"), S.count("out_roots"))

            def c_rms(l, i):
                for b in range(3):
                    act.wait_ge(S.sem(f"bank{b}_read"), S.count(f"bank{b}_read"))
                act.wait_ge(S.sem("b_done"), S.count("b_done"))
                act.wait_ge(S.sem("b_snew"), S.count("b_snew"))
                fn(SQ[i][:, :, :], QC[:, 4 * i:4 * i + 4, :], ACT.Square).then_inc(S.sem("squares"), 1)
                act.wait_ge(S.sem("squares"), S.count("squares"))
                act.wait_ge(S.sem("square_sums"), S.count("square_sums"))
                inv_root(SQ[i][:, :, :], PS[:, 3:7, 0:NTOK], 1.0 / 64, "c_eps").then_inc(S.sem("inv_roots"), 1)
                act.wait_ge(S.sem("inv_roots"), S.count("inv_roots"))

            def c_nat(l, i):
                act.wait_ge(S.sem("c_nt"), S.count("c_nt"))
                dst = (CKN, CVN)[i]
                for t in range(3):
                    ins = fn(dst[0:wid(t), t, :], M[t][0:wid(t), :], ACT.Copy)
                ins.then_inc(S.sem("c_ns"), 1)
                act.wait_ge(S.sem("c_ns"), S.count("c_ns"))

            def probs(dst, i, row):
                return fn(dst, dst, ACT.Exp, scale=0.125, bias=CMX[:, 0, i:i + 1], accum_out=CMX[:, 1, i:i + 1])

            def c_prob(l, t, g):
                act.wait_ge(S.sem("c_max"), S.count("c_max"))
                for hd in range(4):
                    ins = probs(CP[:, hd, 0:128 * (t + 1)], hd, 128)
                ins.then_inc(S.sem("c_e"), 1)
                act.wait_ge(S.sem("c_e"), S.count("c_e"))
                act.wait_ge(S.sem("c_pt"), S.count("c_pt"))
                for st in range(t + 1):
                    ins = fn(CPT[:, st, :, :].rearrange("p a b -> p (a b)"), M[2 + st], ACT.Copy)
                ins.then_inc(S.sem("c_pts"), 1)
                act.wait_ge(S.sem("c_pts"), S.count("c_pts"))

            def c_keys(l, g, j):
                s = 4 * g + j
                act.wait_ge(S.sem("past_k_t"), S.count("past_k_t"))
                act.wait_ge(S.sem("c_ssc"), S.count("c_ssc"))
                for pg in range(2):
                    ins = fn(CKT[:, s % 2, :, 128 * pg:128 * pg + 128], v4(M[3 * (s % 2) + pg], 128), ACT.Copy)
                ins.then_inc(S.sem("past_k_ts"), 1)
                act.wait_ge(S.sem("past_k_ts"), S.count("past_k_ts"))

            def c_sprob(l, g):
                act.wait_ge(S.sem("c_max"), S.count("c_max"))
                probs(CPS, 0, 128).then_inc(S.sem("c_e"), 1)
                act.wait_ge(S.sem("c_e"), S.count("c_e"))
                act.wait_ge(S.sem("c_spt"), S.count("c_spt"))
                fn(CPTS[:, 0:2, :].rearrange("p a b -> p (a b)"), M[4][:, 0:256], ACT.Copy)
                fn(CPTS[0:32, 2, :], M[4][0:32, 256:384], ACT.Copy).then_inc(S.sem("c_spts"), 1)
                act.wait_ge(S.sem("c_spts"), S.count("c_spts"))

            do = dict(params=params, norm=norm, p_a=p_a, p_f=p_f, p_c=p_c, p_z=p_z, p_g=p_g, p_pg=p_pg, p_ba=p_ba,
                      a_convout=a_convout, a_silu=a_silu, a_l2=a_l2, a_rows=a_rows, a_scale=a_scale, a_pairs=a_pairs,
                      tri=tri, lev=lev, a_u=a_u, a_norm2=a_norm2, a_norm4=a_norm4, b_shiftout=b_shiftout, b_lora=b_lora, b_kk=b_kk,
                      b_exp=b_exp, b_pairs=b_pairs, b_nat=b_nat, b_st=b_st, b_u=b_u, b_fin=b_fin, b_norm2=b_norm2, b_norm4=b_norm4,
                      c_rms=c_rms, c_nat=c_nat, c_prob=c_prob, c_keys=c_keys, c_sprob=c_sprob)
            for i, st in enumerate(order):
                S.at = i
                if st[0] in do:
                    do[st[0]](*st[1:])

        @block.vector
        def _(dve):
            own = [0]

            def link(ins):
                own[0] += 1
                ins.then_inc(S.sem("dve_link"), 1)
                dve.wait_ge(S.sem("dve_link"), own[0])

            tt, ts, stt, cp = dve.tensor_tensor, dve.tensor_scalar, dve.scalar_tensor_tensor, dve.tensor_copy
            MUL, ADD, SUB = ALU.mult, ALU.add, ALU.subtract

            def x_in(l, t):
                dve.wait_ge(S.sem("x_tr"), S.count("x_tr"))
                for k in range(2):
                    ins = cp(XA[:, 4 * k:4 * k + 4, tok(t)], v4(M[2 * (t % 2) + k], wid(t)))
                ins.then_inc(S.sem("x_t"), 1)
                dve.wait_ge(S.sem("x_t"), S.count("x_t"))

            def params(l):
                dve.wait_ge(S.sem("param_t"), S.count("param_t"))
                dve.wait_ge(S.sem("decay_rate"), S.count("decay_rate"))
                if l:
                    for b in range(3):
                        dve.wait_ge(S.sem(f"bank{b}_read"), S.count(f"bank{b}_read", S.at - 1))
                cp(PT[:, :], M[0][:, 0:NPAR])
                cp(PLT[:, 0, :], M[1][:, 0:NTOK])
                link(cp(PLT[:, 1, :], M[2][:, 0:NTOK]))
                ts(HP[:, 3:4], HP[:, 2:3], -1.0, None, MUL)
                ts(PH[:, :], PT[:, :], 0.5, None, MUL).then_inc(S.sem("param_done"), 1)
                dve.wait_ge(S.sem("param_done"), S.count("param_done"))

            def norm(l):
                dve.wait_ge(S.sem("inv_roots"), S.count("inv_roots"))
                for k in range(8):
                    stt(H(l)[:, k, :], X(l)[:, k, :], P("norm_g", k), TMP[:, 1, :], MUL, MUL).then_inc(S.sem("h_ready"), 1)
                dve.wait_ge(S.sem("h_ready"), S.count("h_ready"))

            def p_z(l, n, m):
                dve.wait_ge(S.sem("z_tanh"), S.count("z_tanh"))
                stt(Z[:, n, m, :], TH[:, m % 2, :], 1.0, bank()[:, 0:NTOK], ADD, MUL).then_inc(S.sem(freed()), 1)
                dve.wait_ge(S.sem(freed()), S.count(freed()))

            def p_up(l, n, m):
                dve.wait_ge(S.sem("projected"), S.count("projected"))
                for b in range(3):
                    dve.wait_ge(S.sem(f"bank{b}_read"), S.count(f"bank{b}_read", before("p_g")))
                if n == 2:
                    dve.wait_ge(S.sem("kv_stored"), S.count("kv_stored"))
                if n == 0:
                    stt(MG[:, m, :], gate(m), 1.0, bank()[:, 0:NTOK], ADD, MUL).then_inc(S.sem(freed()), 1)
                    dve.wait_ge(S.sem(freed()), S.count(freed()))
                    return
                stt(TMP[:, 0, :], gate(8 * n + m), 1.0, bank()[:, 0:NTOK], ADD, MUL).then_inc(S.sem(freed()), 1)
                dve.wait_ge(S.sem(freed()), S.count(freed()))
                tt(MG[:, m, :], MG[:, m, :], TMP[:, 0, :], ADD).then_inc(S.sem("merged"), 1)
                dve.wait_ge(S.sem("merged"), S.count("merged"))

            def p_y(l, m):
                dve.wait_ge(S.sem("projected"), S.count("projected"))
                stt(X(l)[:, m, :], bank()[:, 0:NTOK], 0.5, X(l)[:, m, :], MUL, ADD).then_inc(S.sem(freed()), 1)
                dve.wait_ge(S.sem(freed()), S.count(freed()))

            def p_ple(l, m):
                dve.wait_ge(S.sem("projected"), S.count("projected"))
                for b in range(3):
                    dve.wait_ge(S.sem(f"bank{b}_read"), S.count(f"bank{b}_read", S.at - 1))
                stt(TMP[:, m % 2, :], TH[:, m % 2, :], 1.0, bank()[:, 0:NTOK], ADD, MUL).then_inc(S.sem(freed()), 1)
                dve.wait_ge(S.sem(freed()), S.count(freed()))
                stt(H(l)[:, m, :], TMP[:, m % 2, :], 0.5, X(l)[:, m, :], MUL, ADD).then_inc(S.sem("x_next"), 1)
                dve.wait_ge(S.sem("x_next"), S.count("x_next"))

            def a_hist(l):
                dve.wait_ge(S.sem("hist_t"), S.count("hist_t"))
                if l:
                    for b in range(3):
                        dve.wait_ge(S.sem(f"bank{b}_read"), S.count(f"bank{b}_read", S.at - 1))
                dve.memset(U[:, :, 0:CONV_W - 1], 0.0)
                cp(Us[:, :, :, 0:CONV_W - 1], M[0][:, 0:24 * NA].rearrange("p (m s c) -> p m s c", m=NA, s=NSEQ)).then_inc(S.sem("hist_in"), 1)
                dve.wait_ge(S.sem("hist_in"), S.count("hist_in"))

            def tails(width, prompt, sampled, n):
                v = CT[:, 0:n * width].rearrange("p (m c) -> p m c", c=width)
                for b in range(3):
                    dve.wait_ge(S.sem(f"bank{b}_read"), S.count(f"bank{b}_read"))
                k = width - prompt.shape[2]
                cp(v[:, :, 0:width - k], prompt)
                return cp(v[:, :, width - k:].rearrange("p m (s c) -> p m s c", s=NSEQ), sampled)

            def a_convout(l):
                dve.wait_ge(S.sem("hist_in"), S.count("hist_in"))
                dve.wait_ge(S.sem("tails_t"), S.count("tails_t", S.at - 1))
                tails(27, U[:, :, UW - 3:UW], Us[:, :, :, US - 3:], NA).then_inc(S.sem("tails"), 1)
                dve.wait_ge(S.sem("tails"), S.count("tails"))

            def conv_w(j, m):
                c = NP1 + NA * j + m
                return PT[:, c:c + 1]

            def a_conv(l, c):
                for b in range(3):
                    dve.wait_ge(S.sem(f"bank{b}_read"), S.count(f"bank{b}_read"))
                dve.wait_ge(S.sem("tails_t"), S.count("tails_t"))
                for j in range(CONV_W):
                    for m in range(4 * c, 4 * c + 4):
                        if j == 0:
                            ins = ts(UC[:, m, 0:SEQ], U[:, m, 0:SEQ], conv_w(0, m), None, MUL)
                        else:
                            ins = stt(UC[:, m, 0:SEQ], U[:, m, j:j + SEQ], conv_w(j, m), UC[:, m, 0:SEQ], MUL, ADD)
                    if j < CONV_W - 1:
                        link(ins)
                ins.then_inc(S.sem("a_conv_p"), 1)
                dve.wait_ge(S.sem("a_conv_p"), S.count("a_conv_p"))

            def a_silu(l, c):
                dve.wait_ge(S.sem("a_tanh"), S.count("a_tanh"))
                stt(UC[:, 4 * c:4 * c + 4, :], TMP[:, :, :], 1.0, UC[:, 4 * c:4 * c + 4, :], ADD, MUL).then_inc(S.sem("a_silu"), 1)
                dve.wait_ge(S.sem("a_silu"), S.count("a_silu"))

            def a_l2(l, i):
                dve.wait_ge(S.sem("inv_roots"), S.count("inv_roots"))
                tt(UC[:, 4 * i:4 * i + 4, :], UC[:, 4 * i:4 * i + 4, :], TMP[:, :, :], MUL).then_inc(S.sem("a_unit"), 1)
                dve.wait_ge(S.sem("a_unit"), S.count("a_unit"))

            def a_rows(l):
                for b in range(3):
                    dve.wait_ge(S.sem(f"bank{b}_read"), S.count(f"bank{b}_read"))
                ts(ABG[0:4, 0, :], ATM[0:4, 0, :], 0.5, 0.5, MUL, ADD)
                link(ts(ATM[0:4, 2, :], ATM[0:4, 1, :], -1.0, None, MUL))
                tt(ATM[0:4, 2, :], ATM[0:4, 1, :], ATM[0:4, 2, :], ALU.min).then_inc(S.sem("ba_neg"), 1)
                dve.wait_ge(S.sem("ba_neg"), S.count("ba_neg"))
                dve.wait_ge(S.sem("ba_ln"), S.count("ba_ln"))
                link(stt(ATM[0:4, 1, :], ATM[0:4, 1, :], 0.0, ATM[0:4, 2, :], ALU.max, ADD))
                link(ts(ATM[0:4, 1, :], ATM[0:4, 1, :], HP[:, 3:4], None, MUL))
                dve.tensor_tensor_scan(ABG[0:4, 1, :], C("keep", 4), ATM[0:4, 1, :], 0.0, MUL, ADD).then_inc(S.sem("a_g"), 1)
                dve.wait_ge(S.sem("a_g"), S.count("a_g"))
                dve.wait_ge(S.sem("a_gcol_t"), S.count("a_gcol_t"))
                for t in range(3):
                    ins = cp(AGC[0:wid(t), t, :], M[4][0:wid(t), 4 * t:4 * t + 4])
                link(ins)

            def a_scale(l, t):
                w = wid(t)
                dve.wait_ge(S.sem("a_gb"), S.count("a_gb"))
                link(cp(AGB[:, :, 0:w], v4(M[0], w)))
                link(tt(ADI[0:w, :, 0:w], AGB[0:w, :, 0:w], bc(AGC[0:w, t, :], 2, [w, 4, w]), SUB))
                ts(ADI[0:w, :, 0:w], ADI[0:w, :, 0:w], 0.0, None, ALU.min)
                if t < 2:
                    last = AGB[:, :, w - 1:w].to_broadcast([128, 4, w])
                    ins = tt(AKD[:, :, 0:w], last, AGB[:, :, 0:w], SUB)
                else:
                    for h in range(4):
                        last = seqs(AGB[:, h, 0:w])[:, :, LS - 1:LS].to_broadcast([128, NSEQ, LS])
                        ins = tt(seqs(AKD[:, h, 0:w]), last, seqs(AGB[:, h, 0:w]), SUB)
                ins.then_inc(S.sem("a_klast"), 1)
                dve.wait_ge(S.sem("a_klast"), S.count("a_klast"))
                tt(AKB[:, :, 0:w], UC[:, 4:8, tok(t)], v4(M[1], w), MUL)
                link(stt(AVB[:, :, 0:w], UC[:, 8:12, tok(t)], 0.5, v4(M[1], w), MUL, MUL))
                dve.wait_ge(S.sem("a_exps"), S.count("a_exps"))
                kq = vx(AKQ, 4, w)
                tt(kq[:, :, 0, :], AKB[:, :, 0:w], AEG[:, :, 0:w], MUL)
                tt(kq[:, :, 1, :], UC[:, 0:4, tok(t)], AEG[:, :, 0:w], MUL)
                tt(AKD[:, :, 0:w], UC[:, 4:8, tok(t)], AKD[:, :, 0:w], MUL)
                m = C("strict_incl")[:, 128:256] if t < 2 else C("strict_incl_s", 32)[:, 32:64]
                tt(ADI[0:w, :, 0:w], ADI[0:w, :, 0:w], bc(m, 1, [w, 4, w]), MUL).then_inc(S.sem("a_scaled"), 1)
                dve.wait_ge(S.sem("a_scaled"), S.count("a_scaled"))

            def a_pairs(l, t):
                w = wid(t)
                dve.wait_ge(S.sem("a_kk0"), S.count("a_kk0"))
                dve.wait_ge(S.sem("tail_rows_stored"), S.count("tail_rows_stored"))
                link(tt(LT[0:w, :, 0:w], v4(M[2], w, w), ADI[0:w, :, 0:w], MUL))

            def a_keys(l, t):
                w = wid(t)
                dve.wait_ge(S.sem("a_kk"), S.count("a_kk"))
                tt(AQK[0:w, :, 0:w], v4(M[3], w, w), ADI[0:w, :, 0:w], MUL).then_inc(S.sem("a_lt"), 1)
                dve.wait_ge(S.sem("a_lt"), S.count("a_lt"))

            def tri(l, t):
                w = wid(t)
                link(tt(LM[0:w, :, 0:w], LT[0:w, :, 0:w], bc(C("level0", w)[:, 0:w], 1, [w, 4, w]), MUL))
                tt(TT[0:w, :, 0:w], bc(ident[0:w, 0:w], 1, [w, 4, w]), LM[0:w, :, 0:w], SUB).then_inc(S.sem("tri_t0"), 1)
                dve.wait_ge(S.sem("tri_t0"), S.count("tri_t0"))

            def lev(l, t, k):
                w = wid(t)
                if k < last_level(t):
                    dve.wait_ge(S.sem("tri_z"), S.count("tri_z"))
                    tt(TI[0:w, :, 0:w], TI[0:w, :, 0:w], v4(M[2], w, w), SUB).then_inc(S.sem("tri_iup"), 1)
                dve.wait_ge(S.sem("tri_zt"), S.count("tri_zt"))
                n = level_width(t, k)
                tt(TT[0:n, :, w - n:w], TT[0:n, :, w - n:w], v4(M[3], w, n)[:, :, w - n:w], SUB).then_inc(S.sem("tri_up"), 1)
                dve.wait_ge(S.sem("tri_up"), S.count("tri_up"))

            def own_seq(rows):
                return C("own_seq", rows).unsqueeze(2).to_broadcast([rows, NSEQ, 128])

            def both(b):
                return PS[:, 3 + b:5 + b, :].rearrange("p b (s n) -> p (b s) n", n=128)

            def a_s0(l, h):
                dve.wait_ge(S.sem("start_read"), S.count("start_read"))
                link(tt(AEX[0:64], both(2 * (h % 2))[0:64], own_seq(64), MUL))
                dve.tensor_reduce(AR[0:64, h, :], AEX[0:64].rearrange("p s v -> p v s"), AXX, ADD).then_inc(S.sem("start_reduced"), 1)
                dve.wait_ge(S.sem("start_reduced"), S.count("start_reduced"))

            def a_w(l, t):
                if t == 1:
                    dve.wait_ge(S.sem("a_ks"), S.count("a_ks"))
                    tt(AW[:, :, :], AVN[:, :, :], v4(M[4], 128), SUB).then_inc(S.sem("a_w"), 1)
                    dve.wait_ge(S.sem("a_w"), S.count("a_w"))
                if t == 2:
                    dve.wait_ge(S.sem("a_nat"), S.count("a_nat"))
                    tt(AW[0:32, :, :], AVN[0:32, :, :], AR[0:32, :, :], SUB).then_inc(S.sem("a_w"), 1)
                    dve.wait_ge(S.sem("a_w"), S.count("a_w"))

            def a_o(l, t):
                w = wid(t)
                dve.wait_ge(S.sem("a_o"), S.count("a_o"))
                if t == 2:
                    tt(AW[0:32, :, :], v4(M[2], 128, 32), AR[32:64, :, :], ADD).then_inc(S.sem("a_os"), 1)
                    dve.wait_ge(S.sem("a_os"), S.count("a_os"))
                    return
                cp(AW[:, :, :], v4(M[2], 128)).then_inc(S.sem("a_os"), 1)
                dve.wait_ge(S.sem("a_os"), S.count("a_os"))
                if t == 0:
                    cp(AST[:, :, :], v4(M[3], 128)).then_inc(S.sem("a_state"), 1)
                    dve.wait_ge(S.sem("a_state"), S.count("a_state"))
                else:
                    for h in range(4):
                        ins = stt(AST[:, h, :], AST[:, h, :], AEG[:, h, w - 1:w], v4(M[3], 128)[:, h, :], MUL, ADD)
                    ins.then_inc(S.sem("a_state"), 1)
                    dve.wait_ge(S.sem("a_state"), S.count("a_state"))

            def a_norm3(l, t):
                w = wid(t)
                dve.wait_ge(S.sem("out_squares"), S.count("out_squares"))
                dve.tensor_reduce(ASM[0:w, 0, :], AKB[0:w, :, :], AXX, ADD).then_inc(S.sem("out_sums"), 1)
                dve.wait_ge(S.sem("out_sums"), S.count("out_sums"))

            def a_norm5(l, t):
                w = wid(t)
                dve.wait_ge(S.sem("out_roots"), S.count("out_roots"))
                tt(AW[0:w, :, :], AW[0:w, :, :], bc(ASM[0:w, 1, :], 2, [w, 4, 128]), MUL).then_inc(S.sem("out_normed"), 1)
                dve.wait_ge(S.sem("out_normed"), S.count("out_normed"))

            def a_norm6(l, t):
                w = wid(t)
                dve.wait_ge(S.sem("out_t"), S.count("out_t"))
                stt(Z[:, 0, :, tok(t)], v4(M[4], w), P("onorm_a"), Z[:, 0, :, tok(t)], MUL, MUL).then_inc(S.sem("a_done"), 1)
                dve.wait_ge(S.sem("a_done"), S.count("a_done"))

            def a_sout(l, h):
                if h >= 1:
                    dve.wait_ge(S.sem("a_dst"), S.count("a_dst", S.at - 1))
                tt(AEX[0:32], bc(AU[0:32, h, :], 1, [32, NSEQ, 128]), own_seq(32), MUL).then_inc(S.sem("a_uex"), 1)
                dve.wait_ge(S.sem("a_uex"), S.count("a_uex"))
                dve.wait_ge(S.sem("a_dst"), S.count("a_dst"))
                dve.wait_ge(S.sem("a_sdec"), S.count("a_sdec"))
                tt(SD[:, h], SD[:, h], both(2 * (h % 2)), ADD).then_inc(S.sem("a_sst"), 1)
                dve.wait_ge(S.sem("a_sst"), S.count("a_sst"))

            def b_hist(l):
                dve.wait_ge(S.sem("hist_t"), S.count("hist_t"))
                dve.memset(F[:, :, 0:1], 0.0)
                cp(Fs[:, :, :, 0], M[0][:, 0:8 * NF].rearrange("p (m s) -> p m s", m=NF)).then_inc(S.sem("hist_in"), 1)
                dve.wait_ge(S.sem("hist_in"), S.count("hist_in"))

            def b_shiftout(l):
                dve.wait_ge(S.sem("tails_t"), S.count("tails_t", S.at - 1))
                tails(9, F[:, :, FW - 1:FW], Fs[:, :, :, FS - 1:FS], NF).then_inc(S.sem("tails"), 1)
                dve.wait_ge(S.sem("tails"), S.count("tails"))

            def b_mix(l):
                dve.wait_ge(S.sem("states_stored"), S.count("states_stored"))
                link(tt(FM[:, :, 0:SEQ], F[:, :, 0:SEQ], F[:, :, 1:FW], SUB))
                for m in range(NF):
                    ins = stt(FM[:, m, 0:SEQ], FM[:, m, 0:SEQ], P("mu_b", m), F[:, m, 1:FW], MUL, ADD)
                ins.then_inc(S.sem("b_mixed"), 1)
                dve.wait_ge(S.sem("b_mixed"), S.count("b_mixed"))

            def b_lora(l):
                dve.wait_ge(S.sem("b_wt"), S.count("b_wt"))
                half = -0.5 * math.exp(-0.5)
                link(ts(LW[:, :, :], LW[:, :, :], half, half, MUL, ADD))
                for h in range(4):
                    dve.tensor_tensor_scan(LC[:, h, :], C("keep"), LW[:, h, :], 0.0, MUL, ADD)
                dve.wait_ge(S.sem("b_at"), S.count("b_at"))
                ts(AA[:, :, :], AA[:, :, :], 0.5, 0.5, MUL, ADD).then_inc(S.sem("b_lc"), 1)
                dve.wait_ge(S.sem("b_lc"), S.count("b_lc"))

            def b_kk(l):
                for h in range(4):
                    ins = ts(KK[:, h, :], FM[:, 4 + h, :], P("kk_b", h), None, MUL)
                ins.then_inc(S.sem("b_kraw"), 1)
                dve.wait_ge(S.sem("b_kraw"), S.count("b_kraw"))
                mid = LC[:, :, 0:SEQ].rearrange("p h (c n) -> p h c n", c=2)
                link(cp(BM[:, :, 0:2], mid[:, :, :, 63]))
                link(tt(mid, mid, bc(BM[:, :, 0:2], 3, [128, 4, 2, 128]), SUB))
                cp(BM[:, :, 2:4], mid[:, :, :, 127])
                cp(BM[:, :, 4:12], LC[:, :, SEQ:NTOK].rearrange("p h (s c) -> p h s c", c=LS)[:, :, :, LS - 1])
                tt(LW[:, :, :], LC[:, :, :], LW[:, :, :], SUB)
                scratch = BX[:, :, :, :].rearrange("p a s n -> p (a s n)")[:, 0:4 * NTOK].rearrange("p (h n) -> p h n", h=4)
                for h in range(4):
                    ins = ts(scratch[:, h, :], AA[:, h, :], -1.0, P("ka_b", h), ADD, MUL)
                link(ins)
                stt(FM[:, 4:8, :], scratch, 1.0, FM[:, 4:8, :], ADD, MUL)
                dve.wait_ge(S.sem("inv_roots"), S.count("inv_roots"))
                link(tt(KK[:, :, :], KK[:, :, :], TMP[:, :, :], MUL))
                tt(AA[:, :, :], AA[:, :, :], KK[:, :, :], MUL).then_inc(S.sem("b_prep"), 1)
                dve.wait_ge(S.sem("b_prep"), S.count("b_prep"))

            def b_bonus(l):
                for h in range(4):
                    ins = stt(TMP[:, h, :], FM[:, h, :], P("rk_b", h), FM[:, 4 + h, :], MUL, MUL)
                ins.then_inc(S.sem("b_rkm"), 1)
                dve.wait_ge(S.sem("b_rkm"), S.count("b_rkm"))
                dve.wait_ge(S.sem("square_sums"), S.count("square_sums"))
                tt(BON[:, :, :], PS[:, 3:7, 0:NTOK], FM[:, 8:12, :], MUL).then_inc(S.sem("b_bonus_done"), 1)
                dve.wait_ge(S.sem("b_bonus_done"), S.count("b_bonus_done"))

            def b_scale(l, g, t):
                w = wid(t)
                q, q4 = slice(2 * g, 2 * g + 2), slice(4 + 2 * g, 6 + 2 * g)
                dve.wait_ge(S.sem("b_exps"), S.count("b_exps"))
                ar, bk = vx(BAR, 2, w), vx(BBK, 2, w)
                stt(ar[:, :, 0, :], KK[:, q, tok(t)], -1.0, BE[:, 2, :, 0:w], MUL, MUL)
                tt(ar[:, :, 1, :], FM[:, q, tok(t)], BE[:, 0, :, 0:w], MUL)
                tt(bk[:, :, 0, :], AA[:, q, tok(t)], BE[:, 1, :, 0:w], MUL)
                tt(bk[:, :, 1, :], FM[:, q4, tok(t)], BE[:, 1, :, 0:w], MUL).then_inc(S.sem("b_scaled"), 1)
                dve.wait_ge(S.sem("b_scaled"), S.count("b_scaled"))

            def b_pairs(l, g, t):
                w = wid(t)
                dve.wait_ge(S.sem("b_m0"), S.count("b_m0"))
                dve.wait_ge(S.sem("tail_rows_stored"), S.count("tail_rows_stored"))
                si = C("strict_incl") if t < 2 else C("strict_incl_s", 32)
                for hh in range(2):
                    m = M[hh][0:w, 0:4 * w].rearrange("p (q x n) -> p q x n", q=2, x=2)
                    ts(of_half(LT, hh)[0:w, :, 0:w], m[:, :, 0, :], -1.0, None, MUL)
                    ins = tt(of_half(BRB, hh)[0:w, :, 0:w], m[:, :, 1, :], bc(si[0:w, w:2 * w], 1, [w, 2, w]), MUL)
                link(ins)

            def b_keys(l, g, t):
                w = wid(t)
                si = C("strict_incl") if t < 2 else C("strict_incl_s", 32)
                kk = BKK[0:w, 0:8 * w].rearrange("p (q h n) -> p q h n", q=2, h=2)
                dve.wait_ge(S.sem("b_m"), S.count("b_m"))
                for hh in range(2):
                    ins = tt(kk[:, :, hh, :], M[2 + hh][0:w, 0:4 * w].rearrange("p (q n) -> p q n", q=2),
                             bc(si[0:w, 0:2 * w], 1, [w, 2, 2 * w]), MUL)
                ins.then_inc(S.sem("b_masked"), 1)
                dve.wait_ge(S.sem("b_masked"), S.count("b_masked"))

            def b_s0(l, g, pr):
                dve.wait_ge(S.sem("start_read"), S.count("start_read"))
                link(tt(BX[0:64, 1], both(2)[0:64], own_seq(64), MUL))
                dve.tensor_reduce(BR[0:64, pr, :], BX[0:64, 1].rearrange("p s v -> p v s"), AXX, ADD).then_inc(S.sem("start_reduced"), 1)
                dve.wait_ge(S.sem("start_reduced"), S.count("start_reduced"))

            def flat(ap):
                return ap.rearrange("p a b -> p (a b)")

            def b_w(l, g, t):
                w = wid(t)
                dve.wait_ge(S.sem("b_wp"), S.count("b_wp"))
                if t == 2:
                    tt(flat(BW[0:w]), M[4][0:w, 0:256], flat(BR[0:32]), ADD).then_inc(S.sem("b_ws"), 1)
                    dve.wait_ge(S.sem("b_ws"), S.count("b_ws"))
                else:
                    cp(flat(BW[0:w]), M[4][0:w, 0:256]).then_inc(S.sem("b_ws"), 1)
                    dve.wait_ge(S.sem("b_ws"), S.count("b_ws"))

            def b_y(l, g, t):
                w = wid(t)
                dve.wait_ge(S.sem("b_y"), S.count("b_y"))
                if t == 2:
                    tt(flat(BY[0:w]), M[2][0:w, 0:256], flat(BR[32:64]), ADD).then_inc(S.sem("b_ys"), 1)
                    dve.wait_ge(S.sem("b_ys"), S.count("b_ys"))
                    return
                cp(flat(BY[0:w]), M[2][0:w, 0:256]).then_inc(S.sem("b_ys"), 1)
                dve.wait_ge(S.sem("b_ys"), S.count("b_ys"))
                dve.wait_ge(S.sem("b_bm"), S.count("b_bm"))
                new = M[3][:, 0:256].rearrange("p (a b) -> p a b", a=2)
                bd = bc(C("ones_head"), 1, [128, 2, 128])
                if t == 0:
                    link(tt(BST[:, :, :], new, bd, MUL))
                    for pr in range(2):
                        q = 2 * g + pr
                        ins = ts(BST[:, pr, :], BST[:, pr, :], BM[:, q, 2:3], BM[:, q, 1:2], MUL, MUL)
                else:
                    link(tt(BW[:, :, :], new, bd, MUL))
                    link(tt(BST[:, :, :], BST[:, :, :], BW[:, :, :], ADD))
                    for pr in range(2):
                        ins = ts(BST[:, pr, :], BST[:, pr, :], BM[:, 2 * g + pr, 3:4], None, MUL)
                ins.then_inc(S.sem("b_state"), 1)
                dve.wait_ge(S.sem("b_state"), S.count("b_state"))

            def b_norm1(l, g, t):
                w = wid(t)
                y = flat(BY[0:w]).rearrange("p (h n) -> p h n", h=4)
                link(dve.tensor_reduce(BSM[0:w, 0, :], y, AXX, ADD))
                link(ts(BSM[0:w, 0, :], BSM[0:w, 0, :], 1.0 / 64, None, MUL))
                tt(y, y, bc(BSM[0:w, 0, :], 2, [w, 4, 64]), SUB).then_inc(S.sem("b_yc"), 1)
                dve.wait_ge(S.sem("b_yc"), S.count("b_yc"))

            def b_norm3(l, g, t):
                w = wid(t)
                sq = flat(BQ[0:w]).rearrange("p (h n) -> p h n", h=4)
                dve.wait_ge(S.sem("out_squares"), S.count("out_squares"))
                dve.tensor_reduce(BSM[0:w, 1, :], sq, AXX, ADD).then_inc(S.sem("out_sums"), 1)
                dve.wait_ge(S.sem("out_sums"), S.count("out_sums"))

            def b_norm5(l, g, t):
                w = wid(t)
                y = flat(BY[0:w]).rearrange("p (h n) -> p h n", h=4)
                dve.wait_ge(S.sem("out_roots"), S.count("out_roots"))
                tt(y, y, bc(BSM[0:w, 1, :], 2, [w, 4, 64]), MUL).then_inc(S.sem("out_normed"), 1)
                dve.wait_ge(S.sem("out_normed"), S.count("out_normed"))

            def b_norm6(l, g, t):
                w = wid(t)
                dve.wait_ge(S.sem("out_t"), S.count("out_t"))
                q = slice(2 * g, 2 * g + 2)
                for pr in range(2):
                    ins = ts(BE[:, 0, pr, 0:w], M[4][:, w * pr:w * pr + w], P("gn_g_b", 2 * g + pr), P("gn_b_b", 2 * g + pr),
                             MUL, ADD)
                link(ins)
                link(tt(BE[:, 0, :, 0:w], BE[:, 0, :, 0:w], BON[:, q, tok(t)], ADD))
                stt(Z[:, 1, q, tok(t)], BE[:, 0, :, 0:w], 0.5, Z[:, 1, q, tok(t)], MUL, MUL).then_inc(S.sem("b_done"), 1)
                dve.wait_ge(S.sem("b_done"), S.count("b_done"))

            def b_sout(l, g, pr):
                dve.wait_ge(S.sem("b_pcb"), S.count("b_pcb", S.at - 1))
                for x in range(2):
                    ins = tt(BX[0:32, x], bc(BN[0:32, pr, x, :], 1, [32, NSEQ, 128]), own_seq(32), MUL)
                ins.then_inc(S.sem("b_bex"), 1)
                dve.wait_ge(S.sem("b_bex"), S.count("b_bex"))
                dve.wait_ge(S.sem("b_ds"), S.count("b_ds"))
                tt(BX[0:8, 1], bc(M[2][0:8, 0:128], 1, [8, NSEQ, 128]),
                      C("eye8", 8).unsqueeze(2).to_broadcast([8, NSEQ, 128]), MUL).then_inc(S.sem("b_pcx"), 1)
                dve.wait_ge(S.sem("b_pcx"), S.count("b_pcx"))

            def b_sdec(l, g, pr):
                for hh in range(2):
                    r = slice(64 * hh, 64 * hh + 64)
                    ins = tt(BSB[r, pr, :, r], both(0)[r, :, r], BSB[r, pr, :, r], ADD)
                link(ins)
                dve.wait_ge(S.sem("b_pcb"), S.count("b_pcb"))
                for hh in range(2):
                    r = slice(64 * hh, 64 * hh + 64)
                    ins = tt(BSB[r, pr, :, r], both(3)[r, :, r], BSB[r, pr, :, r], MUL)
                ins.then_inc(S.sem("b_snew"), 1)
                dve.wait_ge(S.sem("b_snew"), S.count("b_snew"))

            def c_rms(l, i):
                dve.wait_ge(S.sem("inv_roots"), S.count("inv_roots"))
                q = QC[:, 4 * i:4 * i + 4, :]
                stt(q, q, P(("qn_c", "kn_c")[i]), SQ[i][:, :, :], MUL, MUL).then_inc(S.sem("c_n"), 1)
                dve.wait_ge(S.sem("c_n"), S.count("c_n"))

            def c_rope(l, i):
                q = QC[:, 4 * i:4 * i + 4, :]
                dve.wait_ge(S.sem("c_sw"), S.count("c_sw"))
                tt(SQ[i][:, :, :], PS[:, 3:7, 0:NTOK], bc(C("sin"), 1, [128, 4, NTOK]), MUL)
                link(tt(q, q, bc(C("cos"), 1, [128, 4, NTOK]), MUL))
                tt(q, q, SQ[i][:, :, :], ADD).then_inc(S.sem("c_rope"), 1)
                dve.wait_ge(S.sem("c_rope"), S.count("c_rope"))

            def row_max(out, src):
                link(dve.tensor_reduce(out, src, AXX, ALU.max))
                ts(out, out, -0.125, None, MUL).then_inc(S.sem("c_max"), 1)
                dve.wait_ge(S.sem("c_max"), S.count("c_max"))

            def c_score(l, t, g):
                dve.wait_ge(S.sem("c_s"), S.count("c_s"))
                dve.wait_ge(S.sem("c_pt"), S.count("c_pt", S.at - 1))
                dve.wait_ge(S.sem("c_spt"), S.count("c_spt"))
                mask = C("causal")
                n = 128 * (t + 1)
                for hh in range(2):
                    sc = M[hh][:, 0:2 * n].rearrange("p (q n) -> p q n", q=2)
                    dst = of_half(CP, hh)
                    if t:
                        cp(dst[:, :, 0:128], sc[:, :, 0:128])
                    ins = tt(dst[:, :, n - 128:n], sc[:, :, n - 128:n], bc(mask, 1, [128, 2, 128]), ADD)
                link(ins)
                row_max(CMX[:, 0, :], CP[:, :, 0:128 * (t + 1)])

            def c_prob(l, t, g):
                dve.wait_ge(S.sem("c_e"), S.count("c_e"))
                link(dve.reciprocal(CMX[:, 2, :], CMX[:, 1, :]))

            def c_pv(l, t, g):
                dve.wait_ge(S.sem("c_o"), S.count("c_o"))
                dve.wait_ge(S.sem("c_ot"), S.count("c_ot", S.at - 1))
                tt(CON[:, 256 * g:256 * g + 256].rearrange("p (h n) -> p h n", h=4),
                      M[4][:, 0:256].rearrange("p (h n) -> p h n", h=4), bc(CMX[:, 2, :], 2, [128, 4, 64]), MUL).then_inc(S.sem("c_os"), 1)
                dve.wait_ge(S.sem("c_os"), S.count("c_os"))

            def c_out(l, t):
                dve.wait_ge(S.sem("c_ot"), S.count("c_ot"))
                stt(Z[:, 2, :, tok(t)], v4(M[2], 128), 0.5, Z[:, 2, :, tok(t)], MUL, MUL).then_inc(S.sem("c_done"), 1)
                dve.wait_ge(S.sem("c_done"), S.count("c_done"))

            def c_sprob(l, g):
                dve.wait_ge(S.sem("c_ssc"), S.count("c_ssc"))
                cp(CPS[:, 0:256], M[2][:, 0:256])
                link(tt(CPS[:, 256:NTOK], M[2][:, 256:NTOK], C("causal_new")[:, 32 * g:32 * g + 32], ADD))
                row_max(CMX[:, 0, 0:1], CPS)
                dve.wait_ge(S.sem("c_e"), S.count("c_e"))
                link(dve.reciprocal(CMX[:, 2, 0:1], CMX[:, 1, 0:1]))
                ts(CPS, CPS, CMX[:, 2, 0:1], None, MUL).then_inc(S.sem("c_sp"), 1)
                dve.wait_ge(S.sem("c_sp"), S.count("c_sp"))

            def c_spv(l, g):
                dve.wait_ge(S.sem("c_so"), S.count("c_so"))
                for hh in range(2):
                    r = slice(64 * hh, 64 * hh + 64)
                    o = M[0][r, 0:128].rearrange("p (j q h t) -> p q j h t", j=4, q=4, h=2)[:, :, :, hh, :]
                    z = Z[r, 2, :, SEQ + 16 * g:SEQ + 16 * g + 16].rearrange("p q (j t) -> p q j t", j=4)
                    for q in range(4):
                        ins = stt(z[:, q], o[:, q], 0.5, z[:, q], MUL, MUL)
                ins.then_inc(S.sem("c_sdone"), 1)
                dve.wait_ge(S.sem("c_sdone"), S.count("c_sdone"))

            def finish(l, t):
                dve.wait_ge(S.sem("y_t"), S.count("y_t"))
                for k in range(2):
                    ins = cp(STG[0:wid(t), t, 512 * k:512 * k + 512], M[2 * (t % 2) + k][0:wid(t), :])
                ins.then_inc(S.sem("y_rows"), 1)
                dve.wait_ge(S.sem("y_rows"), S.count("y_rows"))

            do = dict(x_in=x_in, params=params, norm=norm, p_z=p_z, p_up=p_up, p_y=p_y, p_ple=p_ple, a_hist=a_hist,
                      a_convout=a_convout, a_conv=a_conv, a_silu=a_silu, a_l2=a_l2, a_rows=a_rows, a_scale=a_scale,
                      a_pairs=a_pairs, a_keys=a_keys, tri=tri, lev=lev, a_s0=a_s0, a_w=a_w, a_o=a_o, a_norm3=a_norm3, a_norm5=a_norm5, a_norm6=a_norm6, a_sout=a_sout,
                      b_hist=b_hist, b_shiftout=b_shiftout, b_mix=b_mix, b_lora=b_lora, b_kk=b_kk, b_bonus=b_bonus,
                      b_scale=b_scale, b_pairs=b_pairs, b_keys=b_keys, b_s0=b_s0, b_w=b_w, b_y=b_y, b_norm1=b_norm1, b_norm3=b_norm3, b_norm5=b_norm5, b_norm6=b_norm6, b_sout=b_sout, b_sdec=b_sdec,
                      c_rms=c_rms, c_rope=c_rope, c_score=c_score, c_prob=c_prob, c_pv=c_pv, c_out=c_out, c_sprob=c_sprob, c_spv=c_spv,
                      finish=finish)
            for i, st in enumerate(order):
                S.at = i
                if st[0] in do:
                    do[st[0]](*st[1:])

        @block.gpsimd
        def _(pool):
            own = [0]

            def link(ins):
                own[0] += 1
                ins.then_inc(S.sem("pool_link"), 1)
                pool.wait_ge(S.sem("pool_link"), own[0])

            tt = pool.tensor_tensor
            MUL, ADD, SUB = ALU.mult, ALU.add, ALU.subtract

            def store(out, src, name):
                pool.dma_start(out, src).then_inc(S.sem(name), 16)

            def a_convout(l):
                pool.wait_ge(S.sem("tail_rows"), S.count("tail_rows"))
                store(O["dn_conv_prompt"][l, 0], ROWS[0:3, 0:QKV_A], "tail_rows_stored")
                store(O["dn_conv_sample"][l].rearrange("s c n -> (s c) n"), ROWS[3:27, 0:QKV_A], "tail_rows_stored")

            def a_conv(l, c):
                if c:
                    return
                for b in range(3):
                    pool.wait_ge(S.sem(f"bank{b}_read"), S.count(f"bank{b}_read"))
                pool.wait_ge(S.sem("hist_in"), S.count("hist_in"))
                pool.wait_ge(S.sem("param_done"), S.count("param_done"))
                if l:
                    pool.wait_ge(S.sem("x_next"), S.count("x_next", S.at - 1))
                out = UC[:, :, SEQ:NTOK].rearrange("p m (s c) -> p m s c", c=LS)
                tmp = TMP[:, 0:2, :].rearrange("p a n -> p (a n)")[:, 0:NA * NS].rearrange("p (m s c) -> p m s c", m=NA, s=NSEQ)
                pool.wait_ge(S.sem("h_ready"), S.count("h_ready"))
                for j in range(CONV_W):
                    w = PT[:, NP1 + NA * j:NP1 + NA * j + NA].unsqueeze(2).unsqueeze(3).to_broadcast([128, NA, NSEQ, LS])
                    link(tt(out if j == 0 else tmp, Us[:, :, :, j:j + LS], w, MUL))
                    if j:
                        ins = tt(out, out, tmp, ADD)
                        if j < CONV_W - 1:
                            link(ins)
                ins.then_inc(S.sem("a_conv_s"), 1)
                pool.wait_ge(S.sem("a_conv_s"), S.count("a_conv_s"))

            def level(t, k, name="tri_lm"):
                w = wid(t)
                tt(LM[0:w, :, 0:w], LT[0:w, :, 0:w], bc(C(f"level{k}", w)[:, 0:w], 1, [w, 4, w]), MUL).then_inc(S.sem(name), 1)
                pool.wait_ge(S.sem(name), S.count(name))

            def tri(l, t):
                pool.wait_ge(S.sem("tri_t0"), S.count("tri_t0"))
                level(t, 1)

            def lev(l, t, k):
                if k < last_level(t):
                    pool.wait_ge(S.sem("tri_y"), S.count("tri_y"))
                    level(t, k + 1)

            def a_o(l, t):
                if t == 1:
                    pool.wait_ge(S.sem("a_state"), S.count("a_state"))
                    store(O["dn_prompt"][l, 0].rearrange("h k v -> k h v"), AST[:, :, :], "states_stored")

            def a_sout(l, h):
                pool.wait_ge(S.sem("a_exps"), S.count("a_exps"))
                pool.wait_ge(S.sem("start_read"), S.count("start_read"))
                last = seqs(AEG[:, h, 0:32])[:, :, LS - 1:LS].to_broadcast([128, NSEQ, 128])
                tt(SD[:, h], SD[:, h], last, MUL).then_inc(S.sem("a_sdec"), 1)
                pool.wait_ge(S.sem("a_sst"), S.count("a_sst"))
                store(O["dn_sample"][l, :, h].rearrange("s k v -> k s v"), SD[:, h], "states_stored")

            def b_shiftout(l):
                pool.wait_ge(S.sem("tail_rows"), S.count("tail_rows"))
                store(O["rwkv_shift_prompt"][l], ROWS[0:1, :], "tail_rows_stored")
                store(O["rwkv_shift_sample"][l], ROWS[1:9, :], "tail_rows_stored")

            def b_mix(l):
                for b in range(3):
                    pool.wait_ge(S.sem(f"bank{b}_read"), S.count(f"bank{b}_read"))
                pool.wait_ge(S.sem("hist_in"), S.count("hist_in"))
                pool.wait_ge(S.sem("states_stored"), S.count("states_stored"))
                pool.wait_ge(S.sem("a_done"), S.count("a_done"))
                v = FM[:, :, SEQ:NTOK].rearrange("p m (s c) -> p m s c", c=LS)
                mu = PT[:, PAT["mu_b"]:PAT["mu_b"] + NF].unsqueeze(2).unsqueeze(3).to_broadcast([128, NF, NSEQ, LS])
                link(tt(v, Fs[:, :, :, 0:LS], Fs[:, :, :, 1:], SUB))
                link(tt(v, v, mu, MUL))
                tt(v, v, Fs[:, :, :, 1:], ADD).then_inc(S.sem("b_mixed_s"), 1)
                pool.wait_ge(S.sem("b_mixed_s"), S.count("b_mixed_s"))
                pool.memset(BSB[:, :, :, :], 0.0).then_inc(S.sem("b_cleared"), 1)
                pool.wait_ge(S.sem("b_cleared"), S.count("b_cleared"))

            def b_fin(l, g):
                pool.wait_ge(S.sem("b_fin_s"), S.count("b_fin_s"))
                for pr in range(2):
                    for hh in range(2):
                        r = slice(64 * hh, 64 * hh + 64)
                        store(O["rwkv_prompt"][l, 0, 4 * g + 2 * pr + hh], BSO[r, pr, r], "states_stored")

            def b_sdec(l, g, pr):
                pool.wait_ge(S.sem("b_snew"), S.count("b_snew"))
                for hh in range(2):
                    r = slice(64 * hh, 64 * hh + 64)
                    store(O["rwkv_sample"][l, :, 4 * g + 2 * pr + hh].rearrange("s v k -> v s k"), BSB[r, pr, :, r],
                          "states_stored")

            def c_nat(l, i):
                if i == 0:
                    pool.wait_ge(S.sem("c_rope"), S.count("c_rope"))
                    pool.wait_ge(S.sem("b_snew"), S.count("b_snew"))
                    link(pool.memset(CQX[:, :, :, :], 0.0))
                    for pr in range(4):
                        for hh in range(2):
                            r = slice(64 * hh, 64 * hh + 64)
                            h = 2 * pr + hh
                            ins = pool.tensor_copy(CQX[r, pr, :, 4 * h:4 * h + 4], seqs(QC[r, pr, SEQ:NTOK]))
                    ins.then_inc(S.sem("c_qx"), 1)
                    pool.wait_ge(S.sem("c_qx"), S.count("c_qx"))
                pool.wait_ge(S.sem("c_ns"), S.count("c_ns"))
                src, name = ((CKN, "k"), (CVN, "v"))[i]
                store(O[f"{name}_prompt"][l, 0].rearrange("(t p) h d -> p t (h d)", p=128), src[:, 0:2, :], "kv_stored")
                store(O[f"{name}_sample"][l].rearrange("s t h d -> (s t) (h d)"), src[0:32, 2, :], "kv_stored")

            def finish(l, t):
                pool.wait_ge(S.sem("y_rows"), S.count("y_rows"))
                a, n = TILES[t]
                if t < 2:
                    store(O["y_prompt"][0, a:a + n, :], STG[0:n, t, :], "y_stored")
                else:
                    store(O["y_sample"].rearrange("s t d -> (s t) d"), STG[0:n, t, :], "y_stored")
                    for name in ("y_stored", "kv_stored", "states_stored", "tail_rows_stored"):
                        pool.wait_ge(S.sem(name), S.count(name))

            do = dict(a_convout=a_convout, a_conv=a_conv, tri=tri, lev=lev, a_o=a_o, a_sout=a_sout, b_shiftout=b_shiftout,
                      b_mix=b_mix, b_fin=b_fin, b_sdec=b_sdec, c_nat=c_nat, finish=finish)
            for i, st in enumerate(order):
                S.at = i
                if st[0] in do:
                    do[st[0]](*st[1:])


IN_NAMES = ["x_prompt", "x_sample", "cache_k", "cache_v", "state_dn", "state_dn_conv", "state_rwkv",
            "state_rwkv_shift", "page_table", "p_prompt", "p_sample", "norm_g", "w_in", "conv_a", "a_log", "dt_bias",
            "onorm_a", "mu_b", "w0_b", "w2_b", "a0_b", "a2_b", "kk_b", "ka_b", "rk_b", "gn_g_b", "gn_b_b", "qn_c",
            "kn_c", "w_branch", "b_gate", "w_out", "w_ple", "w_pg", "b_pg"]
OUT_SHAPES = [("y_prompt", (1, 256, 1024)), ("y_sample", (8, 4, 1024)), ("k_prompt", (2, 1, 256, 8, 64)),
              ("v_prompt", (2, 1, 256, 8, 64)), ("dn_prompt", (2, 1, 4, 128, 128)), ("dn_conv_prompt", (2, 1, 3, 1536)),
              ("rwkv_prompt", (2, 1, 8, 64, 64)), ("rwkv_shift_prompt", (2, 1, 1664)), ("k_sample", (2, 8, 4, 8, 64)),
              ("v_sample", (2, 8, 4, 8, 64)), ("dn_sample", (2, 8, 4, 128, 128)), ("dn_conv_sample", (2, 8, 3, 1536)),
              ("rwkv_sample", (2, 8, 8, 64, 64)), ("rwkv_shift_sample", (2, 8, 1664))]


def kernel(**inputs):
    import concourse.bacc as bacc
    from concourse.bass_utils import run_bass_kernel_spmd
    arrays = {n: np.ascontiguousarray(inputs[n]) for n in IN_NAMES}
    arrays["const_table"] = CONSTS
    nc = bacc.Bacc("TRN2", target_bir_lowering=False, num_devices=1)
    A = {n: nc.dram_tensor(f"in_{n}", a.shape, mybir.dt.from_np(a.dtype), kind="ExternalInput").ap()
         for n, a in arrays.items()}
    O = {n: nc.dram_tensor(f"out_{n}", s, FP32, kind="ExternalOutput").ap() for n, s in OUT_SHAPES}
    program(nc, A, O)
    r = run_bass_kernel_spmd(nc, [{f"in_{n}": a for n, a in arrays.items()}], core_ids=[0])
    return tuple(r.results[0][f"out_{n}"] for n, _ in OUT_SHAPES)
```
